# Optimizing a Trainium2 kernel written in Bass

```python
import math
import jax, jax.numpy as jnp
from jax import lax
import numpy as np

D_MODEL = 1024
BATCH = 1
SEQ = 256
DEPTH = 1

MIX_WIDTH = D_MODEL
CONV_WIDTH = MIX_WIDTH // 2
FFT_WIDTH = MIX_WIDTH - CONV_WIDTH
GROUP_DIM = 64
CONV_HEADS = CONV_WIDTH // GROUP_DIM
FFT_GROUPS = FFT_WIDTH // GROUP_DIM
IN_PROJ_WIDTH = 3 * CONV_WIDTH + FFT_WIDTH
CONV_K = 3
MEM_LEN = 256
XATTN_HEADS = 4
XATTN_HEAD_DIM = D_MODEL // XATTN_HEADS
N_EXPERTS = 32
TOP_K = 4
D_EXPERT = D_MODEL
SWIGLU_LIMIT = 7.0
SWIGLU_ALPHA = 1.702
ROW_BLOCK = 128
EPS = 1e-5


def rmsnorm(x, g):
    xf = x.astype(jnp.float32)
    y = xf * lax.rsqrt(jnp.mean(xf * xf, axis=-1, keepdims=True) + EPS)
    return (y * g.astype(jnp.float32)).astype(x.dtype)

def short_conv3(u, w):
    up = jnp.pad(u, ((0, 0), (1, 1), (0, 0)))
    return w[0] * up[:, :-2] + w[1] * up[:, 1:-1] + w[2] * up[:, 2:]

def hybrid_mixer(h, w_in, conv_w, g_conv_out, g_fft_out, w_out):
    bsz, s, _ = h.shape
    z = h @ w_in
    b_gate = z[..., :CONV_WIDTH]
    c_gate = z[..., CONV_WIDTH:2 * CONV_WIDTH]
    v = z[..., 2 * CONV_WIDTH:3 * CONV_WIDTH]
    u = z[..., 3 * CONV_WIDTH:]
    y_conv = b_gate * short_conv3(c_gate * v, conv_w)
    uf = u.astype(jnp.float32).reshape(bsz, s, FFT_GROUPS, GROUP_DIM)
    y_fft = jnp.fft.fftn(uf, axes=(1, 3), norm="ortho").real
    y_fft = y_fft.reshape(bsz, s, FFT_WIDTH).astype(h.dtype)
    y = jnp.concatenate([rmsnorm(y_conv, g_conv_out), rmsnorm(y_fft, g_fft_out)], axis=-1)
    return y @ w_out

def memory_cross_attention(h, mem_n, w_q, w_k, w_v, w_o):
    bsz, s, d = h.shape
    m = mem_n.shape[1]
    q = (h @ w_q).reshape(bsz, s, XATTN_HEADS, XATTN_HEAD_DIM)
    k = (mem_n @ w_k).reshape(bsz, m, XATTN_HEADS, XATTN_HEAD_DIM)
    v = (mem_n @ w_v).reshape(bsz, m, XATTN_HEADS, XATTN_HEAD_DIM)
    scores = jnp.einsum('bshd,bmhd->bhsm', q, k).astype(jnp.float32) * (XATTN_HEAD_DIM ** -0.5)
    p = jax.nn.softmax(scores, axis=-1).astype(v.dtype)
    o = jnp.einsum('bhsm,bmhd->bshd', p, v).reshape(bsz, s, d)
    return o @ w_o

def moe_ffn(h, w_router, b_router, w_gate_up, b_gate_up, w_down, b_down):
    bsz, s, d = h.shape
    t = bsz * s
    hf = h.reshape(t, d)
    logits = (hf @ w_router).astype(jnp.float32) + b_router.astype(jnp.float32)
    top_v, top_i = lax.top_k(logits, TOP_K)
    top_w = jax.nn.softmax(top_v, axis=-1)
    n_assign = t * TOP_K
    flat_e = top_i.reshape(n_assign)
    flat_tok = jnp.repeat(jnp.arange(t, dtype=jnp.int32), TOP_K)
    flat_w = top_w.reshape(n_assign)
    order = jnp.argsort(flat_e)
    sorted_e = flat_e[order]
    counts = jnp.bincount(flat_e, length=N_EXPERTS)
    padded = ((counts + ROW_BLOCK - 1) // ROW_BLOCK) * ROW_BLOCK
    start = jnp.cumsum(counts) - counts
    pad_end = jnp.cumsum(padded)
    pad_start = pad_end - padded
    dest = pad_start[sorted_e] + jnp.arange(n_assign) - start[sorted_e]
    n_blocks = -(-n_assign // ROW_BLOCK) + N_EXPERTS
    n_rows = n_blocks * ROW_BLOCK
    row_tok = jnp.full((n_rows,), t, dtype=jnp.int32).at[dest].set(flat_tok[order])
    row_w = jnp.zeros((n_rows,), jnp.float32).at[dest].set(flat_w[order])
    block_e = jnp.minimum(
        jnp.searchsorted(pad_end, jnp.arange(n_blocks) * ROW_BLOCK, side='right'), N_EXPERTS - 1)
    h_pad = jnp.concatenate([hf, jnp.zeros((1, d), hf.dtype)], axis=0)
    xs = h_pad[row_tok].reshape(n_blocks, ROW_BLOCK, d)

    def expert_block(args):
        xb, e = args
        gu = xb @ w_gate_up[e] + b_gate_up[e]
        gate = jnp.minimum(gu[:, :D_EXPERT], SWIGLU_LIMIT)
        up = jnp.clip(gu[:, D_EXPERT:], -SWIGLU_LIMIT, SWIGLU_LIMIT)
        glu = gate * jax.nn.sigmoid(SWIGLU_ALPHA * gate)
        return ((up + 1.0) * glu) @ w_down[e] + b_down[e]

    out = lax.map(expert_block, (xs, block_e)).reshape(n_rows, d)
    y = jnp.zeros((t + 1, d), out.dtype).at[row_tok].add(out * row_w[:, None].astype(out.dtype))
    return y[:t].reshape(bsz, s, d)

def first_inputs(seed: int = 0) -> dict:
    key = jax.random.key(seed)
    ks = jax.random.split(key, 24)
    f32 = jnp.float32

    def nrm(k, shape, scale):
        return jax.random.normal(k, shape, f32) * scale

    def gain(k, shape):
        return 1.0 + 0.02 * jax.random.normal(k, shape, f32)

    L = DEPTH
    return {
        "x": nrm(ks[0], (BATCH, SEQ, D_MODEL), 1.0),
        "mem": nrm(ks[1], (BATCH, MEM_LEN, D_MODEL), 1.0),
        "norm_mix": gain(ks[2], (L, D_MODEL)),
        "w_in": nrm(ks[3], (L, D_MODEL, IN_PROJ_WIDTH), D_MODEL ** -0.5),
        "conv_w": nrm(ks[4], (L, CONV_K, CONV_WIDTH), CONV_K ** -0.5),
        "g_conv_out": gain(ks[5], (L, CONV_WIDTH)),
        "g_fft_out": gain(ks[6], (L, FFT_WIDTH)),
        "w_out": nrm(ks[7], (L, MIX_WIDTH, D_MODEL), MIX_WIDTH ** -0.5),
        "norm_xattn": gain(ks[8], (L, D_MODEL)),
        "norm_mem": gain(ks[9], (L, D_MODEL)),
        "w_q": nrm(ks[10], (L, D_MODEL, D_MODEL), D_MODEL ** -0.5),
        "w_k": nrm(ks[11], (L, D_MODEL, D_MODEL), D_MODEL ** -0.5),
        "w_v": nrm(ks[12], (L, D_MODEL, D_MODEL), D_MODEL ** -0.5),
        "w_o": nrm(ks[13], (L, D_MODEL, D_MODEL), D_MODEL ** -0.5),
        "norm_ffn": gain(ks[14], (L, D_MODEL)),
        "w_router": nrm(ks[15], (L, D_MODEL, N_EXPERTS), D_MODEL ** -0.5),
        "b_router": nrm(ks[16], (L, N_EXPERTS), 0.01),
        "w_gate_up": nrm(ks[17], (L, N_EXPERTS, D_MODEL, 2 * D_EXPERT), D_MODEL ** -0.5),
        "b_gate_up": nrm(ks[18], (L, N_EXPERTS, 2 * D_EXPERT), 0.02),
        "w_down": nrm(ks[19], (L, N_EXPERTS, D_EXPERT, D_MODEL), D_EXPERT ** -0.5),
        "b_down": nrm(ks[20], (L, N_EXPERTS, D_MODEL), 0.02),
        "norm_final": gain(ks[21], (D_MODEL,)),
    }

def first_block(x, mem, norm_mix, w_in, conv_w, g_conv_out, g_fft_out, w_out,
              norm_xattn, norm_mem, w_q, w_k, w_v, w_o, norm_ffn, w_router, b_router,
              w_gate_up, b_gate_up, w_down, b_down, norm_final):
    for l in range(DEPTH):
        h = rmsnorm(x, norm_mix[l])
        x = x + hybrid_mixer(h, w_in[l], conv_w[l], g_conv_out[l], g_fft_out[l], w_out[l])
        h = rmsnorm(x, norm_xattn[l])
        mem_n = rmsnorm(mem, norm_mem[l])
        x = x + memory_cross_attention(h, mem_n, w_q[l], w_k[l], w_v[l], w_o[l])
        h = rmsnorm(x, norm_ffn[l])
        x = x + moe_ffn(h, w_router[l], b_router[l], w_gate_up[l], b_gate_up[l], w_down[l], b_down[l])
    return rmsnorm(x, norm_final)


DEPTH_2 = 2

HEAD_DIM = 64
ROPE_THETA = 10000.0
A_Q_HEADS = 8
A_KV_HEADS = 2
A_WINDOW = 128
A_BLOCK = 128
B_Q_HEADS = 8
B_Q_RANK = 256
B_IDX_HEADS = 8
B_IDX_DIM = HEAD_DIM
B_TOPK_MAX = 256
B_QBLOCK = 128
C_HEADS = 16
C_BLOCK = 256
C_TOPK = 3
C_QCHUNK = 16
D_FF = 4 * D_MODEL
N_EVEN = (DEPTH_2 + 1) // 2
N_ODD = DEPTH_2 // 2
DN_ALPHA = (2 * DEPTH_2) ** 0.25
DN_BETA = (8 * DEPTH_2) ** -0.25
LN_EPS = 1e-5
RMS_EPS = 1e-6

AB_WIDTHS = (A_Q_HEADS * HEAD_DIM, A_KV_HEADS * HEAD_DIM, A_KV_HEADS * HEAD_DIM,
             B_Q_RANK, HEAD_DIM, HEAD_DIM, B_IDX_DIM, B_IDX_HEADS)
AB_IN_WIDTH = sum(AB_WIDTHS)
AB_MIX_WIDTH = (A_Q_HEADS + B_Q_HEADS) * HEAD_DIM
C_WIDTH = C_HEADS * HEAD_DIM


def _split_widths(t, widths):
    return jnp.split(t, np.cumsum(widths)[:-1].tolist(), axis=-1)

def layer_norm(x, g, b):
    xf = x.astype(jnp.float32)
    mu = jnp.mean(xf, axis=-1, keepdims=True)
    var = jnp.mean(jnp.square(xf - mu), axis=-1, keepdims=True)
    return ((xf - mu) * lax.rsqrt(var + LN_EPS) * g.astype(jnp.float32) + b.astype(jnp.float32)).astype(x.dtype)

def rms_norm(x, g):
    xf = x.astype(jnp.float32)
    ms = jnp.mean(jnp.square(xf), axis=-1, keepdims=True)
    return (xf * lax.rsqrt(ms + RMS_EPS) * g.astype(jnp.float32)).astype(x.dtype)

def rope_tables(positions):
    inv = ROPE_THETA ** (-jnp.arange(0, HEAD_DIM, 2, dtype=jnp.float32) / HEAD_DIM)
    ang = positions.astype(jnp.float32)[..., None] * inv
    ang = jnp.concatenate([ang, ang], axis=-1)
    return jnp.cos(ang)[:, :, None, :], jnp.sin(ang)[:, :, None, :]

def apply_rope(t, cos, sin):
    t1, t2 = jnp.split(t, 2, axis=-1)
    rot = jnp.concatenate([-t2, t1], axis=-1)
    return (t * cos + rot * sin).astype(t.dtype)

def ada_modulation(c, w, b):
    m = jax.nn.silu(c) @ w + b
    shift, scale, gate = jnp.split(m[:, None, :], 3, axis=-1)
    return shift, scale, 1.0 + gate

def swa_sink_attention(q, k, v, sinks):
    Bn, S, HQ, hd = q.shape
    HKV = k.shape[2]
    G = HQ // HKV
    nb = S // A_BLOCK
    qb = q.reshape(Bn, nb, A_BLOCK, HKV, G, hd)

    def band(t):
        tb = t.reshape(Bn, nb, A_BLOCK, HKV, hd)
        prev = jnp.pad(tb[:, :-1], ((0, 0), (1, 0), (0, 0), (0, 0), (0, 0)))
        return jnp.concatenate([prev, tb], axis=2)

    kb, vb = band(k), band(v)
    s = jnp.einsum('bnqkgd,bnskd->bnkgqs', qb, kb, preferred_element_type=jnp.float32) * (hd ** -0.5)
    qpos = jnp.arange(nb)[:, None, None] * A_BLOCK + jnp.arange(A_BLOCK)[None, :, None]
    kpos = jnp.arange(nb)[:, None, None] * A_BLOCK - A_BLOCK + jnp.arange(2 * A_BLOCK)[None, None, :]
    diff = qpos - kpos
    mask = (diff >= 0) & (diff < A_WINDOW) & (kpos >= 0)
    s = jnp.where(mask[None, :, None, None], s, -jnp.inf)
    sink = jnp.broadcast_to(sinks.astype(jnp.float32).reshape(HKV, G)[None, None, :, :, None, None],
                            s.shape[:-1] + (1,))
    p = jax.nn.softmax(jnp.concatenate([s, sink], axis=-1), axis=-1)[..., :-1]
    o = jnp.einsum('bnkgqs,bnskd->bnqkgd', p.astype(vb.dtype), vb)
    return o.reshape(Bn, S, HQ * hd)

def dsa_attention(q, k, v, iq, ik, iw):
    Bn, S, H, hd = q.shape
    n_top = min(B_TOPK_MAX, S // 4)
    nqb = S // B_QBLOCK

    def to_blocks(t):
        return jnp.moveaxis(t.reshape((Bn, nqb, B_QBLOCK) + t.shape[2:]), 1, 0)

    kpos = jnp.arange(S)
    bidx = jnp.arange(Bn)[:, None, None]
    scale = hd ** -0.5

    def one_block(args):
        i, qb, iqb, iwb = args
        tpos = i * B_QBLOCK + jnp.arange(B_QBLOCK)
        raw = jnp.einsum('bqhd,bsd->bhqs', iqb, ik, preferred_element_type=jnp.float32)
        score = jnp.einsum('bhqs,bqh->bqs', jax.nn.relu(raw), iwb.astype(jnp.float32))
        causal = kpos[None, :] <= tpos[:, None]
        score = jnp.where(causal[None], score, -jnp.inf)
        _, idx = lax.top_k(score, n_top)
        valid = idx <= tpos[None, :, None]
        kg = k[bidx, idx]
        vg = v[bidx, idx]
        s = jnp.einsum('bqhd,bqkd->bhqk', qb, kg, preferred_element_type=jnp.float32) * scale
        s = jnp.where(valid[:, None], s, -jnp.inf)
        p = jax.nn.softmax(s, axis=-1)
        o = jnp.einsum('bhqk,bqkd->bqhd', p.astype(vg.dtype), vg)
        return o.reshape(Bn, B_QBLOCK, H * hd)

    out = lax.map(one_block, (jnp.arange(nqb), to_blocks(q), to_blocks(iq), to_blocks(iw)))
    return jnp.moveaxis(out, 0, 1).reshape(Bn, S, H * hd)

def moba_attention(q, k, v):
    Bn, S, H, hd = q.shape
    nb = -(-S // C_BLOCK)
    Sp = nb * C_BLOCK
    pad = ((0, 0), (0, Sp - S), (0, 0), (0, 0))
    kb = jnp.pad(k, pad).reshape(Bn, nb, C_BLOCK, H, hd).transpose(0, 3, 1, 2, 4)
    vb = jnp.pad(v, pad).reshape(Bn, nb, C_BLOCK, H, hd).transpose(0, 3, 1, 2, 4)
    kmean = jnp.mean(kb.astype(jnp.float32), axis=3)
    n_sel = min(C_TOPK, nb - 1)
    nqc = S // C_QCHUNK
    qc = q.reshape(Bn, nqc, C_QCHUNK, H, hd).transpose(1, 0, 3, 2, 4)
    bi = jnp.arange(Bn)[:, None, None, None]
    hi = jnp.arange(H)[None, :, None, None]
    scale = hd ** -0.5

    def one_chunk(args):
        i, qblk = args
        tpos = i * C_QCHUNK + jnp.arange(C_QCHUNK)
        own = tpos // C_BLOCK
        own_idx = jnp.broadcast_to(own[None, None, :, None], (Bn, H, C_QCHUNK, 1))
        own_ok = jnp.ones((Bn, H, C_QCHUNK, 1), dtype=bool)
        if n_sel > 0:
            gate = jnp.einsum('bhqd,bhnd->bhqn', qblk, kmean, preferred_element_type=jnp.float32)
            past = jnp.arange(nb)[None, :] < own[:, None]
            gate = jnp.where(past[None, None], gate, -jnp.inf)
            _, sel = lax.top_k(gate, n_sel)
            sel_ok = sel < own[None, None, :, None]
            blk = jnp.concatenate([sel, own_idx], axis=-1)
            blk_ok = jnp.concatenate([sel_ok, own_ok], axis=-1)
        else:
            blk, blk_ok = own_idx, own_ok
        kg = kb[bi, hi, blk]
        vg = vb[bi, hi, blk]
        s = jnp.einsum('bhqd,bhqnjd->bhqnj', qblk, kg, preferred_element_type=jnp.float32) * scale
        kpos = blk[..., None] * C_BLOCK + jnp.arange(C_BLOCK)
        ok = blk_ok[..., None] & (kpos <= tpos[None, None, :, None, None])
        s = jnp.where(ok, s, -jnp.inf)
        p = jax.nn.softmax(s.reshape(s.shape[:3] + (-1,)), axis=-1).reshape(s.shape)
        o = jnp.einsum('bhqnj,bhqnjd->bqhd', p.astype(vg.dtype), vg)
        return o.reshape(Bn, C_QCHUNK, H * hd)

    out = lax.map(one_chunk, (jnp.arange(nqc), qc))
    return jnp.moveaxis(out, 0, 1).reshape(Bn, S, H * hd)

def mixer_ab(h, cos, sin, w_in, q_norm, w_uq, w_uiq, sinks, w_out):
    Bn, S, _ = h.shape
    aq, ak, av, cq, bk, bv, bik, biw = _split_widths(h @ w_in, AB_WIDTHS)
    aq = apply_rope(aq.reshape(Bn, S, A_Q_HEADS, HEAD_DIM), cos, sin)
    ak = apply_rope(ak.reshape(Bn, S, A_KV_HEADS, HEAD_DIM), cos, sin)
    av = av.reshape(Bn, S, A_KV_HEADS, HEAD_DIM)
    ya = swa_sink_attention(aq, ak, av, sinks)
    cq = rms_norm(cq, q_norm)
    bq = apply_rope((cq @ w_uq).reshape(Bn, S, B_Q_HEADS, HEAD_DIM), cos, sin)
    biq = apply_rope((cq @ w_uiq).reshape(Bn, S, B_IDX_HEADS, B_IDX_DIM), cos, sin)
    bk = apply_rope(bk[:, :, None, :], cos, sin)[:, :, 0]
    bik = apply_rope(bik[:, :, None, :], cos, sin)[:, :, 0]
    iw = biw * (B_IDX_HEADS ** -0.5 * B_IDX_DIM ** -0.5)
    yb = dsa_attention(bq, bk, bv, biq, bik, iw)
    return jnp.concatenate([ya, yb], axis=-1) @ w_out

def mixer_c(h, cos, sin, w_in, w_out):
    Bn, S, _ = h.shape
    q, k, v = jnp.split(h @ w_in, 3, axis=-1)
    q = apply_rope(q.reshape(Bn, S, C_HEADS, HEAD_DIM), cos, sin)
    k = apply_rope(k.reshape(Bn, S, C_HEADS, HEAD_DIM), cos, sin)
    v = v.reshape(Bn, S, C_HEADS, HEAD_DIM)
    return moba_attention(q, k, v) @ w_out

def squared_relu_mlp(h, w1, w2):
    return jnp.square(jax.nn.relu(h @ w1)) @ w2

def second_inputs(seed: int = 0) -> dict:
    key = jax.random.key(seed)
    ks = jax.random.split(key, 20)
    f32 = jnp.float32
    n = lambda k, shp, s: jax.random.normal(k, shp, f32) * s
    D = D_MODEL
    return {
        "x": n(ks[0], (BATCH, SEQ, D), 1.0),
        "c": n(ks[1], (BATCH, D), 1.0),
        "positions": jnp.broadcast_to(jnp.arange(SEQ, dtype=jnp.int32)[None, :], (BATCH, SEQ)),
        "ab_w_in": n(ks[2], (N_EVEN, D, AB_IN_WIDTH), D ** -0.5),
        "ab_q_norm": 1.0 + n(ks[3], (N_EVEN, B_Q_RANK), 0.02),
        "ab_w_uq": n(ks[4], (N_EVEN, B_Q_RANK, B_Q_HEADS * HEAD_DIM), B_Q_RANK ** -0.5),
        "ab_w_uiq": n(ks[5], (N_EVEN, B_Q_RANK, B_IDX_HEADS * B_IDX_DIM), B_Q_RANK ** -0.5),
        "ab_sinks": n(ks[6], (N_EVEN, A_Q_HEADS), 1.0),
        "ab_w_out": n(ks[7], (N_EVEN, AB_MIX_WIDTH, D), AB_MIX_WIDTH ** -0.5 * DN_BETA),
        "c_w_in": n(ks[8], (N_ODD, D, 3 * C_WIDTH), D ** -0.5),
        "c_w_out": n(ks[9], (N_ODD, C_WIDTH, D), C_WIDTH ** -0.5 * DN_BETA),
        "ada_w": n(ks[10], (DEPTH_2, 2, D, 3 * D), 0.1 * D ** -0.5),
        "ada_b": n(ks[11], (DEPTH_2, 2, 3 * D), 0.02),
        "ln_g": 1.0 + n(ks[12], (DEPTH_2, 2, D), 0.02),
        "ln_b": n(ks[13], (DEPTH_2, 2, D), 0.02),
        "mlp_w1": n(ks[14], (DEPTH_2, D, D_FF), D ** -0.5),
        "mlp_w2": n(ks[15], (DEPTH_2, D_FF, D), D_FF ** -0.5 * DN_BETA),
    }

def second_block(x, c, positions, ab_w_in, ab_q_norm, ab_w_uq, ab_w_uiq, ab_sinks, ab_w_out,
              c_w_in, c_w_out, ada_w, ada_b, ln_g, ln_b, mlp_w1, mlp_w2):
    cos, sin = rope_tables(positions)
    for layer in range(DEPTH_2):
        shift, scale, gate = ada_modulation(c, ada_w[layer, 0], ada_b[layer, 0])
        h = x * (1.0 + scale) + shift
        if layer % 2 == 0:
            e = layer // 2
            y = mixer_ab(h, cos, sin, ab_w_in[e], ab_q_norm[e], ab_w_uq[e], ab_w_uiq[e],
                         ab_sinks[e], ab_w_out[e])
        else:
            o = layer // 2
            y = mixer_c(h, cos, sin, c_w_in[o], c_w_out[o])
        x = layer_norm(DN_ALPHA * x + gate * y, ln_g[layer, 0], ln_b[layer, 0])
        shift, scale, gate = ada_modulation(c, ada_w[layer, 1], ada_b[layer, 1])
        h = x * (1.0 + scale) + shift
        y = squared_relu_mlp(h, mlp_w1[layer], mlp_w2[layer])
        x = layer_norm(DN_ALPHA * x + gate * y, ln_g[layer, 1], ln_b[layer, 1])
    return x


def setup_inputs(seed=0):
    out = dict(first_inputs(seed))
    for name, value in second_inputs(seed + 1).items():
        if name != "x":
            out[name + "_2"] = value
    return out


def reference(
    x, mem, norm_mix, w_in, conv_w, g_conv_out, g_fft_out, w_out, norm_xattn, norm_mem, w_q,
    w_k, w_v, w_o, norm_ffn, w_router, b_router, w_gate_up, b_gate_up, w_down, b_down,
    norm_final, c_2, positions_2, ab_w_in_2, ab_q_norm_2, ab_w_uq_2, ab_w_uiq_2, ab_sinks_2,
    ab_w_out_2, c_w_in_2, c_w_out_2, ada_w_2, ada_b_2, ln_g_2, ln_b_2, mlp_w1_2, mlp_w2_2,
):
    x = first_block(
        x, mem, norm_mix, w_in, conv_w, g_conv_out, g_fft_out, w_out, norm_xattn, norm_mem, w_q,
        w_k, w_v, w_o, norm_ffn, w_router, b_router, w_gate_up, b_gate_up, w_down, b_down,
        norm_final,
    )
    return second_block(
        x, c_2, positions_2, ab_w_in_2, ab_q_norm_2, ab_w_uq_2, ab_w_uiq_2, ab_sinks_2,
        ab_w_out_2, c_w_in_2, c_w_out_2, ada_w_2, ada_b_2, ln_g_2, ln_b_2, mlp_w1_2, mlp_w2_2,
    )


_drawn_inputs = setup_inputs


def setup_inputs(seed=0):
    import zlib

    import numpy as np

    out = dict(_drawn_inputs(seed))
    spreads = {}
    factors = {'norm_xattn': 8.0,
     'norm_mem': 3.514,
     'b_gate_up': 5.73,
     'b_down': 6.513,
     'ab_q_norm_2': 8.0,
     'ab_sinks_2': 8.0}
    for name, (base, spread) in spreads.items():
        noise = np.random.default_rng([zlib.crc32(name.encode()), seed]).standard_normal(out[name].shape)
        drawn = base * np.exp(spread * noise) if base else spread * noise
        out[name] = __import__('jax').numpy.asarray(drawn.astype(out[name].dtype))
    for name, factor in factors.items():
        out[name] = (out[name] * factor).astype(out[name].dtype)
    return out
```

```python
from contextlib import ExitStack

import numpy as np
import concourse.bass as bass
from concourse import mybir

F32 = mybir.dt.float32
I32 = mybir.dt.int32
ALU = mybir.AluOpType
ACT = mybir.ActivationFunctionType
AX = mybir.AxisListType
ENG = mybir.EngineType

P = 128
S = 256
TB = S // P
D = 1024
KC = D // P
NE = 32
TOPK = 4
CAP = 64
NB_MAX = S // CAP
NCAND = (NB_MAX - 1) * NE
NX_MAX = S * TOPK // CAP
SLOT = 4096
HW = 512
HD = 64
NEG = -1e30
TAKEN = -3e38
FAR = 10000.0

T_COLS = {}


def tables():
    p = np.arange(P)[:, None]
    c = np.arange(P)[None, :]
    parts = {}
    parts["ident"] = (p == c) * 1.0
    parts["tri"] = (p < c) * 1.0
    parts["ones"] = np.ones((P, P))
    parts["quads"] = (p % 32 == 0) * 1.0
    parts["iota"] = np.repeat(c % CAP, P, 0)
    causal = np.where(c <= p, 0.0, NEG)
    parts["full"] = np.concatenate([causal, np.zeros((P, P)), causal], 1)
    parts["window"] = np.concatenate([causal, np.where(c > p, 0.0, NEG), causal], 1)
    ang = 2 * np.pi * np.outer(np.arange(64), np.arange(64)) / 64
    same = np.kron(np.eye(2), np.ones((64, 64)))
    parts["cg"] = np.tile(np.cos(ang), (2, 2)) * same / 8
    parts["sg"] = -np.tile(np.sin(ang), (2, 2)) * same / 8
    inv = np.float32(10000.0) ** (-np.arange(0, HD, 2, dtype=np.float32) / np.float32(HD))
    parts["inv"] = np.repeat(inv[None], P, 0)
    parts["eps5"] = np.full((P, 1), 1e-5)
    parts["eps6"] = np.full((P, 1), 1e-6)
    parts["zero"] = np.zeros((P, 1))
    parts["halfpi"] = np.full((P, 1), np.pi / 2)
    q = np.minimum(np.arange(P), NCAND - 1)[:, None]
    parts["thr"] = CAP * (1 + q // NE)
    parts["cand_e"] = q % NE
    parts["cand_q"] = (1 + q // NE) * (NE + 1) + q % NE
    parts["shift"] = np.repeat(CAP * np.arange(NB_MAX)[None], P, 0)
    at = 0
    for n, a in parts.items():
        T_COLS[n] = (at, at + a.shape[1])
        at += a.shape[1]
    t = np.concatenate([np.asarray(a, np.float32) for a in parts.values()], 1)
    ang = 2 * np.pi * (np.outer(np.arange(S), np.arange(S)) % S) / S
    dft = np.concatenate([np.cos(ang), np.sin(ang)], 1) / 16
    return np.ascontiguousarray(t), np.ascontiguousarray(dft.astype(np.float32))


tables()
TAB_W = max(b for _, b in T_COLS.values())

VEC = {"norm_mix": 0, "norm_xattn": 8, "norm_mem": 16, "norm_ffn": 24, "g_conv_out": 32, "g_fft_out": 36,
       "conv_w": 40, "ab_q_norm_2": 52, "c_2": 54}
NVEC = 62
NADA = 4
ADA_UNITS = NADA * 6

ADA_AT = [("mix_in", 5), ("fft", 3), ("yfft", 2), ("mixss", 2), ("mix_out", 2), ("q", 1), ("scores", 3),
          ("w_o", 2), ("router", 4)]


def pre_stream():
    out = [("w_k", i) for i in range(2)] + [("w_v", i) for i in range(2)] + [("w_in", i) for i in range(4)]
    u = 0
    tail = {"mixss": [("w_out", 0), ("w_out", 1)], "mix_out": [("w_q", 0), ("w_q", 1)],
            "scores": [("w_o", 0), ("w_o", 1)]}
    for name, n in ADA_AT:
        out += [("ada", u + i) for i in range(n)]
        u += n
        out += tail.get(name, [])
    assert u == ADA_UNITS
    return out


PRE = pre_stream()
NPRE = len(PRE)
R1 = 6
PER_E = 6
MOE_END = NPRE + NE * PER_E
POST = ([("ab_in", i) for i in range(3)] + [("uq", 0)] + [("ab_out", i) for i in range(2)] + [("mlp0", i) for i in range(16)]
        + [("c_in", i) for i in range(6)] + [("c_out", i) for i in range(2)] + [("mlp1", i) for i in range(16)])
R2 = 8
POST_SLOTS = [6, 7] + [(NPRE + j) % R1 for j in range(R1)]


def slot_of(g):
    return g % R1 if g < MOE_END else POST_SLOTS[(g - MOE_END) % R2]


FILL, OWNER = {}, {}


def lay_stream():
    count, last = [0] * R2, {}
    for g in range(MOE_END + len(POST)):
        s = slot_of(g)
        count[s] += 2 if g == MOE_END + 3 else 1
        FILL[g] = 16 * count[s]
        OWNER[g] = last.get(s)
        last[s] = g


lay_stream()


NORMS = ("mem", "mix", "xa", "ffn", "fin")
TURNS = ("mem", "mix", "xa", "ffn", "m0", "m1", "m2", "m3")
LNS = ("ln0", "ln1", "ln2", "ln3")
ATTNS = {"aa": (2, 9), "bb": (2, 8), "cc": (4, 8)}
SHARES = {}
for _kind, _per in (("sq", 2), ("root", 1), ("xn", 2)):
    SHARES[_kind] = [(st, _per) for st in NORMS]
for _kind in ("T", "xt_a", "xt_v"):
    SHARES[_kind] = [(st, 4) for st in TURNS]
for _kind, _per in (("ln_var", 1), ("ln_root", 1), ("ln_x", 2), ("ln_landed", 32), ("gate_diag", 1), ("gate_mm", 1),
                    ("gate", 2)):
    SHARES[_kind] = [(st, _per) for st in LNS]
for _kind, _per in (("sc", 4), ("s", 4), ("nm", 1), ("p", 2), ("pt", 4), ("pte", 4), ("o", 1), ("ot", 1)):
    SHARES[_kind] = [(st, _per * g) for st, (g, _) in ATTNS.items()]
SHARES["e"] = [(st, g * n) for st, (g, n) in ATTNS.items()]
for _kind, _per in (("mlp_zero", 4), ("mlp_h", 8), ("mlp_relu", 16), ("mlp_sq", 16)):
    SHARES[_kind] = [(st, _per) for st in ("mlp0", "mlp1")]


def base_of(st, kind):
    at = 0
    for name, n in SHARES[kind]:
        if name == st:
            return at
        at += n
    raise KeyError(st)


def build_program(nc, A, tab_d, dft_d, out_d):
    ctx = ExitStack()
    with ctx:
        sems = {}

        def sem(name):
            if name not in sems:
                sems[name] = ctx.enter_context(nc.semaphore(name))
            return sems[name]

        def done(name, i):
            g = PRE.index((name, i)) if (name, i) in PRE else MOE_END + POST.index((name, i))
            return sem("granules_used"), g + 1

        def upto(st, kind, v):
            return sem(kind), v + base_of(st, kind)

        def sb(name, shape, dt=F32):
            return ctx.enter_context(nc.sbuf_tensor("sb_" + name, shape, dt))

        B = [ctx.enter_context(nc.psum_tensor(f"bank{i}", [P, HW], F32)) for i in range(8)]
        ring = sb("ring", [P, R2 * SLOT])
        tab = sb("tab", [P, TAB_W])
        X = sb("X", [P, TB, D])
        XN = sb("XN", [P, TB, D])
        XT = sb("XT", [P, KC, S])
        arena = sb("arena", [P, 5 * 2048])
        vec = sb("vec", [P, 2, P])
        col = sb("col", [P, NVEC])
        ada_bT = sb("ada_bT", [P, NADA * 24])
        mod = sb("mod", [P, NADA, 24])
        cs = sb("cs", [P, KC, 32])
        sil = sb("sil", [P, 2, 8])
        stat = sb("stat", [P, 128])
        pos = sb("pos", [P, NB_MAX, NE + 1, TB])
        gat = sb("gat", [P, NE + 1, TB])
        logit = sb("logit", [P, TB, 40])
        rt = sb("rt", [P, 6, 64])
        brow = sb("brow", [P, NE])
        wr = sb("wr", [P, KC, NE])
        table_i = sb("table_i", [1, 40], I32)
        ropeC = sb("ropeC", [P, TB, HD])
        ropeS = sb("ropeS", [P, TB, HD])
        posi = sb("posi", [P, TB], I32)
        sinkb = sb("sinkb", [P, 8])
        att = sb("att", [P, 6, 16])
        mrep = vec[:, :, 0:NCAND]
        flag = sb("flag", [NCAND, 1])[:]
        chosen = sb("chosen", [NCAND, NX_MAX])[:]

        def tb_(n):
            a, b = T_COLS[n]
            return tab[:, a:b]

        ident, tri, ones, quads, iota = (tb_(n) for n in ("ident", "tri", "ones", "quads", "iota"))
        eps5, eps6, zero = tb_("eps5"), tb_("eps6"), tb_("zero")

        def slot(s, w=SLOT):
            return ring[:, s * SLOT:s * SLOT + w]

        def arn(a, w):
            return arena[:, a:a + w]

        ext = ring[:, 6 * SLOT:8 * SLOT]
        MEM = arn(0, 2048).rearrange("p (t d) -> p t d", t=TB)
        MEMN = arn(2048, 2048).rearrange("p (t d) -> p t d", t=TB)
        MEMT = arn(4096, 2048).rearrange("p (k s) -> p k s", k=KC)
        KT = ext[:, 0:2048].rearrange("p (k s) -> p k s", k=KC)
        V = ext[:, 2048:4096].rearrange("p (t d) -> p t d", t=TB)
        dft = ext[:, 4096:5120].rearrange("p (t n) -> p t n", t=TB)
        ada_part = ext[:, 5120:6144].rearrange("p (i n) -> p i n", i=2)
        QT = ext[:, 6144:8192].rearrange("p (k s) -> p k s", k=KC)
        CT = arn(0, 1024)
        U = arn(1024, 1024).rearrange("p (t n) -> p t n", t=TB)
        SQ = arn(2048, 2048).rearrange("p (k s) -> p k s", k=8)
        FT = arn(4096, 2048).rearrange("p (k n) -> p k n", k=4)
        GP = arn(6144, 4 * (S + 2)).rearrange("p (k s) -> p k s", k=4)
        RMS = arn(7300, 512).rearrange("p (k s) -> p k s", k=2)
        YT = arn(8192, 2048).rearrange("p (k s) -> p k s", k=8)
        PR = arn(0, 2048).rearrange("p (h t m) -> p h t m", h=4, t=TB)
        PRT = arn(2048, 2048).rearrange("p (h m s) -> p h m s", h=4, m=2)
        OT = arn(4096, 2048).rearrange("p (k s) -> p k s", k=KC)
        bias = arn(0, 3 * D)
        gcl, ucl, sig, gl, hh_ = (arn(3072 + 512 * i, 512) for i in range(5))
        hT = arn(5632, 512).rearrange("p (c n) -> p c n", c=4)
        ysb = arn(6144, 512)
        sel_tok = arn(6656, TB * CAP).rearrange("p (t n) -> p t n", t=TB)
        wsel = arn(6784, TB * P).rearrange("p (t n) -> p t n", t=TB)
        wselT = arn(7040, 2 * TB * P).rearrange("p (h t n) -> p h t n", h=2, t=TB)
        selG = arn(7552, CAP)
        selD = arn(7616, CAP)
        xe = arn(7680, KC * CAP).rearrange("p (k n) -> p k n", k=KC)
        nfin = arn(8192, D)
        Z = arn(0, 2 * 1224).rearrange("p (t n) -> p t n", t=TB)
        R1b = arn(2448, 1280)
        R2b = arn(3728, 512).rearrange("p (t n) -> p t n", t=TB)
        R4b = arn(4240, 1024)
        aqT = arn(5264, 1024).rearrange("p (k s) -> p k s", k=4)
        bqT = arn(6288, 1024).rearrange("p (k s) -> p k s", k=4)
        iqT = arn(7312, 1024).rearrange("p (k s) -> p k s", k=4)
        akT = arn(8336, 256)
        bkT = arn(8592, 256)
        ikT = arn(8848, 256)
        OTa = arn(9104, 1024).rearrange("p (k s) -> p k s", k=4)
        OTb = R4b.rearrange("p (k s) -> p k s", k=4)
        lng = arn(5264, D)
        lnb = arn(6288, D)
        hid = arn(0, 1024).rearrange("p (k s) -> p k s", k=4)

        XNf = XN[:].rearrange("p t d -> p (t d)")
        XTf = XT[:].rearrange("p k s -> p (k s)")
        SC = XNf[:, 0:1536].rearrange("p (h n) -> p h n", h=4)
        idx = XNf[:, 1536:1920]
        PT = XTf[:, 0:1536].rearrange("p (h n) -> p h n", h=4)
        bmask = XTf[:, 1536:1920]
        relu_i = R1b[:, 0:768].rearrange("p (i n) -> p i n", i=2)
        left = R1b[:, 768:1152]

        used = sem("granules_used")
        landed = [sem(f"slot{s}_landed") for s in range(R2)]

        def kview(a, k):
            return a.rearrange("(k p) n -> p k n", p=P)

        W2 = {n: kview(A[n][0], KC) for n in ("w_k", "w_v", "w_in", "w_out", "w_q", "w_o", "ab_w_in_2",
                                              "ab_w_out_2", "c_w_in_2", "c_w_out_2")}

        def granule_source(name, i, s):
            if name in ("w_k", "w_v", "w_out", "w_q", "w_o"):
                return [(slot(s).rearrange("p (k n) -> p k n", k=4), W2[name][:, 4 * i:4 * i + 4, :])]
            if name == "w_in":
                return [(slot(s).rearrange("p (k n) -> p k n", k=2), W2[name][:, 2 * i:2 * i + 2, :])]
            if name == "ada":
                a, nb = i // 6, i % 6
                src = A["ada_w_2"][a // 2, a % 2].rearrange("(k p) n -> p k n", p=P)
                return [(slot(s).rearrange("p (k n) -> p k n", k=8), src[:, :, HW * nb:HW * nb + HW])]
            if name == "ab_in":
                k = min(3, KC - 3 * i)
                return [(slot(s, k * 1224).rearrange("p (k n) -> p k n", k=k), W2["ab_w_in_2"][:, 3 * i:3 * i + k, :])]
            if name == "uq":
                return [(slot(s)[:, j * 1024:(j + 1) * 1024].rearrange("p (k n) -> p k n", k=2),
                         kview(A[w][0], 2)) for j, w in enumerate(("ab_w_uq_2", "ab_w_uiq_2"))]
            if name in ("ab_out", "c_out"):
                w = W2["ab_w_out_2" if name == "ab_out" else "c_w_out_2"]
                return [(slot(s).rearrange("p (k n) -> p k n", k=4), w[:, 4 * i:4 * i + 4, :])]
            assert name == "c_in"
            return [(slot(s).rearrange("p (k n) -> p k n", k=4),
                     W2["c_w_in_2"][:, 4 * (i % 2):4 * (i % 2) + 4, D * (i // 2):D * (i // 2) + D])]

        block = ctx.enter_context(nc.Block())

        @block.sync
        def _(sp):
            sp.dma_start(tab[:], tab_d).then_inc(sem("tab_landed"), 16)
            sp.dma_start(MEM, A["mem"][0].rearrange("(t p) d -> p t d", p=P)).then_inc(sem("mem_landed"), 16)
            sp.dma_start(X[:], A["x"][0].rearrange("(t p) d -> p t d", p=P)).then_inc(sem("x_landed"), 16)

            def fill(g, name, i):
                if OWNER[g] is not None:
                    sp.wait_ge(used, OWNER[g] + 1)
                for dst, src in granule_source(name, i, slot_of(g)):
                    sp.dma_start(dst, src).then_inc(landed[slot_of(g)], 16)

            for g, (name, i) in enumerate(PRE):
                fill(g, name, i)
                if g == 3:
                    sp.dma_start(dft, dft_d.rearrange("(t p) n -> p t n", p=P)).then_inc(sem("dft_landed"), 16)

            def expert_slot(j):
                return slot_of(NPRE + j)

            def expert_source(j, e):
                if j < 4:
                    return A["w_gate_up"][0, bass.ds(e, 1), 2 * P * j:2 * P * (j + 1), :].rearrange(
                        "e (k p) n -> p (e k) n", p=P)
                return A["w_down"][0, bass.ds(e, 1), 4 * P * (j - 4):4 * P * (j - 3), :].rearrange(
                    "e (k p) n -> p (e k) n", p=P)

            with sp.Fori(0, NE) as e:
                for j in range(PER_E):
                    s = expert_slot(j)
                    sp.wait_ge(used, e * PER_E + (OWNER[NPRE + j] + 1))
                    sp.dma_start(slot(s).rearrange("p (k n) -> p k n", k=2 if j < 4 else 4),
                                 expert_source(j, e)).then_inc(landed[s], 16)

            sp.wait_ge(sem("table_ready"), 1)
            n = nc.values_load(table_i[0:1, 32:33], engines=[ENG.SP], min_val=0, max_val=NX_MAX)
            with sp.If(n > 0):
                sp.wait_ge(used, MOE_END)
                with sp.Fori(0, n) as i:
                    e = nc.values_load(table_i[0:1, bass.ds(i, 1)], engines=[ENG.SP], min_val=0, max_val=NE - 1)
                    sp.wait_ge(sem("extra_used"), i + 1)
                    for j in range(PER_E):
                        sp.dma_start(slot(expert_slot(j)).rearrange("p (k n) -> p k n", k=2 if j < 4 else 4),
                                     expert_source(j, e)).then_inc(sem("extra_landed"), 16)
                sp.wait_ge(sem("moe_x"), 1)

            g = MOE_END
            for name, count in (("ab_in", 3), ("uq", 1), ("ab_out", 2), ("mlp0", 16), ("c_in", 6), ("c_out", 2),
                                ("mlp1", 16)):
                if name[:3] != "mlp":
                    for i in range(count):
                        if OWNER[g] is None:
                            sp.wait_ge(used, NPRE)
                        fill(g, name, i)
                        g += 1
                    continue
                l = int(name[3])
                w1 = A["mlp_w1_2"][l].rearrange("(k p) n -> p k n", p=P)
                w2 = A["mlp_w2_2"][l].rearrange("(k p) n -> p k n", p=P)
                with sp.Fori(0, 2) as i:
                    for j in range(R2):
                        s = slot_of(g + j)
                        sp.wait_ge(used, i * R2 + (OWNER[g + j] + 1))
                        if j % 2 == 0:
                            src = w1[:, :, bass.ds(i * (4 * HW) + (j // 2) * HW, HW)]
                            dst = slot(s).rearrange("p (k n) -> p k n", k=8)
                        else:
                            src = w2[:, bass.ds(i * 16 + (j // 2) * 4, 4), :]
                            dst = slot(s).rearrange("p (k n) -> p k n", k=4)
                        sp.dma_start(dst, src).then_inc(landed[s], 16)
                g += 16
            sp.wait_ge(*upto("ln3", "ln_x", 2))
            sp.dma_start(out_d[0].rearrange("(t p) d -> p t d", p=P), X[:]).then_inc(sem("stored"), 16)
            sp.wait_ge(sem("stored"), 16)

        @block.gpsimd
        def _(pool):
            pool.memset(GP[:, :, 0:1], 0.0).then_inc(sem("conv_pad"), 1)
            pool.memset(GP[:, :, S + 1:S + 2], 0.0).then_inc(sem("conv_pad"), 1)
            pool.wait_ge(sem("wo_x"), 4)
            pool.memset(bias, 0.0).then_inc(sem("moe_zero"), 1)
            pool.memset(ysb, 0.0).then_inc(sem("e_y"), 1)
            pool.memset(arn(7040, 512), 0.0).then_inc(sem("moe_zero"), 1)
            pool.memset(stat[:, 127:128], 0.0).then_inc(sem("extra_used"), 1)

        @block.scalar
        def _(act):
            def vec_rows(name, ap):
                n = ap.shape[0]
                act.dma_start(vec[VEC[name]:VEC[name] + n, 0, :], ap).then_inc(sem("vec_landed"), 16)

            def rows(ap):
                return ap.rearrange("(k p) -> k p", p=P)

            for n in ("norm_mem", "norm_mix", "norm_xattn", "norm_ffn", "g_conv_out", "g_fft_out", "ab_q_norm_2"):
                vec_rows(n, rows(A[n][0]))
            vec_rows("conv_w", A["conv_w"][0].rearrange("t (k p) -> (t k) p", p=P))
            vec_rows("c_2", rows(A["c_2"][0]))
            act.dma_start(vec[0:NADA * 24, 1, :], A["ada_b_2"].rearrange("a b (k p) -> (a b k) p", p=P)).then_inc(
                sem("vec_landed"), 16)
            act.dma_start(wr[:], kview(A["w_router"][0], KC)).then_inc(sem("router_landed"), 16)
            act.dma_start(brow[:], A["b_router"][0:1, :].to_broadcast((P, NE))).then_inc(sem("router_landed"), 16)
            for t in range(TB):
                act.dma_start(posi[:, t:t + 1], A["positions_2"][0, t * P:(t + 1) * P, None]).then_inc(
                    sem("pos_landed"), 16)
            act.dma_start(sinkb[:], A["ab_sinks_2"][0:1, :].to_broadcast((P, 8))).then_inc(sem("sink_landed"), 16)

            def norm_stats(st, src, junk, at, ready):
                act.wait_ge(*ready)
                for t in range(TB):
                    act.activation(junk[:, t, :], src[:, t, :], ACT.Square, bias=zero,
                                   accum_out=stat[:, at + t:at + t + 1]).then_inc(sem("sq"), 1)
                act.wait_ge(*upto(st, "sq", TB))
                act.activation(stat[:, at + 2:at + 4], stat[:, at:at + 2], ACT.Sqrt, bias=eps5,
                               scale=1.0 / D).then_inc(sem("root"), 1)

            def evac_T(st, base, XTo, g1, g0=None):
                for n, q in enumerate((0, 2)):
                    act.wait_ge(*upto(st, "T", q + 1))
                    for r in range(2):
                        k = 2 * q + r
                        src = B[base + q][:, r * S:(r + 1) * S]
                        if g0 is None:
                            act.activation(XTo[:, k, :], src, ACT.Copy, scale=g1(k)).then_inc(sem("xt_a"), 1)
                        else:
                            act.activation(XTo[:, k, :], src, ACT.Identity, scale=g1(k),
                                           bias=g0(k)).then_inc(sem("xt_a"), 1)

            unit = [0]

            def ada(n):
                for _ in range(n):
                    u = unit[0]
                    unit[0] += 1
                    act.wait_ge(*done("ada", u))
                    if u >= 2:
                        act.wait_ge(sem("ada_comb"), u - 1)
                    act.activation(ada_part[:, u % 2, :], B[6][:], ACT.Copy).then_inc(sem("ada_part"), 1)

            def gain(name):
                return lambda k: col[:, VEC[name] + k:VEC[name] + k + 1]

            act.wait_ge(sem("tab_landed"), 16)
            norm_stats("mem", MEM, MEMN, 0, (sem("mem_landed"), 16))
            norm_stats("mix", X, XN, 4, (sem("x_landed"), 16))
            act.wait_ge(sem("vecT"), 1)
            act.activation(col[:], B[4][:, 0:NVEC], ACT.Copy).then_inc(sem("col_ready"), 1)
            act.activation(ada_bT[:], B[4][:, 128:128 + NADA * 24], ACT.Copy).then_inc(sem("col_ready"), 1)
            act.wait_ge(sem("col_ready"), 2)
            act.activation(sil[:, 0, :], col[:, VEC["c_2"]:VEC["c_2"] + 8], ACT.Sigmoid,
                           bias=zero).then_inc(sem("c_sig"), 1)
            evac_T("mem", 0, MEMT, gain("norm_mem"))
            act.wait_ge(*done("w_k", 1))
            for i in range(4):
                act.activation(KT[:, 2 * i:2 * i + 2, :], B[4 + i][:].rearrange("p (k s) -> p k s", k=2),
                               ACT.Copy).then_inc(sem("kT"), 1)
            evac_T("mix", 4, XT, gain("norm_mix"))
            act.wait_ge(*done("w_in", 3))
            for i in range(2):
                act.activation(CT[:, i * HW:(i + 1) * HW], B[2 + i][:], ACT.Copy).then_inc(sem("mix_c"), 1)
            for t in range(TB):
                act.activation(U[:, t, :], B[6 + t][:], ACT.Copy).then_inc(sem("mix_u"), 1)
            ada(5)
            act.wait_ge(sem("fft_seq"), 1)
            for i, b in enumerate((2, 3, 4, 5)):
                act.activation(FT[:, i, :], B[b][:], ACT.Copy).then_inc(sem("fft_ev"), 1)
            ada(3)
            act.wait_ge(sem("conv_y"), 2)
            act.activation(SQ[:, 0:4, :], YT[:, 0:4, :], ACT.Square, bias=zero).then_inc(sem("mix_sq"), 1)
            ada(2)
            act.wait_ge(sem("fft_y"), 2)
            act.activation(SQ[:, 4:8, :], YT[:, 4:8, :], ACT.Square, bias=zero).then_inc(sem("mix_sq"), 1)
            act.wait_ge(sem("mix_ss"), 1)
            act.activation(RMS[:, 0:2, :], B[4][:].rearrange("p (k s) -> p k s", k=2), ACT.Sqrt, bias=eps5,
                           scale=1.0 / 512).then_inc(sem("mix_rms"), 1)
            ada(2)
            norm_stats("xa", X, XN, 8, (sem("wout_x"), 4))
            ada(2)
            evac_T("xa", 0, XT, gain("norm_xattn"))
            act.wait_ge(*done("w_q", 1))
            for i in range(4):
                act.activation(QT[:, 2 * i:2 * i + 2, :], B[i][:].rearrange("p (k s) -> p k s", k=2), ACT.Copy).then_inc(sem("qT"), 1)
            ada(1)
            for h in range(4):
                act.wait_ge(sem("xa_nm"), h + 1)
                for t in range(TB):
                    act.activation(PR[:, h, t, :], B[h][:, t * S:(t + 1) * S], ACT.Exp, scale=1.0 / 16,
                                   bias=att[:, 0, 2 * h + t:2 * h + t + 1],
                                   accum_out=att[:, 1, 2 * h + t:2 * h + t + 1]).then_inc(sem("xa_e"), 1)
            ada(3)
            for h in range(4):
                act.wait_ge(sem("xa_pt"), h + 1)
                act.activation(PRT[:, h, :, :], B[h][:].rearrange("p (m s) -> p m s", m=2), ACT.Copy).then_inc(
                    sem("xa_pte"), 1)
            for h in range(4):
                act.wait_ge(sem("xa_o"), h + 1)
                act.activation(OT[:, 2 * h:2 * h + 2, :], B[(4, 5, 0, 1)[h]][:].rearrange("p (m s) -> p m s", m=2),
                               ACT.Copy).then_inc(sem("xa_ot"), 1)
            norm_stats("ffn", X, XN, 12, (sem("wo_x"), 4))
            ada(2)
            evac_T("ffn", 0, XT, gain("norm_ffn"))
            act.wait_ge(sem("moe_zero"), 1)
            act.dma_start(bias[0:NE, 0:2 * D], A["b_gate_up"][0]).then_inc(sem("bias_landed"), 16)
            act.dma_start(bias[0:NE, 2 * D:3 * D], A["b_down"][0]).then_inc(sem("bias_landed"), 16)
            act.dma_start(nfin, A["norm_final"][None, :].to_broadcast((P, D))).then_inc(sem("nfin_landed"), 16)
            act.wait_ge(sem("rt_nm"), TB)
            for t in range(TB):
                act.activation(rt[:, t, 0:NE], logit[:, t, 0:NE], ACT.Exp,
                               bias=att[:, 2, t:t + 1]).then_inc(sem("rt_e"), 1)
            ada(4)

            def expert(i, down_done):
                act.wait_ge(sem("e_clamp"), 2 * i + 1)
                act.activation(sig, gcl, ACT.Sigmoid, bias=zero, scale=1.702).then_inc(sem("e_sig"), 1)
                act.wait_ge(sem("e_wT"), i + 1)
                act.activation(wselT[0:CAP, 0], B[2][0:CAP, 0:TB * P].rearrange("p (t n) -> p t n", t=TB),
                               ACT.Copy).then_inc(sem("e_wTe"), 1)
                act.activation(wselT[CAP:P, 1], B[2][CAP:P, 0:TB * P].rearrange("p (t n) -> p t n", t=TB),
                               ACT.Copy).then_inc(sem("e_wTe"), 1)
                act.wait_ge(sem("e_hT"), i + 1)
                act.activation(hT, B[3][:].rearrange("p (c n) -> p c n", c=4), ACT.Copy).then_inc(sem("e_hTe"), 1)
                act.wait_ge(*down_done)
                act.activation(ysb, B[2][:], ACT.Copy).then_inc(sem("e_y"), 1)

            with act.Fori(0, NE) as i:
                expert(i, (used, i * PER_E + (NPRE + PER_E)))
            act.wait_ge(sem("table_ready"), 1)
            n = nc.values_load(table_i[0:1, 32:33], engines=[ENG.Activation], min_val=0, max_val=NX_MAX)
            with act.If(n > 0):
                with act.Fori(0, n) as i:
                    expert(i + NE, (sem("x_down"), i + 1))

            norm_stats("fin", X, XN, 16, (sem("moe_x"), 4))

            act.wait_ge(sem("rope_ang"), 1)
            act.activation(ropeS[:, :, 32:64], ropeS[:, :, 32:64], ACT.Sin, bias=zero).then_inc(sem("rope_sc"), 1)
            act.activation(ropeC[:, :, 0:32], ropeC[:, :, 0:32], ACT.Sin, bias=tb_("halfpi"),
                           scale=-1.0).then_inc(sem("rope_sc"), 1)

            def modcol(a):
                return (lambda k: mod[:, a, 8 + k:9 + k]), (lambda k: mod[:, a, k:k + 1])

            def load_ln(l, ready):
                act.wait_ge(*ready)
                act.dma_start(lng, A["ln_g_2"][l // 2, l % 2, None, :].to_broadcast((P, D))).then_inc(sem("ln_landed"), 16)
                act.dma_start(lnb, A["ln_b_2"][l // 2, l % 2, None, :].to_broadcast((P, D))).then_inc(sem("ln_landed"), 16)

            def gate_rows(l):
                act.wait_ge(*upto(f"ln{l}", "gate_mm", 1))
                for h in range(2):
                    act.activation(XN[:, 1, h * HW:(h + 1) * HW], B[6 + h][:], ACT.Copy).then_inc(sem("gate"), 1)

            def ln_root(l):
                act.wait_ge(*upto(f"ln{l}", "ln_var", 1))
                act.activation(att[:, 5, 4:6], att[:, 5, 0:4].rearrange("p (t n) -> p t n", t=2)[:, :, 1], ACT.Sqrt,
                               bias=eps5).then_inc(sem("ln_root"), 1)

            def attend(st, heads, sink, ot):
                for g in range(heads // 4):
                    act.wait_ge(*upto(st, "nm", g + 1))
                    for h in range(4):
                        for t, (a, b) in enumerate(((0, P), (P, 3 * P))):
                            act.activation(SC[:, h, a:b], SC[:, h, a:b], ACT.Exp, bias=att[:, 1, 4 * t + h:4 * t + h + 1],
                                           accum_out=att[:, 2, 4 * t + h:4 * t + h + 1]).then_inc(sem("e"), 1)
                    if sink:
                        act.activation(att[:, 4, 0:8], att[:, 3, 0:8], ACT.Exp, bias=zero).then_inc(sem("e"), 1)
                    for h in range(4):
                        act.wait_ge(*upto(st, "pt", 4 * g + h + 1))
                        act.activation(PT[:, h, :], B[4 + h % 2][:, 0:3 * P], ACT.Copy).then_inc(sem("pte"), 1)
                    act.wait_ge(*upto(st, "o", g + 1))
                    act.activation(ot[:, 2 * g:2 * g + 2, :], B[6 + g % 2][:].rearrange("p (m s) -> p m s", m=2),
                                   ACT.Copy).then_inc(sem("ot"), 1)

            evac_T("m0", 0, XT, *modcol(0))
            act.wait_ge(*done("ab_in", 2))
            for c in range(3):
                act.activation(Z[:, 0, 408 * c:408 * c + 408], B[c][:, 0:408], ACT.Copy).then_inc(sem("z0"), 1)
            act.wait_ge(sem("z0"), 3)
            act.wait_ge(sem("z1"), 3)
            for t in range(TB):
                act.activation(XN[:, t, 0:256], Z[:, t, 768:1024], ACT.Square, bias=zero,
                               accum_out=stat[:, 20 + t:21 + t]).then_inc(sem("cq_sq"), 1)
            act.wait_ge(sem("cq_sq"), TB)
            act.activation(stat[:, 22:24], stat[:, 20:22], ACT.Sqrt, bias=eps6, scale=1.0 / 256).then_inc(sem("cq_root"), 1)
            act.wait_ge(sem("a_T"), 1)
            act.activation(aqT[:, 0:2, :], B[6][:].rearrange("p (m s) -> p m s", m=2), ACT.Copy).then_inc(sem("a_Te"), 1)
            act.activation(aqT[:, 2:4, :], B[7][:].rearrange("p (m s) -> p m s", m=2), ACT.Copy).then_inc(sem("a_Te"), 1)
            act.wait_ge(sem("k_T"), 1)
            act.activation(akT, B[4][:, 0:S], ACT.Copy).then_inc(sem("k_Te"), 1)
            act.activation(bkT, B[4][:, S:2 * S], ACT.Copy).then_inc(sem("k_Te"), 1)
            act.activation(ikT, B[5][:, 0:S], ACT.Copy).then_inc(sem("k_Te"), 1)
            act.wait_ge(sem("i_T"), 1)
            act.activation(iqT[:, 0:2, :], B[6][:].rearrange("p (m s) -> p m s", m=2), ACT.Copy).then_inc(sem("i_Te"), 1)
            act.activation(iqT[:, 2:4, :], B[7][:].rearrange("p (m s) -> p m s", m=2), ACT.Copy).then_inc(sem("i_Te"), 1)
            act.wait_ge(sem("b_T"), 1)
            act.activation(bqT[:, 0:2, :], B[4][:].rearrange("p (m s) -> p m s", m=2), ACT.Copy).then_inc(sem("b_Te"), 1)
            act.activation(bqT[:, 2:4, :], B[5][:].rearrange("p (m s) -> p m s", m=2), ACT.Copy).then_inc(sem("b_Te"), 1)
            for h in range(8):
                act.wait_ge(sem("ix_mm"), h + 1)
                if h >= 2:
                    act.wait_ge(sem("ix_acc"), 2 * (h - 1))
                act.activation(relu_i[:, h % 2, :], B[h % 4][:, 0:3 * P], ACT.Relu, bias=zero).then_inc(sem("ix_relu"), 1)
            attend("aa", 8, True, OTa)
            attend("bb", 8, False, OTb)
            gate_rows(0)
            load_ln(0, upto("bb", "o", 2))
            ln_root(0)
            evac_T("m1", 0, XT, *modcol(1))
            gate_rows(1)
            load_ln(1, upto("ln0", "ln_x", 2))
            ln_root(1)
            evac_T("m2", 0, XT, *modcol(2))
            act.wait_ge(*done("c_in", 5))
            for i in range(4):
                act.activation(arn(8192 + HW * i, HW), B[i][:], ACT.Copy).then_inc(sem("cv"), 1)
            for m, dst in enumerate((arn(4096, 2048), arn(6144, 2048))):
                for i in range(4):
                    act.wait_ge(sem("c_T"), 4 * m + i + 1)
                    act.activation(dst[:, HW * i:HW * i + HW], B[4 + i][:], ACT.Copy).then_inc(sem("c_Te"), 1)
            attend("cc", 16, False, arn(0, 2048).rearrange("p (k s) -> p k s", k=KC))
            gate_rows(2)
            load_ln(2, upto("cc", "o", 4))
            ln_root(2)
            evac_T("m3", 0, XT, *modcol(3))
            gate_rows(3)
            load_ln(3, upto("ln2", "ln_x", 2))
            ln_root(3)


        @block.tensor
        def _(pe):
            at = [0]

            def granule(w=SLOT):
                g = at[0]
                at[0] += 1
                pe.wait_ge(landed[slot_of(g)], FILL[g])
                return slot(slot_of(g), w)

            def transpose_x(st, base, src, ready):
                pe.wait_ge(*ready)
                for q in range(4):
                    for r in range(2):
                        for t in range(TB):
                            k = 2 * q + r
                            mm = pe.transpose(B[base + q][:, r * S + t * P:r * S + t * P + P],
                                              src[:, t, k * P:(k + 1) * P], ident)
                    mm.then_inc(sem("T"), 1)

            def xt_ready(st):
                pe.wait_ge(*upto(st, "xt_a", 4))
                pe.wait_ge(*upto(st, "xt_v", 4))

            def project_T(XTi, base):
                for j in range(2):
                    w = granule().rearrange("p (k n) -> p k n", k=4)
                    for kl in range(4):
                        k = 4 * j + kl
                        for f in range(8):
                            mm = pe.matmul(B[base + f // 2][:, (f % 2) * S:(f % 2) * S + S],
                                           w[:, kl, f * P:(f + 1) * P], XTi[:, k, :],
                                           start=(k == 0 and f % 2 == 0), stop=(k == KC - 1), skip_group_check=True)
                    mm.then_inc(used, 1)

            def project(XTi, base):
                for j in range(2):
                    w = granule().rearrange("p (k n) -> p k n", k=4)
                    for kl in range(4):
                        k = 4 * j + kl
                        for t in range(TB):
                            for h in range(2):
                                mm = pe.matmul(B[base + 2 * t + h][:], XTi(k)[:, t * P:(t + 1) * P],
                                               w[:, kl, h * HW:(h + 1) * HW], start=(k == 0), stop=(k == KC - 1))
                    mm.then_inc(used, 1)

            unit = [0]

            def ada(n):
                def combine(u):
                    pe.wait_ge(sem("ada_part"), u + 1)
                    if u:
                        pe.wait_ge(sem("ada_done"), u)
                    part = ada_part[:, u % 2, :]
                    for c in range(4):
                        mm = pe.matmul(B[7][:, c:c + 1], part[:, c * P:(c + 1) * P], quads[:, 0:1], start=True, stop=True)
                    mm.then_inc(sem("ada_comb"), 1)

                first = unit[0]
                for u in range(first, first + n):
                    w = granule().rearrange("p (k n) -> p k n", k=KC)
                    if u:
                        pe.wait_ge(sem("ada_part"), u)
                    for r in range(2):
                        for c in range(4):
                            mm = pe.matmul(B[6][32 * c:32 * c + 32, :], cs[:, 2 * c + r, :], w[:, 2 * c + r, :],
                                           start=(r == 0), stop=(r == 1))
                    mm.then_inc(used, 1)
                    if u > first:
                        combine(u - 1)
                combine(first + n - 1)
                unit[0] += n

            pe.wait_ge(sem("tab_landed"), 16)
            pe.wait_ge(sem("vec_landed"), 160)
            pe.transpose(B[4][:, 0:NVEC], vec[0:NVEC, 0, :], ident[0:NVEC, 0:NVEC])
            pe.transpose(B[4][:, P:P + NADA * 24], vec[0:NADA * 24, 1, :],
                         ident[0:NADA * 24, 0:NADA * 24]).then_inc(sem("vecT"), 1)
            transpose_x("mem", 0, MEMN, upto("mem", "xn", 2))
            xt_ready("mem")
            pe.wait_ge(sem("col_ready"), 2)
            project_T(MEMT, 4)
            project(lambda k: MEMT[:, k, :], 0)
            pe.wait_ge(sem("kT"), 4)
            transpose_x("mix", 4, XN, upto("mix", "xn", 2))
            xt_ready("mix")
            pe.wait_ge(sem("v"), 4)
            for j in range(4):
                w = granule().rearrange("p (k n) -> p k n", k=2)
                for kl in range(2):
                    k = 2 * j + kl
                    for f in range(12):
                        pe.matmul(B[f // 2][:, (f % 2) * S:(f % 2) * S + S], w[:, kl, f * P:(f + 1) * P],
                                  XT[:, k, :], start=(k == 0 and f % 2 == 0), stop=(k == KC - 1),
                                  skip_group_check=True)
                    for t in range(TB):
                        mm = pe.matmul(B[6 + t][:], XT[:, k, t * P:(t + 1) * P], w[:, kl, 1536:2048],
                                       start=(k == 0), stop=(k == KC - 1))
                mm.then_inc(used, 1)
            pe.wait_ge(sem("mix_u"), 2)
            pe.wait_ge(sem("cs"), 1)
            ada(5)
            pe.wait_ge(sem("dft_landed"), 16)
            pe.wait_ge(sem("mix_c"), 2)
            pe.wait_ge(sem("conv_g"), 2)
            for i, b in enumerate((2, 3, 4, 5)):
                for t in range(TB):
                    mm = pe.matmul(B[b][:], U[:, t, i * P:(i + 1) * P], dft[:, t, :], start=(t == 0), stop=(t == 1))
            mm.then_inc(sem("fft_seq"), 1)
            ada(3)
            pe.wait_ge(sem("fft_ev"), 4)
            for i in range(4):
                o = B[2 + i // 2][:, (i % 2) * S:(i % 2) * S + S]
                pe.matmul(o, tb_("cg"), FT[:, i, 0:S], start=True, stop=False)
                mm = pe.matmul(o, tb_("sg"), FT[:, i, S:2 * S], start=False, stop=True)
            mm.then_inc(sem("fft_grp"), 1)
            ada(2)
            for m in range(2):
                pe.wait_ge(sem("mix_sq"), m + 1)
                for i in range(4):
                    mm = pe.matmul(B[4][:, m * S:(m + 1) * S], ones, SQ[:, 4 * m + i, :], start=(i == 0), stop=(i == 3))
            mm.then_inc(sem("mix_ss"), 1)
            ada(2)
            pe.wait_ge(sem("mix_yn"), 8)
            project(lambda k: YT[:, k, :], 0)
            ada(2)
            transpose_x("xa", 0, XN, upto("xa", "xn", 2))
            xt_ready("xa")
            project_T(XT, 0)
            ada(1)
            pe.wait_ge(sem("qT"), 4)
            for h in range(4):
                for t in range(TB):
                    for c in range(2):
                        mm = pe.matmul(B[h][:, t * S:(t + 1) * S], QT[:, 2 * h + c, t * P:(t + 1) * P],
                                       KT[:, 2 * h + c, :], start=(c == 0), stop=(c == 1))
                mm.then_inc(sem("xa_s"), 1)
            ada(3)
            for h in range(4):
                pe.wait_ge(sem("xa_p"), 2 * h + 2)
                for m in range(2):
                    for t in range(TB):
                        mm = pe.transpose(B[h][:, m * S + t * P:m * S + t * P + P], PR[:, h, t, m * P:(m + 1) * P], ident)
                mm.then_inc(sem("xa_pt"), 1)
            for h in range(4):
                pe.wait_ge(sem("xa_pte"), h + 1)
                for c in range(2):
                    for m in range(2):
                        mm = pe.matmul(B[(4, 5, 0, 1)[h]][:, c * S:(c + 1) * S],
                                       V[:, m, h * 2 * P + c * P:h * 2 * P + c * P + P], PRT[:, h, m, :],
                                       start=(m == 0), stop=(m == 1))
                mm.then_inc(sem("xa_o"), 1)
            pe.wait_ge(sem("xa_ot"), 4)
            project(lambda k: OT[:, k, :], 0)
            ada(2)
            transpose_x("ffn", 0, XN, upto("ffn", "xn", 2))
            xt_ready("ffn")
            pe.wait_ge(sem("router_landed"), 32)
            for t in range(TB):
                for k in range(KC):
                    mm = pe.matmul(B[4][:, t * NE:(t + 1) * NE], XT[:, k, t * P:(t + 1) * P], wr[:, k, :],
                                   start=(k == 0), stop=(k == KC - 1))
            mm.then_inc(sem("logits"), 1)
            ada(4)
            assert at[0] == NPRE
            mask = [rt[:, 4 + t, 0:NE] for t in range(TB)]
            pe.wait_ge(sem("rt_mask"), 4)
            pe.matmul(B[5][:, 0:NE], tri, mask[0], start=True, stop=True)
            pe.matmul(B[5][:, NE:2 * NE], tri, mask[1], start=True, stop=False)
            pe.matmul(B[5][:, NE:2 * NE], ones, mask[0], start=False, stop=True)
            for t in range(TB):
                mm = pe.matmul(B[5][0:NCAND, 64:65], mrep[:, t, :], ones[:, 0:1], start=(t == 0), stop=(t == 1))
            mm.then_inc(sem("rt_pos"), 1)
            pe.wait_ge(sem("flag"), 1)
            pe.matmul(B[5][0:NCAND, 65:66], tri[0:NCAND, 0:NCAND], flag, start=True, stop=True).then_inc(sem("rank"), 1)
            pe.wait_ge(sem("chosen"), 1)
            pe.matmul(B[5][0:1, 96:112], tb_("cand_e")[0:NCAND, :], chosen, start=True, stop=True)
            pe.matmul(B[5][0:1, 112:128], tb_("cand_q")[0:NCAND, :], chosen, start=True, stop=True)
            pe.matmul(B[5][0:1, 128:129], ones[0:NCAND, 0:1], flag, start=True, stop=True).then_inc(sem("table_mm"), 1)

            def gather():
                for k in range(KC):
                    for t in range(TB):
                        mm = pe.matmul(B[3][:, k * CAP:(k + 1) * CAP], XN[:, t, k * P:(k + 1) * P], sel_tok[:, t, :],
                                       start=(t == 0), stop=(t == 1))
                mm.then_inc(sem("e_gather"), 1)

            def bias_gu():
                for m in range(2):
                    for h in range(2):
                        pe.matmul(B[m][CAP * h:CAP * h + CAP, :], selG, bias[:, m * D + h * HW:m * D + (h + 1) * HW],
                                  start=True, stop=False)

            def gate_up(j):
                w = slot(slot_of(NPRE + j)).rearrange("p (k n) -> p k n", k=2)
                for kl in range(2):
                    for m in range(2):
                        for h in range(2):
                            mm = pe.matmul(B[m][CAP * h:CAP * h + CAP, :], xe[:, 2 * j + kl, :],
                                           w[:, kl, m * D + h * HW:m * D + (h + 1) * HW],
                                           start=False, stop=(j == 3 and kl == 1))
                return mm

            def weights_T():
                for t in range(TB):
                    mm = pe.transpose(B[2][:, t * P:(t + 1) * P], wsel[:, t, :], ident)
                mm.then_inc(sem("e_wT"), 1)

            def hidden_T():
                for c in range(4):
                    mm = pe.transpose(B[3][:, c * P:(c + 1) * P], hh_[:, c * P:(c + 1) * P], ident)
                mm.then_inc(sem("e_hT"), 1)

            def bias_d():
                for h in range(2):
                    pe.matmul(B[2][CAP * h:CAP * h + CAP, :], selD, bias[:, 2 * D + h * HW:2 * D + (h + 1) * HW],
                              start=True, stop=False)

            def down(j):
                w = slot(slot_of(NPRE + 4 + j)).rearrange("p (k n) -> p k n", k=4)
                for c in range(4):
                    for h in range(2):
                        mm = pe.matmul(B[2][CAP * h:CAP * h + CAP, :], hT[:, c, CAP * j:CAP * j + CAP],
                                       w[:, c, h * HW:(h + 1) * HW], start=False, stop=(j == 1 and c == 3))
                return mm

            def scatter():
                for t in range(TB):
                    for h in range(2):
                        mm = pe.matmul(B[4 + 2 * t + h][:], wselT[:, h, t, :], ysb, start=False, stop=False,
                                       skip_group_check=True)
                return mm

            pe.wait_ge(sem("e_sel"), 2)
            gather()
            pe.wait_ge(sem("acc_zero"), 4)
            pe.wait_ge(sem("moe_zero"), 2)
            pe.wait_ge(sem("bias_landed"), 32)
            with pe.Fori(0, NE) as i:
                pe.wait_ge(sem("e_selG"), i + 1)
                pe.wait_ge(sem("e_xe"), i + 1)
                bias_gu()
                for j in range(4):
                    g = NPRE + j
                    pe.wait_ge(landed[slot_of(g)], i * 16 + FILL[g])
                    gate_up(j).then_inc(used, 1)
                    if j == 0:
                        pe.wait_ge(sem("e_y"), i + 1)
                        scatter()
                pe.wait_ge(sem("e_sel"), 2 * i + 4)
                gather()
                pe.wait_ge(sem("e_wsel"), 2 * i + 2)
                weights_T()
                pe.wait_ge(sem("e_xe"), i + 2)
                pe.wait_ge(sem("e_h"), i + 1)
                hidden_T()
                pe.wait_ge(sem("e_selD"), i + 1)
                pe.wait_ge(sem("e_wTe"), 2 * i + 2)
                bias_d()
                pe.wait_ge(sem("e_hTe"), i + 1)
                for j in range(2):
                    g = NPRE + 4 + j
                    pe.wait_ge(landed[slot_of(g)], i * 16 + FILL[g])
                    down(j).then_inc(used, 1)
            pe.wait_ge(sem("e_y"), NE + 1)
            scatter().then_inc(sem("acc_main"), 1)
            pe.wait_ge(sem("table_ready"), 1)
            n = nc.values_load(table_i[0:1, 32:33], engines=[ENG.PE], min_val=0, max_val=NX_MAX)
            with pe.If(n > 0):
                with pe.Fori(0, n) as i:
                    pe.wait_ge(sem("e_sel"), 2 * i + (2 * NE + 4))
                    gather()
                    pe.wait_ge(sem("e_selG"), i + (NE + 2))
                    pe.wait_ge(sem("e_xe"), i + (NE + 2))
                    bias_gu()
                    pe.wait_ge(sem("extra_landed"), 16 * PER_E * i + 16 * PER_E)
                    for j in range(4):
                        mm = gate_up(j)
                    mm.then_inc(sem("x_gu"), 1)
                    pe.wait_ge(sem("e_wsel"), 2 * i + (2 * NE + 2))
                    weights_T()
                    pe.wait_ge(sem("e_h"), i + (NE + 1))
                    hidden_T()
                    pe.wait_ge(sem("e_selD"), i + (NE + 1))
                    pe.wait_ge(sem("e_wTe"), 2 * i + (2 * NE + 2))
                    bias_d()
                    pe.wait_ge(sem("e_hTe"), i + (NE + 1))
                    for j in range(2):
                        mm = down(j)
                    mm.then_inc(sem("x_down"), 1)
                    pe.wait_ge(sem("e_y"), i + (NE + 2))
                    scatter().then_inc(sem("extra_used"), 1)
            at[0] = MOE_END

            def gate_rows(l):
                pe.wait_ge(*upto(f"ln{l}", "gate_diag", 1))
                for h in range(2):
                    mm = pe.matmul(B[6 + h][:], ones, XN[:, 0, h * HW:(h + 1) * HW], start=True, stop=True)
                mm.then_inc(sem("gate_mm"), 1)

            def attend(st, heads, q, k, v):
                def scores(g):
                    for h in range(4):
                        if g:
                            pe.wait_ge(*upto(st, "s", 4 * (g - 1) + h + 1))
                        a = 4 * g + h
                        pe.matmul(B[h][:, 0:P], q(a)[:, 0:P], k(a)[:, 0:P], start=True, stop=True)
                        pe.matmul(B[h][:, P:3 * P], q(a)[:, P:2 * P], k(a), start=True, stop=True).then_inc(
                            sem("sc"), 1)

                scores(0)
                for g in range(heads // 4):
                    if g + 1 < heads // 4:
                        scores(g + 1)
                    pe.wait_ge(*upto(st, "p", 2 * g + 2))
                    for h in range(4):
                        n = 4 * g + h
                        if n >= 2:
                            pe.wait_ge(*upto(st, "pte", n - 1))
                        for c in range(3):
                            mm = pe.transpose(B[4 + h % 2][:, c * P:(c + 1) * P], SC[:, h, c * P:(c + 1) * P], ident)
                        mm.then_inc(sem("pt"), 1)
                    if g >= 2:
                        pe.wait_ge(*upto(st, "ot", g - 1))
                    for h in range(4):
                        pe.wait_ge(*upto(st, "pte", 4 * g + h + 1))
                        a, r = 4 * g + h, 64 * (h % 2)
                        o = B[6 + g % 2][r:r + 64, (h // 2) * S:(h // 2) * S + S]
                        pe.matmul(o, v(a, 0), PT[:, h, 0:S], start=True, stop=False, skip_group_check=True)
                        mm = pe.matmul(o[:, P:S], v(a, 1), PT[:, h, S:3 * P], start=False, stop=True,
                                       skip_group_check=True)
                    mm.then_inc(sem("o"), 1)

            def mlp(l):
                n = f"mlp{l}"
                g0 = at[0]
                pe.wait_ge(*upto(n, "mlp_zero", 4))
                with pe.Fori(0, 2) as i:
                    for p in range(4):
                        g = g0 + 2 * p
                        pe.wait_ge(landed[slot_of(g)], i * 16 + FILL[g])
                        w = slot(slot_of(g)).rearrange("p (k n) -> p k n", k=KC)
                        for b in range(2):
                            for k in range(KC):
                                for r in range(2):
                                    f = 2 * b + r
                                    mm = pe.matmul(B[4 + b][:, r * S:(r + 1) * S], w[:, k, f * P:(f + 1) * P],
                                                   XT[:, k, :], start=(k == 0 and r == 0), stop=(k == KC - 1),
                                                   skip_group_check=True)
                            mm.then_inc(sem("mlp_h") if b == 0 else used, 1)
                        g = g + 1
                        pe.wait_ge(landed[slot_of(g)], i * 16 + FILL[g])
                        w = slot(slot_of(g)).rearrange("p (k n) -> p k n", k=4)
                        for b in range(2):
                            pe.wait_ge(*upto(n, "mlp_sq", i * 8 + (2 * p + b + 1)))
                            for r in range(2):
                                for t in range(TB):
                                    for h in range(2):
                                        mm = pe.matmul(B[2 * t + h][:], hid[:, 2 * b + r, t * P:(t + 1) * P],
                                                       w[:, 2 * b + r, h * HW:(h + 1) * HW], start=False, stop=False,
                                                       skip_group_check=True)
                        mm.then_inc(used, 1)
                at[0] = g0 + 16

            transpose_x("m0", 0, X, (sem("fin_x"), 4))
            xt_ready("m0")
            for j in range(3):
                kn = min(3, KC - 3 * j)
                w = granule(kn * 1224).rearrange("p (k n) -> p k n", k=kn)
                for kl in range(kn):
                    k = 3 * j + kl
                    for t in range(TB):
                        for c in range(3):
                            mm = pe.matmul(B[3 * t + c][:, 0:408], XT[:, k, t * P:(t + 1) * P],
                                           w[:, kl, 408 * c:408 * c + 408], start=(k == 0), stop=(k == KC - 1))
                mm.then_inc(used, 1)
            pe.wait_ge(sem("cq_n"), 2)
            for k in range(2):
                for t in range(TB):
                    mm = pe.transpose(B[6][:, k * S + t * P:k * S + t * P + P],
                                      XN[:, t, S + k * P:S + (k + 1) * P], ident)
            mm.then_inc(sem("cq_T"), 1)
            pe.wait_ge(sem("cqT"), 2)
            pe.wait_ge(sem("z0"), 3)
            pe.wait_ge(sem("z1"), 3)
            w = granule()
            for m in (1, 0):
                wm = w[:, m * 1024:(m + 1) * 1024].rearrange("p (k n) -> p k n", k=2)
                for t in range(TB):
                    for k in range(2):
                        mm = pe.matmul(B[2 * m + t][:], XTf[:, k * S + t * P:k * S + t * P + P], wm[:, k, :],
                                       start=(k == 0), stop=(k == 1))
                if m:
                    mm.then_inc(sem("iq_mm"), 1)
            mm.then_inc(used, 1)
            pe.wait_ge(sem("a_rope"), 2)
            R1a = R1b.rearrange("p (t n) -> p t n", t=TB)
            for j in range(4):
                for t in range(TB):
                    mm = pe.transpose(B[6 + j // 2][:, (j % 2) * S + t * P:(j % 2) * S + t * P + P],
                                      R1a[:, t, j * P:(j + 1) * P], ident)
            mm.then_inc(sem("a_T"), 1)
            pe.wait_ge(sem("k_rope"), 2)
            for t in range(TB):
                pe.transpose(B[4][:, t * P:(t + 1) * P], R1a[:, t, 512:640], ident)
                pe.transpose(B[4][:, S + t * P:S + (t + 1) * P], R2b[:, t, 0:P], ident)
                mm = pe.transpose(B[5][:, t * P:(t + 1) * P], R2b[:, t, P:2 * P], ident)
            mm.then_inc(sem("k_T"), 1)
            for m, (st, src, e) in enumerate((("i_", R4b, "a_Te"), ("b_", R1b, "k_Te"))):
                pe.wait_ge(sem(st + "rope"), 2)
                pe.wait_ge(sem(e), 2 + m)
                s2 = src[:, 0:1024].rearrange("p (t n) -> p t n", t=TB)
                for j in range(4):
                    for t in range(TB):
                        mm = pe.transpose(B[(6, 4)[m] + j // 2][:, (j % 2) * S + t * P:(j % 2) * S + t * P + P],
                                          s2[:, t, j * P:(j + 1) * P], ident)
                mm.then_inc(sem(st + "T"), 1)
            pe.wait_ge(sem("i_Te"), 2)
            pe.wait_ge(sem("k_Te"), 3)
            for h in range(8):
                if h >= 4:
                    pe.wait_ge(sem("ix_relu"), h - 3)
                r = 64 * (h % 2)
                pe.matmul(B[h % 4][:, 0:P], iqT[r:r + 64, h // 2, 0:P], ikT[r:r + 64, 0:P], start=True, stop=True)
                pe.matmul(B[h % 4][:, P:3 * P], iqT[r:r + 64, h // 2, P:S], ikT[r:r + 64, :], start=True,
                          stop=True).then_inc(sem("ix_mm"), 1)
            pe.wait_ge(sem("ix_relu"), 8)
            pe.wait_ge(sem("b_Te"), 2)
            attend("aa", 8, lambda a: aqT[64 * (a // 4):64 * (a // 4) + 64, a % 4, :],
                   lambda a: akT[64 * (a // 4):64 * (a // 4) + 64, :],
                   lambda a, t: Z[:, t, 640 + 64 * (a // 4):704 + 64 * (a // 4)])
            pe.wait_ge(*upto("aa", "s", 8))
            pe.wait_ge(*upto("aa", "ot", 2))
            attend("bb", 8, lambda a: bqT[64 * (a % 2):64 * (a % 2) + 64, a // 2, :],
                   lambda a: bkT[64 * (a % 2):64 * (a % 2) + 64, :], lambda a, t: Z[:, t, 1088:1152])
            pe.wait_ge(*upto("bb", "ot", 2))
            gate_rows(0)
            project(lambda k: OTa[:, k, :] if k < 4 else OTb[:, k - 4, :], 0)
            transpose_x("m1", 0, X, upto("ln0", "ln_x", 2))
            xt_ready("m1")
            gate_rows(1)
            mlp(0)
            transpose_x("m2", 0, X, upto("ln1", "ln_x", 2))
            xt_ready("m2")
            xk = lambda k: XT[:, k, :]
            project(xk, 0)
            project(xk, 4)
            pe.wait_ge(sem("c_rope"), 4)
            project(xk, 0)
            for m in range(2):
                pe.wait_ge(sem("c_rope"), 8)
                src = arn(2048 * m, 2048).rearrange("p (t n) -> p t n", t=TB)
                for q in range(4):
                    if m:
                        pe.wait_ge(sem("c_Te"), q + 1)
                    for r in range(2):
                        for t in range(TB):
                            k = 2 * q + r
                            mm = pe.transpose(B[4 + q][:, r * S + t * P:r * S + t * P + P],
                                              src[:, t, k * P:(k + 1) * P], ident)
                    mm.then_inc(sem("c_T"), 1)
            pe.wait_ge(sem("c_Te"), 8)
            pe.wait_ge(sem("cv"), 4)
            cqT = arn(4096, 2048).rearrange("p (k s) -> p k s", k=KC)
            ckT = arn(6144, 2048).rearrange("p (k s) -> p k s", k=KC)
            cv = arn(8192, 2048).rearrange("p (t n) -> p t n", t=TB)
            attend("cc", 16, lambda a: cqT[64 * (a % 2):64 * (a % 2) + 64, a // 2, :],
                   lambda a: ckT[64 * (a % 2):64 * (a % 2) + 64, a // 2, :], lambda a, t: cv[:, t, 64 * a:64 * a + 64])
            pe.wait_ge(*upto("cc", "ot", 4))
            gate_rows(2)
            cot = arn(0, 2048).rearrange("p (k s) -> p k s", k=KC)
            project(lambda k: cot[:, k, :], 0)
            transpose_x("m3", 0, X, upto("ln2", "ln_x", 2))
            xt_ready("m3")
            gate_rows(3)
            mlp(1)

        @block.vector
        def _(dve):
            steps = [0]

            def link(ins):
                steps[0] += 1
                ins.then_inc(sem("dve_step"), 1)
                dve.wait_ge(sem("dve_step"), steps[0])

            def gain(name):
                return lambda k: col[:, VEC[name] + k:VEC[name] + k + 1]

            def bc(ap, n):
                return ap[:, :, None].to_broadcast((P, ap.shape[1], n))

            def norm(st, src, dst, at):
                dve.wait_ge(*upto(st, "root", 1))
                link(dve.reciprocal(stat[:, 64 + at:66 + at], stat[:, at + 2:at + 4]))
                for t in range(TB):
                    dve.tensor_scalar(dst[:, t, :], src[:, t, :], stat[:, 64 + at + t:65 + at + t], None,
                                      ALU.mult).then_inc(sem("xn"), 1)

            def evac_T(st, base, XTo, g1, g0=None):
                for q in (1, 3):
                    dve.wait_ge(*upto(st, "T", q + 1))
                    for r in range(2):
                        k = 2 * q + r
                        src = B[base + q][:, r * S:(r + 1) * S]
                        if g0 is None:
                            ins = dve.tensor_scalar(XTo[:, k, :], src, g1(k), None, ALU.mult)
                        else:
                            ins = dve.tensor_scalar(XTo[:, k, :], src, g1(k), g0(k), ALU.mult, ALU.add)
                        ins.then_inc(sem("xt_v"), 1)

            unit = [0]

            def ada(n):
                for _ in range(n):
                    u = unit[0]
                    unit[0] += 1
                    a, nb = u // 6, u % 6
                    dve.wait_ge(sem("ada_comb"), u + 1)
                    dve.scalar_tensor_tensor(mod[:, a, 4 * nb:4 * nb + 4], B[7][:, 0:4], float(nb >= 2),
                                             ada_bT[:, 24 * a + 4 * nb:24 * a + 4 * nb + 4], ALU.add,
                                             ALU.add).then_inc(sem("ada_done"), 1)

            def add_residual(st, base, w):
                dve.wait_ge(*done(w, 1))
                for t in range(TB):
                    for h in range(2):
                        xs = X[:, t, h * HW:(h + 1) * HW]
                        dve.tensor_tensor(xs, B[base + 2 * t + h][:], xs, ALU.add).then_inc(sem(st), 1)

            norm("mem", MEM, MEMN, 0)
            norm("mix", X, XN, 4)
            dve.wait_ge(sem("c_sig"), 1)
            link(dve.tensor_tensor(sil[:, 1, :], sil[:, 0, :], col[:, VEC["c_2"]:VEC["c_2"] + 8], ALU.mult))
            dve.tensor_copy(cs[:], bc(sil[:, 1, :], 32)).then_inc(sem("cs"), 1)
            evac_T("mem", 0, MEMT, gain("norm_mem"))
            dve.wait_ge(*done("w_v", 1))
            for t in range(TB):
                for h in range(2):
                    dve.tensor_copy(V[:, t, h * HW:(h + 1) * HW], B[2 * t + h][:]).then_inc(sem("v"), 1)
            evac_T("mix", 4, XT, gain("norm_mix"))
            dve.wait_ge(sem("mix_c"), 2)
            for i in range(2):
                dve.tensor_tensor(GP[:, 2 * i:2 * i + 2, 1:S + 1], CT[:, i * HW:(i + 1) * HW].rearrange(
                    "p (k s) -> p k s", k=2), B[4 + i][:].rearrange("p (k s) -> p k s", k=2),
                    ALU.mult).then_inc(sem("conv_g"), 1)
            dve.wait_ge(sem("conv_g"), 2)
            dve.wait_ge(sem("conv_pad"), 2)
            cw = VEC["conv_w"]
            for tap in (1, 0, 2):
                for k in range(4):
                    wcol = col[:, cw + 4 * tap + k:cw + 4 * tap + k + 1]
                    g = GP[:, k, tap:tap + S]
                    if tap == 1:
                        ins = dve.tensor_scalar(YT[:, k, :], g, wcol, None, ALU.mult)
                    else:
                        ins = dve.scalar_tensor_tensor(YT[:, k, :], g, wcol, YT[:, k, :], ALU.mult, ALU.add)
                    if k == 3:
                        link(ins)
            for i in range(2):
                y = YT[:, 2 * i:2 * i + 2, :]
                dve.tensor_tensor(y, B[i][:].rearrange("p (k s) -> p k s", k=2), y, ALU.mult).then_inc(sem("conv_y"), 1)
            ada(5)
            ada(3)
            dve.wait_ge(sem("conv_y"), 2)
            dve.wait_ge(sem("fft_grp"), 1)
            for i in range(2):
                dve.tensor_copy(YT[:, 4 + 2 * i:6 + 2 * i, :], B[2 + i][:].rearrange("p (k s) -> p k s", k=2)).then_inc(
                    sem("fft_y"), 1)
            ada(2)
            dve.wait_ge(sem("mix_rms"), 1)
            dve.wait_ge(sem("fft_y"), 2)
            link(dve.reciprocal(RMS, RMS))
            for k in range(8):
                gk = gain("g_conv_out")(k)
                dve.scalar_tensor_tensor(YT[:, k, :], YT[:, k, :], gk, RMS[:, k // 4, :], ALU.mult,
                                         ALU.mult).then_inc(sem("mix_yn"), 1)
            ada(2)
            add_residual("wout_x", 0, "w_out")
            norm("xa", X, XN, 8)
            ada(2)
            evac_T("xa", 0, XT, gain("norm_xattn"))
            ada(1)
            for h in range(4):
                dve.wait_ge(sem("xa_s"), h + 1)
                link(dve.reduce_max(att[:, 3, 2 * h:2 * h + 2], B[h][:].rearrange("p (t m) -> p t m", t=TB), AX.X))
                dve.tensor_scalar(att[:, 0, 2 * h:2 * h + 2], att[:, 3, 2 * h:2 * h + 2], -1.0 / 16, None,
                                  ALU.mult).then_inc(sem("xa_nm"), 1)
            for h in range(4):
                dve.wait_ge(sem("xa_e"), 2 * h + 2)
                link(dve.reciprocal(att[:, 4, 2 * h:2 * h + 2], att[:, 1, 2 * h:2 * h + 2]))
                for t in range(TB):
                    dve.tensor_scalar(PR[:, h, t, :], PR[:, h, t, :], att[:, 4, 2 * h + t:2 * h + t + 1], None,
                                      ALU.mult).then_inc(sem("xa_p"), 1)
            ada(3)
            add_residual("wo_x", 0, "w_o")
            norm("ffn", X, XN, 12)
            ada(2)
            evac_T("ffn", 0, XT, gain("norm_ffn"))
            dve.memset(logit[:, :, NE:NE + 4], 3e38).then_inc(sem("rt_pad"), 1)
            dve.memset(gat[:, NE, :], 0.0).then_inc(sem("rt_pad"), 1)
            dve.wait_ge(sem("rt_pad"), 2)
            dve.wait_ge(sem("logits"), 1)
            for t in range(TB):
                link(dve.tensor_tensor(logit[:, t, 0:NE], B[4][:, t * NE:(t + 1) * NE], brow[:], ALU.add))
                link(dve.max(rt[:, t, 40:48], logit[:, t, 0:NE + 4]))
                dve.tensor_scalar(att[:, 2, t:t + 1], rt[:, t, 44:45], -1.0, None, ALU.mult).then_inc(sem("rt_nm"), 1)
                link(dve.match_replace(rt[:, 2 + t, 0:NE + 4], rt[:, t, 40:48], logit[:, t, 0:NE + 4], TAKEN))
                dve.tensor_scalar(rt[:, 4 + t, 0:NE], rt[:, 2 + t, 0:NE], -2e38, None, ALU.is_lt).then_inc(
                    sem("rt_mask"), 1)
            dve.wait_ge(sem("rt_mask"), 2)
            for t in range(TB):
                dve.tensor_copy(mrep[:, t, :].rearrange("p (r e) -> p r e", r=NB_MAX - 1),
                                rt[:, 4 + t, None, 0:NE].to_broadcast((P, NB_MAX - 1, NE))).then_inc(sem("rt_mask"), 1)
            dve.wait_ge(sem("rt_e"), 2)
            for t in range(TB):
                link(dve.tensor_tensor(rt[:, 2 + t, 0:NE], rt[:, t, 0:NE], rt[:, 4 + t, 0:NE], ALU.mult))
                link(dve.reduce_sum(rt[:, t, 50:51], rt[:, 2 + t, 0:NE], AX.X))
                link(dve.reciprocal(rt[:, t, 51:52], rt[:, t, 50:51]))
                link(dve.tensor_scalar(gat[:, 0:NE, t], rt[:, 2 + t, 0:NE], rt[:, t, 51:52], None, ALU.mult))
                link(dve.tensor_scalar(rt[:, 2 + t, 0:NE], rt[:, 4 + t, 0:NE], -FAR, FAR, ALU.mult, ALU.add))
            ada(4)
            dve.wait_ge(sem("rt_pos"), 1)
            link(dve.memset(pos[:], FAR))
            for t in range(TB):
                link(dve.tensor_tensor(pos[:, 0, 0:NE, t], B[5][:, t * NE:(t + 1) * NE], rt[:, 2 + t, 0:NE], ALU.add))
            for b in range(1, NB_MAX):
                link(dve.tensor_scalar(pos[:, b], pos[:, 0], -float(CAP * b), None, ALU.add))
            dve.tensor_tensor(flag, B[5][0:NCAND, 64:65], tb_("thr")[0:NCAND], ALU.is_gt).then_inc(sem("flag"), 1)

            posf = pos[:].rearrange("p b e t -> p (b e) t")

            def select(q):
                for t in range(TB):
                    ins = dve.tensor_scalar(sel_tok[:, t, :], iota[:, 0:CAP], posf[:, bass.ds(q, 1), t], None,
                                            ALU.is_equal)
                    ins.then_inc(sem("e_sel"), 1)

            def expert_row(dst, e):
                return dve.tensor_scalar(dst, ones[:, 0:CAP], ident[:, bass.ds(e, 1)], None, ALU.mult)

            def weigh(q, e):
                for t in range(TB):
                    ins = dve.tensor_scalar(wsel[:, t, :], iota, posf[:, bass.ds(q, 1), t], gat[:, bass.ds(e, 1), t],
                                            ALU.is_equal, ALU.mult)
                    ins.then_inc(sem("e_wsel"), 1)

            def gains_xe():
                g = VEC["norm_ffn"]
                dve.tensor_tensor(xe, B[3][:].rearrange("p (k n) -> p k n", k=KC), bc(col[:, g:g + KC], CAP),
                                  ALU.mult).then_inc(sem("e_xe"), 1)

            def clamp():
                dve.tensor_scalar(gcl, B[0][:], 7.0, None, ALU.min).then_inc(sem("e_clamp"), 1)
                dve.tensor_scalar(ucl, B[1][:], 7.0, -7.0, ALU.min, ALU.max).then_inc(sem("e_clamp"), 1)

            def swiglu(i):
                dve.wait_ge(sem("e_sig"), i + 1)
                dve.wait_ge(sem("e_clamp"), 2 * i + 2)
                dve.tensor_tensor(gl, gcl, sig, ALU.mult).then_inc(sem("e_glu"), 1)
                dve.wait_ge(sem("e_glu"), i + 1)
                dve.scalar_tensor_tensor(hh_, ucl, 1.0, gl, ALU.add, ALU.mult).then_inc(sem("e_h"), 1)

            select(0)
            expert_row(selG, 0).then_inc(sem("e_selG"), 1)
            for b in range(4):
                if b != 1:
                    dve.memset(B[4 + b][:], 0.0).then_inc(sem("acc_zero"), 1)
            dve.wait_ge(sem("rank"), 1)
            dve.tensor_scalar(chosen, iota[0:NCAND, 0:NX_MAX], B[5][0:NCAND, 65:66], flag, ALU.is_equal,
                              ALU.mult).then_inc(sem("chosen"), 1)
            dve.wait_ge(sem("table_mm"), 1)
            dve.tensor_copy(table_i[0:1, 0:33], B[5][0:1, 96:129]).then_inc(sem("table_ready"), 1)
            dve.wait_ge(sem("table_ready"), 1)
            dve.memset(B[5][:], 0.0).then_inc(sem("acc_zero"), 1)
            dve.wait_ge(sem("e_gather"), 1)
            gains_xe()

            with dve.Fori(0, NE) as i:
                dve.wait_ge(used, i * PER_E + (NPRE + 1))
                select(i + 1)
                weigh(i, i)
                expert_row(selG, i + 1).then_inc(sem("e_selG"), 1)
                expert_row(selD, i).then_inc(sem("e_selD"), 1)
                dve.wait_ge(used, i * PER_E + (NPRE + 4))
                clamp()
                dve.wait_ge(sem("e_gather"), i + 2)
                gains_xe()
                swiglu(i)
            n = nc.values_load(table_i[0:1, 32:33], engines=[ENG.DVE], min_val=0, max_val=NX_MAX)
            dve.wait_ge(sem("acc_main"), 1)
            with dve.If(n > 0):
                with dve.Fori(0, n) as i:
                    e = nc.values_load(table_i[0:1, bass.ds(i, 1)], engines=[ENG.DVE], min_val=0, max_val=NE - 1)
                    q = nc.values_load(table_i[0:1, bass.ds(i + 16, 1)], engines=[ENG.DVE], min_val=0,
                                       max_val=NB_MAX * (NE + 1) - 1)
                    select(q)
                    weigh(q, e)
                    expert_row(selG, e).then_inc(sem("e_selG"), 1)
                    expert_row(selD, e).then_inc(sem("e_selD"), 1)
                    dve.wait_ge(sem("e_gather"), i + (NE + 2))
                    gains_xe()
                    dve.wait_ge(sem("x_gu"), i + 1)
                    clamp()
                    swiglu(i + NE)
                    dve.wait_ge(sem("extra_used"), i + 2)
            for t in range(TB):
                for h in range(2):
                    xs = X[:, t, h * HW:(h + 1) * HW]
                    dve.tensor_tensor(xs, B[4 + 2 * t + h][:], xs, ALU.add).then_inc(sem("moe_x"), 1)
            dve.wait_ge(*upto("fin", "root", 1))
            link(dve.reciprocal(stat[:, 80:82], stat[:, 18:20]))
            dve.wait_ge(sem("nfin_landed"), 16)
            for t in range(TB):
                for h in range(2):
                    xs = X[:, t, h * HW:(h + 1) * HW]
                    dve.scalar_tensor_tensor(xs, xs, stat[:, 80 + t:81 + t], nfin[:, h * HW:(h + 1) * HW], ALU.mult,
                                             ALU.mult).then_inc(sem("fin_x"), 1)

            dve.wait_ge(sem("pos_landed"), 32)
            link(dve.tensor_copy(stat[:, 100:102], posi[:]))
            ang, kf, r = ropeS[:, :, 32:64], ropeS[:, :, 0:32], ropeC[:, :, 0:32]
            for t in range(TB):
                link(dve.tensor_scalar(ang[:, t], tb_("inv"), stat[:, 100 + t:101 + t], None, ALU.mult))
            magic = 12582912.0
            c1 = 6.28125
            c2 = float(np.float32(np.floor((2 * np.pi - c1) * 2 ** 20) / 2 ** 20))
            c3 = 2 * np.pi - c1 - c2
            link(dve.tensor_scalar(kf, ang, 1.0 / (2 * np.pi), magic, ALU.mult, ALU.add))
            link(dve.tensor_scalar(kf, kf, -magic, None, ALU.add))
            for c in (c1, c2, c3):
                link(dve.scalar_tensor_tensor(ang, kf, -c, ang, ALU.mult, ALU.add))
            link(dve.tensor_scalar(ang, ang, 3.1415925, -3.1415925, ALU.min, ALU.max))
            dve.scalar_tensor_tensor(r, ang, -1.0, ang, ALU.mult, ALU.max).then_inc(sem("rope_ang"), 1)
            dve.wait_ge(sem("rope_sc"), 2)
            link(dve.tensor_copy(ropeC[:, :, 32:64], ropeC[:, :, 0:32]))
            link(dve.tensor_scalar(ropeS[:, :, 0:32], ropeS[:, :, 32:64], -1.0, None, ALU.mult))

            def rope(out, x, tmp, t, st):
                nd = len(out.shape) - 2

                def cs_(tile, a, b):
                    v = tile[:, t, a:b]
                    for _ in range(nd):
                        v = v[:, None]
                    return v.to_broadcast(tuple(out.shape[:-1]) + (b - a,))

                def half(v, a, b):
                    return v[:, :, :, a:b] if nd == 2 else v[:, :, a:b]

                dve.tensor_tensor(out, x, cs_(ropeC, 0, HD), ALU.mult)
                dve.tensor_tensor(half(tmp, 0, 32), half(x, 32, 64), cs_(ropeS, 0, 32), ALU.mult)
                link(dve.tensor_tensor(half(tmp, 32, 64), half(x, 0, 32), cs_(ropeS, 32, 64), ALU.mult))
                dve.tensor_tensor(out, out, tmp, ALU.add).then_inc(sem(st), 1)

            def modcol(a):
                return (lambda k: mod[:, a, 8 + k:9 + k]), (lambda k: mod[:, a, k:k + 1])

            def attend(st, heads, mask, sink):
                for g in range(heads // 4):
                    if g:
                        dve.wait_ge(*upto(st, "pt", 4 * g))
                    for h in range(4):
                        dve.wait_ge(*upto(st, "sc", 4 * g + h + 1))
                        dve.scalar_tensor_tensor(SC[:, h, :], B[h][:, 0:3 * P], HD ** -0.5, mask, ALU.mult,
                                                 ALU.add).then_inc(sem("s"), 1)
                    dve.wait_ge(*upto(st, "s", 4 * g + 4))
                    dve.reduce_max(att[:, 0, 0:4], SC[:, :, 0:P], AX.X)
                    link(dve.reduce_max(att[:, 0, 4:8], SC[:, :, P:3 * P], AX.X))
                    if sink:
                        sk = sinkb[:, None, 4 * g:4 * g + 4].to_broadcast((P, TB, 4))
                        mx = att[:, 0, 0:8].rearrange("p (t h) -> p t h", t=TB)
                        link(dve.tensor_tensor(mx, mx, sk, ALU.max))
                    ins = dve.tensor_scalar(att[:, 1, 0:8], att[:, 0, 0:8], -1.0, None, ALU.mult)
                    if sink:
                        link(ins)
                        ins = dve.tensor_tensor(att[:, 3, 0:8].rearrange("p (t h) -> p t h", t=TB), sk,
                                                att[:, 1, 0:8].rearrange("p (t h) -> p t h", t=TB), ALU.add)
                    ins.then_inc(sem("nm"), 1)
                    dve.wait_ge(*upto(st, "e", (9 if sink else 8) * (g + 1)))
                    if sink:
                        link(dve.tensor_tensor(att[:, 2, 0:8], att[:, 2, 0:8], att[:, 4, 0:8], ALU.add))
                    link(dve.reciprocal(att[:, 0, 8:16], att[:, 2, 0:8]))
                    for t, (a, b) in enumerate(((0, P), (P, 3 * P))):
                        dve.tensor_tensor(SC[:, :, a:b], SC[:, :, a:b], bc(att[:, 0, 8 + 4 * t:12 + 4 * t], b - a),
                                          ALU.mult).then_inc(sem("p"), 1)

            def gate_diag(l):
                dve.tensor_tensor(XN[:, 0, :].rearrange("p (k n) -> p k n", k=KC),
                                  ident[:, None, :].to_broadcast((P, KC, P)), bc(mod[:, l, 16:24], P),
                                  ALU.mult).then_inc(sem("gate_diag"), 1)

            def layer_norm(l, w, last):
                dve.wait_ge(*done(w, last))
                dve.wait_ge(*upto(f"ln{l}", "gate", 2))
                for t in range(TB):
                    for h in range(2):
                        ins = dve.tensor_tensor(XN[:, 0, h * HW:(h + 1) * HW], B[2 * t + h][:],
                                                XN[:, 1, h * HW:(h + 1) * HW], ALU.mult)
                    link(ins)
                    link(dve.scalar_tensor_tensor(X[:, t, :], X[:, t, :], 4.0 ** 0.25, XN[:, 0, :], ALU.mult, ALU.add))
                for t in range(TB):
                    for h in range(2):
                        ins = dve.bn_stats(rt[:, t, 6 * h:6 * h + 6], X[:, t, h * HW:(h + 1) * HW])
                link(ins)
                dve.bn_aggr(att[:, 5, 0:2], rt[:, 0, 0:12])
                dve.bn_aggr(att[:, 5, 2:4], rt[:, 1, 0:12]).then_inc(sem("ln_var"), 1)
                dve.wait_ge(*upto(f"ln{l}", "ln_root", 1))
                link(dve.reciprocal(att[:, 5, 6:8], att[:, 5, 4:6]))
                dve.wait_ge(*upto(f"ln{l}", "ln_landed", 32))
                for t in range(TB):
                    link(dve.tensor_scalar(X[:, t, :], X[:, t, :], att[:, 5, 2 * t:2 * t + 1], att[:, 5, 6 + t:7 + t],
                                           ALU.subtract, ALU.mult))
                    link(dve.tensor_tensor(X[:, t, :], X[:, t, :], lng, ALU.mult))
                    dve.tensor_tensor(X[:, t, :], X[:, t, :], lnb, ALU.add).then_inc(sem("ln_x"), 1)

            def mlp(l):
                n = f"mlp{l}"
                gate_diag(2 * l + 1)
                dve.wait_ge(*upto(f"m{2 * l + 1}", "xt_a", 4))
                dve.wait_ge(*upto(f"m{2 * l + 1}", "xt_v", 4))
                for b in range(4):
                    dve.memset(B[b][:], 0.0).then_inc(sem("mlp_zero"), 1)
                with dve.Fori(0, 2) as i:
                    for p in range(4):
                        for b in range(2):
                            c = 2 * p + b + 1
                            if b == 0:
                                dve.wait_ge(*upto(n, "mlp_h", i * 4 + (p + 1)))
                            else:
                                dve.wait_ge(used, i * R2 + done(n, 2 * p)[1])
                            hb = hid[:, 2 * b:2 * b + 2, :]
                            dve.tensor_scalar(hb, B[4 + b][:].rearrange("p (k s) -> p k s", k=2), 0.0, None,
                                              ALU.max).then_inc(sem("mlp_relu"), 1)
                            dve.wait_ge(*upto(n, "mlp_relu", i * 8 + c))
                            dve.tensor_tensor(hb, hb, hb, ALU.mult).then_inc(sem("mlp_sq"), 1)

            evac_T("m0", 0, XT, *modcol(0))
            dve.wait_ge(*done("ab_in", 2))
            for c in range(3):
                dve.tensor_copy(Z[:, 1, 408 * c:408 * c + 408], B[3 + c][:, 0:408]).then_inc(sem("z1"), 1)
            dve.wait_ge(sem("cq_root"), 1)
            link(dve.reciprocal(stat[:, 84:86], stat[:, 22:24]))
            for t in range(TB):
                dve.tensor_scalar(XN[:, t, S:2 * S], Z[:, t, 768:1024], stat[:, 84 + t:85 + t], None,
                                  ALU.mult).then_inc(sem("cq_n"), 1)
            dve.wait_ge(sem("cq_T"), 1)
            for k in range(2):
                dve.tensor_scalar(XTf[:, k * S:(k + 1) * S], B[6][:, k * S:(k + 1) * S], gain("ab_q_norm_2")(k), None,
                                  ALU.mult).then_inc(sem("cqT"), 1)
            tmp = XNf[:, 512:1152]
            R1a = R1b.rearrange("p (t n) -> p t n", t=TB)
            for t in range(TB):
                out = R1a[:, t, 0:512].rearrange("p (j g d) -> p j g d", j=4, g=2)
                rope(out, Z[:, t, 0:512].rearrange("p (g j d) -> p j g d", j=4, g=2),
                     tmp[:, 0:512].rearrange("p (j g d) -> p j g d", j=4, g=2), t, "a_rope")
                dve.wait_ge(sem("a_rope"), t + 1)
            for t in range(TB):
                rope(R1a[:, t, 512:640].rearrange("p (g d) -> p g d", g=2),
                     Z[:, t, 512:640].rearrange("p (g d) -> p g d", g=2),
                     tmp[:, 0:128].rearrange("p (g d) -> p g d", g=2), t, "ak_rope")
                dve.wait_ge(sem("ak_rope"), t + 1)
                two = Z[:, t, 1024:1280 - 64].rearrange("p (m d) -> p m d", d=HD)[:, 0:3:2, :]
                rope(R2b[:, t, :].rearrange("p (m c d) -> p m c d", m=2, c=2)[:, :, 0, :], two,
                     tmp[:, 0:128].rearrange("p (g d) -> p g d", g=2), t, "bk_rope")
                dve.wait_ge(sem("bk_rope"), t + 1)
                r2 = R2b[:, t, :].rearrange("p (m c d) -> p m c d", m=2, c=2)
                dve.tensor_copy(r2[:, :, 1, :], r2[:, :, 0, :]).then_inc(sem("k_rope"), 1)
            dve.wait_ge(sem("iq_mm"), 1)
            for t in range(TB):
                rope(R4b[:, t * HW:(t + 1) * HW].rearrange("p (h d) -> p h d", d=HD),
                     B[2 + t][:].rearrange("p (h d) -> p h d", d=HD), tmp[:, 0:512].rearrange("p (h d) -> p h d", d=HD),
                     t, "i_rope")
                dve.wait_ge(sem("i_rope"), t + 1)
            dve.wait_ge(*done("uq", 0))
            dve.wait_ge(sem("k_T"), 1)
            for t in range(TB):
                rope(R1b[:, t * HW:(t + 1) * HW].rearrange("p (h d) -> p h d", d=HD),
                     B[t][:].rearrange("p (h d) -> p h d", d=HD), tmp[:, 0:512].rearrange("p (h d) -> p h d", d=HD),
                     t, "b_rope")
                dve.wait_ge(sem("b_rope"), t + 1)
            iw = rt[:, 0, 0:16].rearrange("p (t h) -> p t h", t=TB)
            link(dve.tensor_scalar(iw, Z[:, :, 1216:1224], 8 ** -0.5 * HD ** -0.5, None, ALU.mult))
            for h in range(8):
                dve.wait_ge(sem("ix_relu"), h + 1)
                if h:
                    dve.wait_ge(sem("ix_acc"), 2 * h)
                for t, (a, b) in enumerate(((0, P), (P, 3 * P))):
                    rl, w = relu_i[:, h % 2, a:b], iw[:, t, h:h + 1]
                    if h == 0:
                        ins = dve.tensor_scalar(idx[:, a:b], rl, w, None, ALU.mult)
                    else:
                        ins = dve.scalar_tensor_tensor(idx[:, a:b], rl, w, idx[:, a:b], ALU.mult, ALU.add)
                    ins.then_inc(sem("ix_acc"), 1)
            dve.wait_ge(sem("ix_acc"), 16)
            link(dve.tensor_tensor(idx, idx, tb_("full"), ALU.add))
            topk = 64
            for rnd in range(topk // 8):
                src = idx if rnd == 0 else left
                dve.max(rt[:, 1, 0:8], src[:, 0:P])
                link(dve.max(rt[:, 1, 8:16], src[:, P:3 * P]))
                dve.match_replace(left[:, 0:P], rt[:, 1, 0:8], src[:, 0:P], TAKEN)
                link(dve.match_replace(left[:, P:3 * P], rt[:, 1, 8:16], src[:, P:3 * P], TAKEN))
            link(dve.tensor_scalar(left, left, -2e38, NEG, ALU.is_gt, ALU.mult))
            link(dve.tensor_tensor(bmask, left, tb_("full"), ALU.add))
            dve.wait_ge(sem("sink_landed"), 16)
            attend("aa", 8, tb_("window"), True)
            dve.wait_ge(*upto("aa", "pt", 8))
            attend("bb", 8, bmask, False)
            dve.wait_ge(*upto("bb", "pt", 8))
            gate_diag(0)
            layer_norm(0, "ab_out", 1)
            evac_T("m1", 0, XT, *modcol(1))
            mlp(0)
            layer_norm(1, "mlp0", 15)
            evac_T("m2", 0, XT, *modcol(2))
            tmps = XNf.rearrange("p (i n) -> p i n", i=4)
            for m in range(2):
                dve.wait_ge(*done("c_in", 2 * m + 1))
                dst = arn(2048 * m, 2048)
                for t in range(TB):
                    for h in range(2):
                        a = t * D + h * HW
                        rope(dst[:, a:a + HW].rearrange("p (h d) -> p h d", d=HD),
                             B[4 * m + 2 * t + h][:].rearrange("p (h d) -> p h d", d=HD),
                             tmps[:, 2 * t + h, :].rearrange("p (h d) -> p h d", d=HD), t, "c_rope")
            dve.wait_ge(sem("c_rope"), 8)
            attend("cc", 16, tb_("full"), False)
            dve.wait_ge(*upto("cc", "pt", 16))
            gate_diag(2)
            layer_norm(2, "c_out", 1)
            evac_T("m3", 0, XT, *modcol(3))
            mlp(1)
            layer_norm(3, "mlp1", 15)


_INS = ["x", "mem", "norm_mix", "w_in", "conv_w", "g_conv_out", "g_fft_out", "w_out", "norm_xattn", "norm_mem", "w_q",
        "w_k", "w_v", "w_o", "norm_ffn", "w_router", "b_router", "w_gate_up", "b_gate_up", "w_down", "b_down",
        "norm_final", "c_2", "positions_2", "ab_w_in_2", "ab_q_norm_2", "ab_w_uq_2", "ab_w_uiq_2", "ab_sinks_2",
        "ab_w_out_2", "c_w_in_2", "c_w_out_2", "ada_w_2", "ada_b_2", "ln_g_2", "ln_b_2", "mlp_w1_2", "mlp_w2_2"]


def kernel(**inputs):
    import concourse.bacc as bacc
    from concourse.bass_utils import run_bass_kernel_spmd

    nc = bacc.Bacc("TRN2", target_bir_lowering=False, num_devices=1)
    arrays = {f"in_{name}": np.ascontiguousarray(inputs[name]) for name in _INS}
    arrays["in_tables"], arrays["in_dft"] = tables()
    aps = {n: nc.dram_tensor(n, a.shape, mybir.dt.from_np(a.dtype), kind="ExternalInput").ap()
           for n, a in arrays.items()}
    out = nc.dram_tensor("out", (1, S, D), F32, kind="ExternalOutput").ap()
    build_program(nc, {n: aps[f"in_{n}"] for n in _INS}, aps["in_tables"], aps["in_dft"], out)
    r = run_bass_kernel_spmd(nc, [arrays], core_ids=[0])
    return r.results[0]["out"]
```

```python
from contextlib import ExitStack

import numpy as np
import concourse.bass as bass
from concourse import mybir

F32 = mybir.dt.float32
I32 = mybir.dt.int32
F32R = mybir.dt.float32r
ALU = mybir.AluOpType
ACT = mybir.ActivationFunctionType
AX = mybir.AxisListType
ENG = mybir.EngineType

P = 128
S = 256
TB = S // P
D = 1024
KC = D // P
NE = 32
TOPK = 4
CAP = 64
NB_MAX = S // CAP
NCAND = (NB_MAX - 1) * NE
NX_MAX = S * TOPK // CAP
SLOT = 4096
HW = 512
HD = 64
NEG = -1e30
TAKEN = -3e38
FAR = 10000.0

T_COLS = {}


def tables():
    p = np.arange(P)[:, None]
    c = np.arange(P)[None, :]
    parts = {}
    parts["ident"] = (p == c) * 1.0
    parts["tri"] = (p < c) * 1.0
    parts["ones"] = np.ones((P, P))
    parts["quads"] = (p % 32 == 0) * 1.0
    parts["iota"] = np.repeat(c % CAP, P, 0)
    causal = np.where(c <= p, 0.0, NEG)
    parts["full"] = np.concatenate([causal, np.zeros((P, P)), causal], 1)
    parts["window"] = np.concatenate([causal, np.where(c > p, 0.0, NEG), causal], 1)
    ang = 2 * np.pi * np.outer(np.arange(64), np.arange(64)) / 64
    same = np.kron(np.eye(2), np.ones((64, 64)))
    parts["cg"] = np.tile(np.cos(ang), (2, 2)) * same / 8
    parts["sg"] = -np.tile(np.sin(ang), (2, 2)) * same / 8
    inv = np.float32(10000.0) ** (-np.arange(0, HD, 2, dtype=np.float32) / np.float32(HD))
    parts["inv"] = np.repeat(inv[None], P, 0)
    parts["eps5"] = np.full((P, 1), 1e-5)
    parts["eps6"] = np.full((P, 1), 1e-6)
    parts["zero"] = np.zeros((P, 1))
    parts["halfpi"] = np.full((P, 1), np.pi / 2)
    q = np.minimum(np.arange(P), NCAND - 1)[:, None]
    parts["thr"] = CAP * (1 + q // NE)
    parts["cand_e"] = q % NE
    parts["cand_q"] = (1 + q // NE) * (NE + 1) + q % NE
    parts["shift"] = np.repeat(CAP * np.arange(NB_MAX)[None], P, 0)
    at = 0
    for n, a in parts.items():
        T_COLS[n] = (at, at + a.shape[1])
        at += a.shape[1]
    t = np.concatenate([np.asarray(a, np.float32) for a in parts.values()], 1)
    ang = 2 * np.pi * (np.outer(np.arange(S), np.arange(S)) % S) / S
    dft = np.concatenate([np.cos(ang), np.sin(ang)], 1) / 16
    return np.ascontiguousarray(t), np.ascontiguousarray(dft.astype(np.float32))


tables()
TAB_W = max(b for _, b in T_COLS.values())

VEC = {"norm_mix": 0, "norm_xattn": 8, "norm_mem": 16, "norm_ffn": 24, "g_conv_out": 32, "g_fft_out": 36,
       "conv_w": 40, "ab_q_norm_2": 52, "c_2": 54, "norm_final": 62, "ln_g_2": 70, "ln_b_2": 94}
NVEC = 118
NADA = 4
ADA_UNITS = NADA * 6

ADA_AT = [("mix_in", 5), ("fft", 3), ("yfft", 2), ("mixss", 2), ("mix_out", 2), ("q", 1), ("scores", 3),
          ("w_o", 2), ("router", 4)]


def pre_stream():
    out = [("w_k", i) for i in range(2)] + [("w_v", i) for i in range(2)] + [("w_in", i) for i in range(4)]
    u = 0
    tail = {"mixss": [("w_out", 0), ("w_out", 1)], "mix_out": [("w_q", 0), ("w_q", 1)],
            "scores": [("w_o", 0), ("w_o", 1)]}
    for name, n in ADA_AT:
        out += [("ada", u + i) for i in range(n)]
        u += n
        out += tail.get(name, [])
    assert u == ADA_UNITS
    return out


PRE = pre_stream()
NPRE = len(PRE)
R1 = 6
PER_E = 6
MOE_END = NPRE + NE * PER_E
POST = ([("ab_in", i) for i in range(3)] + [("uq", 0)] + [("ab_out", i) for i in range(2)] + [("mlp0", i) for i in range(16)]
        + [("c_in", i) for i in range(6)] + [("c_out", i) for i in range(2)] + [("mlp1", i) for i in range(16)])
SLOTS = 8
R2 = 4
LAST_E = [(NPRE + j) % R1 for j in range(R1)]
POST_SLOTS = [6, 7] + LAST_E[0:2]
PAIRS = (LAST_E[2:4], LAST_E[4:6])
UQ = POST.index(("uq", 0))


def slot_of(g):
    return g % R1 if g < MOE_END else POST_SLOTS[(g - MOE_END) % R2]


FILL, OWNER = {}, {}


def lay_stream():
    count, last = [0] * SLOTS, {}
    for g in range(MOE_END + len(POST)):
        s = slot_of(g)
        count[s] += 2 if g == MOE_END + UQ else 1
        FILL[g] = 16 * count[s]
        OWNER[g] = last.get(s)
        last[s] = g


lay_stream()


def split_no(g):
    q = g - MOE_END
    assert q >= 0 and q != UQ
    return q + 1 - (q > UQ)


NORMS = ("mem", "mix", "xa", "ffn", "fin")
TURNS = ("mem", "mix", "xa", "ffn", "m0", "m1", "m2", "m3")
HATS = ("fin", "ln0", "ln1", "ln2", "ln3")
LNS = ("ln0", "ln1", "ln2", "ln3")
ATTNS = {"aa": (2, 9), "bb": (2, 8), "cc": (4, 8)}
SHARES = {}
for _kind, _per in (("sq", 2), ("root", 1), ("xn", 2)):
    SHARES[_kind] = [(st, _per) for st in NORMS]
for _kind in ("T", "xt_a", "xt_v"):
    SHARES[_kind] = [(st, 4) for st in TURNS]
SHARES["xt_a"] = [(st, 8 if st[0] == "m" and st[1].isdigit() else 4) for st in TURNS]
SHARES["xt_v"] = SHARES["xt_a"]
for _kind, _per in (("xhat", 2), ("ln_x", 2)):
    SHARES[_kind] = [(st, _per) for st in HATS]
for _kind, _per in (("ln_y0", 1), ("ln_var", 2), ("ln_root", 2), ("ln_landed", 32), ("gate_diag", 1), ("gate_mm", 1),
                    ("gate", 2)):
    SHARES[_kind] = [(st, _per) for st in LNS]
for _kind, _per in (("sc", 4), ("s", 4), ("nm", 1), ("p", 2), ("pt", 4), ("pte", 4), ("o", 1), ("ot", 1), ("otl", 1)):
    SHARES[_kind] = [(st, _per * g) for st, (g, _) in ATTNS.items()]
SHARES["e"] = [(st, g * n) for st, (g, n) in ATTNS.items()]
for _kind, _per in (("mlp_zero", 4), ("mlp_h", 8), ("mlp_relu", 16), ("mlp_sq", 16), ("mlp_tt", 16), ("mlp_lo", 16)):
    SHARES[_kind] = [(st, _per) for st in ("mlp0", "mlp1")]


def base_of(st, kind):
    at = 0
    for name, n in SHARES[kind]:
        if name == st:
            return at
        at += n
    raise KeyError(st)


def build_program(nc, A, tab_d, dft_d, out_d):
    ctx = ExitStack()
    with ctx:
        sems = {}

        def sem(name):
            if name not in sems:
                sems[name] = ctx.enter_context(nc.semaphore(name))
            return sems[name]

        def done(name, i):
            g = PRE.index((name, i)) if (name, i) in PRE else MOE_END + POST.index((name, i))
            return sem("granules_used"), g + 1

        def upto(st, kind, v):
            return sem(kind), v + base_of(st, kind)

        def sb(name, shape, dt=F32):
            return ctx.enter_context(nc.sbuf_tensor("sb_" + name, shape, dt))

        wide = {"ring": [P, SLOTS * SLOT], "XT": [P, KC, S], "arena": [P, 5 * 2048]}
        at = (nc.sbuf_base + 31) // 32 * 32
        sb("fence", [P, 8 + sum(int(np.prod(w[1:])) for w in wide.values())])
        pairs = [[nc.alloc_sbuf_tensor_at(f"w_{part}{i}", [P, SLOT], F32R, offset=at + 4 * SLOT * s)
                  for part, s in zip(("hi", "lo"), slots)] for i, slots in enumerate(PAIRS)]
        for name, shape in wide.items():
            wide[name] = [nc.alloc_sbuf_tensor_at(n, shape, dt, offset=at)
                          for n, dt in ((name, F32), (name + "_r", F32R))[:1 if name == "ring" else 2]]
            at += 4 * int(np.prod(shape[1:]))
        ring, = wide["ring"]
        XT, XT_r = wide["XT"]
        arena, arena_r = wide["arena"]

        B = [ctx.enter_context(nc.psum_tensor(f"bank{i}", [P, HW], F32)) for i in range(8)]
        tab = sb("tab", [P, TAB_W])
        X = sb("X", [P, TB, D])
        XN = sb("XN", [P, TB, D])
        vec = sb("vec", [P, 2, P])
        col = sb("col", [P, NVEC])
        ada_bT = sb("ada_bT", [P, NADA * 24])
        mod = sb("mod", [P, NADA, 24])
        cs = sb("cs", [P, KC, 32])
        sil = sb("sil", [P, 2, 8])
        stat = sb("stat", [P, 128])
        pos = sb("pos", [P, NB_MAX, NE + 1, TB])
        gat = sb("gat", [P, NE + 1, TB])
        logit = sb("logit", [P, TB, 40])
        rt = sb("rt", [P, 6, 64])
        brow = sb("brow", [P, NE])
        wr = sb("wr", [P, KC, NE])
        table_i = sb("table_i", [1, 40], I32)
        ropeC = sb("ropeC", [P, TB, HD])
        ropeS = sb("ropeS", [P, TB, HD])
        posi = sb("posi", [P, TB], I32)
        att = sb("att", [P, 6, 16])
        mrep = vec[:, :, 0:NCAND]
        sinkb = stat[:, 48:56]
        flag = stat[0:NCAND, 56:57]
        chosen = stat[0:NCAND, 104:104 + NX_MAX]

        def tb_(n):
            a, b = T_COLS[n]
            return tab[:, a:b]

        ident, tri, ones, quads, iota = (tb_(n) for n in ("ident", "tri", "ones", "quads", "iota"))
        eps5, eps6, zero = tb_("eps5"), tb_("eps6"), tb_("zero")

        def slot(s, w=SLOT):
            return ring[:, s * SLOT:s * SLOT + w]

        def arn(a, w):
            return arena[:, a:a + w]

        def arn_r(a, w):
            return arena_r[:, a:a + w]

        def pair(n):
            return [part[:] for part in pairs[(n - 1) % 2]]

        ext = ring[:, 6 * SLOT:8 * SLOT]
        MEM = arn(0, 2048).rearrange("p (t d) -> p t d", t=TB)
        MEMN = arn(2048, 2048).rearrange("p (t d) -> p t d", t=TB)
        MEMT = arn(4096, 2048).rearrange("p (k s) -> p k s", k=KC)
        KT = ext[:, 0:2048].rearrange("p (k s) -> p k s", k=KC)
        V = ext[:, 2048:4096].rearrange("p (t d) -> p t d", t=TB)
        dft = ext[:, 4096:5120].rearrange("p (t n) -> p t n", t=TB)
        ada_part = ext[:, 5120:6144].rearrange("p (i n) -> p i n", i=2)
        QT = ext[:, 6144:8192].rearrange("p (k s) -> p k s", k=KC)
        CT = arn(0, 1024)
        U = arn(1024, 1024).rearrange("p (t n) -> p t n", t=TB)
        SQ = arn(2048, 2048).rearrange("p (k s) -> p k s", k=8)
        FT = arn(4096, 2048).rearrange("p (k n) -> p k n", k=4)
        GP = arn(6144, 4 * (S + 2)).rearrange("p (k s) -> p k s", k=4)
        RMS = arn(7300, 512).rearrange("p (k s) -> p k s", k=2)
        YT = arn(8192, 2048).rearrange("p (k s) -> p k s", k=8)
        PR = arn(0, 2048).rearrange("p (h t m) -> p h t m", h=4, t=TB)
        PRT = arn(2048, 2048).rearrange("p (h m s) -> p h m s", h=4, m=2)
        OT = arn(4096, 2048).rearrange("p (k s) -> p k s", k=KC)
        bias = arn(0, 3 * D)
        gcl, ucl, sig, gl, hh_ = (arn(3072 + 512 * i, 512) for i in range(5))
        hT = arn(5632, 512).rearrange("p (c n) -> p c n", c=4)
        ysb = arn(6144, 512)
        sel_tok = arn(6656, TB * CAP).rearrange("p (t n) -> p t n", t=TB)
        wsel = arn(6784, TB * P).rearrange("p (t n) -> p t n", t=TB)
        wselT = arn(7040, 2 * TB * P).rearrange("p (h t n) -> p h t n", h=2, t=TB)
        selG = arn(7552, CAP)
        selD = arn(7616, CAP)
        xe = arn(7680, KC * CAP).rearrange("p (k n) -> p k n", k=KC)
        nfin = arn(8192, D)
        Z = arn(0, 2 * 1224).rearrange("p (t n) -> p t n", t=TB)
        R1b = arn(2448, 1280)
        R2b = arn(3728, 512).rearrange("p (t n) -> p t n", t=TB)
        R4b = arn(4240, 1024)
        aqT = arn(5264, 1024).rearrange("p (k s) -> p k s", k=4)
        bqT = arn(6288, 1024).rearrange("p (k s) -> p k s", k=4)
        iqT = arn(7312, 1024).rearrange("p (k s) -> p k s", k=4)
        akT = arn(8336, 256)
        bkT = arn(8592, 256)
        ikT = arn(8848, 256)
        OTa, OTb = ([arn_r(a, 1024).rearrange("p (k s) -> p k s", k=4) for a in at]
                    for at in ((9104, 2448), (4240, 7312)))
        OTc = [arn_r(a, 2048).rearrange("p (k s) -> p k s", k=KC) for a in (0, 2048)]
        lng = arn(5264, D)
        lnb = arn(6288, D)
        hid = [arn_r(a, 1024).rearrange("p (k s) -> p k s", k=4) for a in (0, 1024)]
        relu_h, sq_h = (arn(a, 1024).rearrange("p (k s) -> p k s", k=4) for a in (2048, 3072))
        XTL = {a: arn_r(4096 if a == 0 else 8192, 2048).rearrange("p (k s) -> p k s", k=KC) for a in range(4)}

        XNf = XN[:].rearrange("p t d -> p (t d)")
        XTf = XT[:].rearrange("p k s -> p (k s)")
        SC = XNf[:, 0:1536].rearrange("p (h n) -> p h n", h=4)
        idx = XNf[:, 1536:1920]
        PT = XTf[:, 0:1536].rearrange("p (h n) -> p h n", h=4)
        bmask = XTf[:, 1536:1920]
        relu_i = R1b[:, 0:768].rearrange("p (i n) -> p i n", i=2)
        left = R1b[:, 768:1152]

        used = sem("granules_used")
        landed = [sem(f"slot{s}_landed") for s in range(SLOTS)]

        def kview(a, k):
            return a.rearrange("(k p) n -> p k n", p=P)

        W2 = {n: kview(A[n][0], KC) for n in ("w_k", "w_v", "w_in", "w_out", "w_q", "w_o", "ab_w_in_2",
                                              "ab_w_out_2", "c_w_in_2", "c_w_out_2")}

        def granule_source(name, i, s):
            if name in ("w_k", "w_v", "w_out", "w_q", "w_o"):
                return [(slot(s).rearrange("p (k n) -> p k n", k=4), W2[name][:, 4 * i:4 * i + 4, :])]
            if name == "w_in":
                return [(slot(s).rearrange("p (k n) -> p k n", k=2), W2[name][:, 2 * i:2 * i + 2, :])]
            if name == "ada":
                a, nb = i // 6, i % 6
                src = A["ada_w_2"][a // 2, a % 2].rearrange("(k p) n -> p k n", p=P)
                return [(slot(s).rearrange("p (k n) -> p k n", k=8), src[:, :, HW * nb:HW * nb + HW])]
            if name == "ab_in":
                k = min(3, KC - 3 * i)
                return [(slot(s, k * 1224).rearrange("p (k n) -> p k n", k=k), W2["ab_w_in_2"][:, 3 * i:3 * i + k, :])]
            if name == "uq":
                return [(slot(s)[:, j * 1024:(j + 1) * 1024].rearrange("p (k n) -> p k n", k=2),
                         kview(A[w][0], 2)) for j, w in enumerate(("ab_w_uq_2", "ab_w_uiq_2"))]
            if name in ("ab_out", "c_out"):
                w = W2["ab_w_out_2" if name == "ab_out" else "c_w_out_2"]
                return [(slot(s).rearrange("p (k n) -> p k n", k=4), w[:, 4 * i:4 * i + 4, :])]
            assert name == "c_in"
            return [(slot(s).rearrange("p (k n) -> p k n", k=4),
                     W2["c_w_in_2"][:, 4 * (i % 2):4 * (i % 2) + 4, D * (i // 2):D * (i // 2) + D])]

        block = ctx.enter_context(nc.Block())

        def granule_no(name, i):
            return MOE_END + POST.index((name, i))

        def width(name, i):
            return SLOT if name != "ab_in" else min(3, KC - 3 * i) * 1224

        def split_hi(act, name, i, it=None):
            g = granule_no(name, i)
            n = split_no(g)
            step = 0 if it is None else it * R2
            act.wait_ge(landed[slot_of(g)], (0 if it is None else it * 16) + FILL[g])
            if n > 2:
                before = g - 2 - (g - 2 <= MOE_END + UQ <= g)
                act.wait_ge(used, step + (before + 1))
            else:
                act.wait_ge(used, MOE_END)
            w = width(name, i)
            act.activation(pair(n)[0][:, 0:w], slot(slot_of(g), w), ACT.Copy).then_inc(sem("w_hi"), 1)

        def split_lo(eng, name, i, it=None):
            n = split_no(granule_no(name, i))
            step = 0 if it is None else it * R2
            hi, lo = pair(n)
            w = width(name, i)
            eng.wait_ge(sem("w_hi"), step + n)
            if n > 1:
                eng.wait_ge(sem("w_lo"), step + (n - 1))
            eng.tensor_tensor(lo[:, 0:w], slot(slot_of(granule_no(name, i)), w), hi[:, 0:w].bitcast(F32),
                              ALU.subtract).then_inc(sem("w_lo"), 1)

        @block.sync
        def _(sp):
            sp.dma_start(tab[:], tab_d).then_inc(sem("tab_landed"), 16)
            sp.dma_start(MEM, A["mem"][0].rearrange("(t p) d -> p t d", p=P)).then_inc(sem("mem_landed"), 16)
            sp.dma_start(X[:], A["x"][0].rearrange("(t p) d -> p t d", p=P)).then_inc(sem("x_landed"), 16)

            def fill(g, name, i):
                if OWNER[g] is not None:
                    sp.wait_ge(used, OWNER[g] + 1)
                for dst, src in granule_source(name, i, slot_of(g)):
                    sp.dma_start(dst, src).then_inc(landed[slot_of(g)], 16)

            for g, (name, i) in enumerate(PRE):
                fill(g, name, i)
                if g == 3:
                    sp.dma_start(dft, dft_d.rearrange("(t p) n -> p t n", p=P)).then_inc(sem("dft_landed"), 16)

            def expert_slot(j):
                return slot_of(NPRE + j)

            def expert_source(j, e):
                if j < 4:
                    return A["w_gate_up"][0, bass.ds(e, 1), 2 * P * j:2 * P * (j + 1), :].rearrange(
                        "e (k p) n -> p (e k) n", p=P)
                return A["w_down"][0, bass.ds(e, 1), 4 * P * (j - 4):4 * P * (j - 3), :].rearrange(
                    "e (k p) n -> p (e k) n", p=P)

            with sp.Fori(0, NE) as e:
                for j in range(PER_E):
                    s = expert_slot(j)
                    sp.wait_ge(used, e * PER_E + (OWNER[NPRE + j] + 1))
                    sp.dma_start(slot(s).rearrange("p (k n) -> p k n", k=2 if j < 4 else 4),
                                 expert_source(j, e)).then_inc(landed[s], 16)

            sp.wait_ge(sem("table_ready"), 1)
            n = nc.values_load(table_i[0:1, 32:33], engines=[ENG.SP], min_val=0, max_val=NX_MAX)
            with sp.If(n > 0):
                sp.wait_ge(used, MOE_END)
                with sp.Fori(0, n) as i:
                    e = nc.values_load(table_i[0:1, bass.ds(i, 1)], engines=[ENG.SP], min_val=0, max_val=NE - 1)
                    sp.wait_ge(sem("extra_used"), i + 1)
                    for j in range(PER_E):
                        sp.dma_start(slot(expert_slot(j)).rearrange("p (k n) -> p k n", k=2 if j < 4 else 4),
                                     expert_source(j, e)).then_inc(sem("extra_landed"), 16)
                sp.wait_ge(sem("moe_x"), 1)

            g = MOE_END
            for name, count in (("ab_in", 3), ("uq", 1), ("ab_out", 2), ("mlp0", 16), ("c_in", 6), ("c_out", 2),
                                ("mlp1", 16)):
                if name[:3] != "mlp":
                    for i in range(count):
                        o = OWNER[g]
                        if o is None:
                            sp.wait_ge(used, NPRE)
                        elif o < MOE_END:
                            sp.wait_ge(used, o + 1)
                        else:
                            sp.wait_ge(sem("w_hi"), split_no(o))
                            sp.wait_ge(sem("w_lo"), split_no(o))
                        for dst, src in granule_source(name, i, slot_of(g)):
                            sp.dma_start(dst, src).then_inc(landed[slot_of(g)], 16)
                        g += 1
                    continue
                if name == "mlp0":
                    sp.wait_ge(*done("uq", 0))
                l = int(name[3])
                w1 = A["mlp_w1_2"][l].rearrange("(k p) n -> p k n", p=P)
                w2 = A["mlp_w2_2"][l].rearrange("(k p) n -> p k n", p=P)
                with sp.Fori(0, 4) as i:
                    for j in range(R2):
                        s = slot_of(g + j)
                        n = split_no(g + j) - R2
                        sp.wait_ge(sem("w_hi"), i * R2 + n)
                        sp.wait_ge(sem("w_lo"), i * R2 + n)
                        if j % 2 == 0:
                            src = w1[:, :, bass.ds(i * (2 * HW) + (j // 2) * HW, HW)]
                            dst = slot(s).rearrange("p (k n) -> p k n", k=8)
                        else:
                            src = w2[:, bass.ds(i * 8 + (j // 2) * 4, 4), :]
                            dst = slot(s).rearrange("p (k n) -> p k n", k=4)
                        sp.dma_start(dst, src).then_inc(landed[s], 16)
                g += 16
            for t in range(TB):
                sp.wait_ge(*upto("ln3", "ln_x", t + 1))
                sp.dma_start(out_d[0, t * P:(t + 1) * P, :], X[:, t, :]).then_inc(sem("stored"), 16)
            sp.wait_ge(sem("stored"), 16 * TB)

        @block.gpsimd
        def _(pool):
            pool.memset(GP[:, :, 0:1], 0.0).then_inc(sem("conv_pad"), 1)
            pool.memset(GP[:, :, S + 1:S + 2], 0.0).then_inc(sem("conv_pad"), 1)
            pool.wait_ge(sem("wo_x"), 4)
            pool.memset(bias, 0.0).then_inc(sem("moe_zero"), 1)
            pool.memset(ysb, 0.0).then_inc(sem("e_y"), 1)
            pool.memset(arn(7040, 512), 0.0).then_inc(sem("moe_zero"), 1)
            pool.memset(stat[:, 127:128], 0.0).then_inc(sem("extra_used"), 1)

            def cols(name, n):
                return col[:, VEC[name]:VEC[name] + 8 * n].rearrange("p (a k) -> p a k", k=8)

            part = stat[:, 24:48].rearrange("p (a k) -> p a k", k=8)
            pool.wait_ge(sem("ada_done"), ADA_UNITS)
            pool.wait_ge(sem("col_ready"), 2)
            pool.tensor_tensor(part, mod[:, 1:4, 8:16], cols("ln_b_2", 3), ALU.mult).then_inc(sem("mod_g"), 1)
            pool.wait_ge(sem("mod_g"), 1)
            pool.tensor_tensor(mod[:, 1:4, 0:8], mod[:, 1:4, 0:8], part, ALU.add).then_inc(sem("mod_g"), 1)
            pool.tensor_tensor(mod[:, 1:4, 8:16], mod[:, 1:4, 8:16], cols("ln_g_2", 3), ALU.mult).then_inc(sem("mod_g"), 1)
            pool.tensor_tensor(mod[:, 0:1, 8:16], mod[:, 0:1, 8:16], cols("norm_final", 1), ALU.mult).then_inc(
                sem("mod_g"), 1)

            def w_lo(name, i):
                split_lo(pool, name, i)

            def affine(st, t):
                steps = [(nfin, ALU.mult)] if st == "fin" else [(lng, ALU.mult), (lnb, ALU.add)]
                for n, (row, op) in enumerate(steps):
                    ins = pool.tensor_tensor(X[:, t, :], X[:, t, :], row, op)
                    if n + 1 < len(steps):
                        ins.then_inc(sem("pool_step"), 1)
                        pool_steps[0] += 1
                        pool.wait_ge(sem("pool_step"), pool_steps[0])
                ins.then_inc(sem("ln_x"), 1)

            pool_steps = [0]
            w_lo("ab_in", 0)
            pool.wait_ge(sem("nfin_landed"), 16)
            pool.wait_ge(*upto("m0", "T", 4))
            for t in range(TB):
                affine("fin", t)
            w_lo("ab_out", 0)
            w_lo("ab_out", 1)
            for l, after in enumerate(("mlp0", "c_in", "mlp1")):
                w_lo(after, 0)
                pool.wait_ge(*upto(f"m{l + 1}", "T", 4))
                pool.wait_ge(*upto(f"ln{l}", "ln_landed", 32))
                for t in range(TB):
                    affine(f"ln{l}", t)
                if after == "c_in":
                    w_lo("c_out", 0)
                    w_lo("c_out", 1)

        @block.scalar
        def _(act):
            def vec_rows(name, ap):
                n = ap.shape[0]
                act.dma_start(vec[VEC[name]:VEC[name] + n, 0, :], ap).then_inc(sem("vec_landed"), 16)

            def rows(ap):
                return ap.rearrange("(k p) -> k p", p=P)

            for n in ("norm_mem", "norm_mix", "norm_xattn", "norm_ffn", "g_conv_out", "g_fft_out", "ab_q_norm_2"):
                vec_rows(n, rows(A[n][0]))
            vec_rows("conv_w", A["conv_w"][0].rearrange("t (k p) -> (t k) p", p=P))
            vec_rows("c_2", rows(A["c_2"][0]))
            vec_rows("norm_final", rows(A["norm_final"]))
            for n in ("ln_g_2", "ln_b_2"):
                vec_rows(n, A[n].rearrange("a b (k p) -> (a b k) p", p=P)[0:24])
            act.dma_start(vec[0:NADA * 24, 1, :], A["ada_b_2"].rearrange("a b (k p) -> (a b k) p", p=P)).then_inc(
                sem("vec_landed"), 16)
            act.dma_start(wr[:], kview(A["w_router"][0], KC)).then_inc(sem("router_landed"), 16)
            act.dma_start(brow[:], A["b_router"][0:1, :].to_broadcast((P, NE))).then_inc(sem("router_landed"), 16)
            for t in range(TB):
                act.dma_start(posi[:, t:t + 1], A["positions_2"][0, t * P:(t + 1) * P, None]).then_inc(
                    sem("pos_landed"), 16)
            act.dma_start(sinkb, A["ab_sinks_2"][0:1, :].to_broadcast((P, 8))).then_inc(sem("sink_landed"), 16)

            def norm_stats(st, src, junk, at, ready):
                act.wait_ge(*ready)
                for t in range(TB):
                    act.activation(junk[:, t, :], src[:, t, :], ACT.Square, bias=zero,
                                   accum_out=stat[:, at + t:at + t + 1]).then_inc(sem("sq"), 1)
                act.wait_ge(*upto(st, "sq", TB))
                act.activation(stat[:, at + 2:at + 4], stat[:, at:at + 2], ACT.Sqrt, bias=eps5,
                               scale=1.0 / D).then_inc(sem("root"), 1)

            def evac_T(st, base, XTo, g1, g0=None):
                for n, q in enumerate((0, 2)):
                    act.wait_ge(*upto(st, "T", q + 1))
                    for r in range(2):
                        k = 2 * q + r
                        src = B[base + q][:, r * S:(r + 1) * S]
                        if g0 is None:
                            act.activation(XTo[:, k, :], src, ACT.Copy, scale=g1(k)).then_inc(sem("xt_a"), 1)
                        else:
                            act.activation(XTo[:, k, :], src, ACT.Identity, scale=g1(k),
                                           bias=g0(k)).then_inc(sem("xt_a"), 1)

            unit = [0]

            def ada(n):
                for _ in range(n):
                    u = unit[0]
                    unit[0] += 1
                    act.wait_ge(*done("ada", u))
                    if u >= 2:
                        act.wait_ge(sem("ada_comb"), u - 1)
                    act.activation(ada_part[:, u % 2, :], B[6][:], ACT.Copy).then_inc(sem("ada_part"), 1)

            def gain(name):
                return lambda k: col[:, VEC[name] + k:VEC[name] + k + 1]

            act.wait_ge(sem("tab_landed"), 16)
            norm_stats("mem", MEM, MEMN, 0, (sem("mem_landed"), 16))
            norm_stats("mix", X, XN, 4, (sem("x_landed"), 16))
            act.wait_ge(sem("vecT"), 1)
            act.activation(col[:], B[4][:, 0:NVEC], ACT.Copy).then_inc(sem("col_ready"), 1)
            act.activation(ada_bT[:], B[4][:, 128:128 + NADA * 24], ACT.Copy).then_inc(sem("col_ready"), 1)
            act.wait_ge(sem("col_ready"), 2)
            act.activation(sil[:, 0, :], col[:, VEC["c_2"]:VEC["c_2"] + 8], ACT.Sigmoid,
                           bias=zero).then_inc(sem("c_sig"), 1)
            evac_T("mem", 0, MEMT, gain("norm_mem"))
            act.wait_ge(*done("w_k", 1))
            for i in range(4):
                act.activation(KT[:, 2 * i:2 * i + 2, :], B[4 + i][:].rearrange("p (k s) -> p k s", k=2),
                               ACT.Copy).then_inc(sem("kT"), 1)
            evac_T("mix", 4, XT, gain("norm_mix"))
            act.wait_ge(*done("w_in", 3))
            for i in range(2):
                act.activation(CT[:, i * HW:(i + 1) * HW], B[2 + i][:], ACT.Copy).then_inc(sem("mix_c"), 1)
            for t in range(TB):
                act.activation(U[:, t, :], B[6 + t][:], ACT.Copy).then_inc(sem("mix_u"), 1)
            ada(5)
            act.wait_ge(sem("fft_seq"), 1)
            for i, b in enumerate((2, 3, 4, 5)):
                act.activation(FT[:, i, :], B[b][:], ACT.Copy).then_inc(sem("fft_ev"), 1)
            ada(3)
            act.wait_ge(sem("conv_y"), 2)
            act.activation(SQ[:, 0:4, :], YT[:, 0:4, :], ACT.Square, bias=zero).then_inc(sem("mix_sq"), 1)
            ada(2)
            act.wait_ge(sem("fft_y"), 2)
            act.activation(SQ[:, 4:8, :], YT[:, 4:8, :], ACT.Square, bias=zero).then_inc(sem("mix_sq"), 1)
            act.wait_ge(sem("mix_ss"), 1)
            act.activation(RMS[:, 0:2, :], B[4][:].rearrange("p (k s) -> p k s", k=2), ACT.Sqrt, bias=eps5,
                           scale=1.0 / 512).then_inc(sem("mix_rms"), 1)
            ada(2)
            norm_stats("xa", X, XN, 8, (sem("wout_x"), 4))
            ada(2)
            evac_T("xa", 0, XT, gain("norm_xattn"))
            act.wait_ge(*done("w_q", 1))
            for i in range(4):
                act.activation(QT[:, 2 * i:2 * i + 2, :], B[i][:].rearrange("p (k s) -> p k s", k=2), ACT.Copy).then_inc(sem("qT"), 1)
            ada(1)
            for h in range(4):
                act.wait_ge(sem("xa_nm"), h + 1)
                for t in range(TB):
                    act.activation(PR[:, h, t, :], B[h][:, t * S:(t + 1) * S], ACT.Exp, scale=1.0 / 16,
                                   bias=att[:, 0, 2 * h + t:2 * h + t + 1],
                                   accum_out=att[:, 1, 2 * h + t:2 * h + t + 1]).then_inc(sem("xa_e"), 1)
            ada(3)
            for h in range(4):
                act.wait_ge(sem("xa_pt"), h + 1)
                act.activation(PRT[:, h, :, :], B[h][:].rearrange("p (m s) -> p m s", m=2), ACT.Copy).then_inc(
                    sem("xa_pte"), 1)
            for h in range(4):
                act.wait_ge(sem("xa_o"), h + 1)
                act.activation(OT[:, 2 * h:2 * h + 2, :], B[(4, 5, 0, 1)[h]][:].rearrange("p (m s) -> p m s", m=2),
                               ACT.Copy).then_inc(sem("xa_ot"), 1)
            norm_stats("ffn", X, XN, 12, (sem("wo_x"), 4))
            ada(2)
            evac_T("ffn", 0, XT, gain("norm_ffn"))
            act.wait_ge(sem("moe_zero"), 1)
            act.dma_start(bias[0:NE, 0:2 * D], A["b_gate_up"][0]).then_inc(sem("bias_landed"), 16)
            act.dma_start(bias[0:NE, 2 * D:3 * D], A["b_down"][0]).then_inc(sem("bias_landed"), 16)
            act.dma_start(nfin, A["norm_final"][None, :].to_broadcast((P, D))).then_inc(sem("nfin_landed"), 16)
            act.wait_ge(sem("rt_nm"), TB)
            for t in range(TB):
                act.activation(rt[:, t, 0:NE], logit[:, t, 0:NE], ACT.Exp,
                               bias=att[:, 2, t:t + 1]).then_inc(sem("rt_e"), 1)
            ada(4)

            def expert(i, down_done):
                act.wait_ge(sem("e_clamp"), 2 * i + 1)
                act.activation(sig, gcl, ACT.Sigmoid, bias=zero, scale=1.702).then_inc(sem("e_sig"), 1)
                act.wait_ge(sem("e_wT"), i + 1)
                act.activation(wselT[0:CAP, 0], B[2][0:CAP, 0:TB * P].rearrange("p (t n) -> p t n", t=TB),
                               ACT.Copy).then_inc(sem("e_wTe"), 1)
                act.activation(wselT[CAP:P, 1], B[2][CAP:P, 0:TB * P].rearrange("p (t n) -> p t n", t=TB),
                               ACT.Copy).then_inc(sem("e_wTe"), 1)
                act.wait_ge(sem("e_hT"), i + 1)
                act.activation(hT, B[3][:].rearrange("p (c n) -> p c n", c=4), ACT.Copy).then_inc(sem("e_hTe"), 1)
                act.wait_ge(*down_done)
                act.activation(ysb, B[2][:], ACT.Copy).then_inc(sem("e_y"), 1)

            with act.Fori(0, NE) as i:
                expert(i, (used, i * PER_E + (NPRE + PER_E)))
            act.wait_ge(sem("table_ready"), 1)
            n = nc.values_load(table_i[0:1, 32:33], engines=[ENG.Activation], min_val=0, max_val=NX_MAX)
            with act.If(n > 0):
                with act.Fori(0, n) as i:
                    expert(i + NE, (sem("x_down"), i + 1))

            split_hi(act, "ab_in", 0)
            norm_stats("fin", X, XN, 16, (sem("moe_x"), 4))

            act.wait_ge(sem("rope_ang"), 1)
            act.activation(ropeS[:, :, 32:64], ropeS[:, :, 32:64], ACT.Sin, bias=zero).then_inc(sem("rope_sc"), 1)
            act.activation(ropeC[:, :, 0:32], ropeC[:, :, 0:32], ACT.Sin, bias=tb_("halfpi"),
                           scale=-1.0).then_inc(sem("rope_sc"), 1)

            def modcol(a):
                return (lambda k: mod[:, a, 8 + k:9 + k]), (lambda k: mod[:, a, k:k + 1])

            def load_ln(l, ready):
                act.wait_ge(*ready)
                act.dma_start(lng, A["ln_g_2"][l // 2, l % 2, None, :].to_broadcast((P, D))).then_inc(sem("ln_landed"), 16)
                act.dma_start(lnb, A["ln_b_2"][l // 2, l % 2, None, :].to_broadcast((P, D))).then_inc(sem("ln_landed"), 16)

            def gate_rows(l):
                act.wait_ge(*upto(f"ln{l}", "gate_mm", 1))
                for h in range(2):
                    act.activation(XN[:, 1, h * HW:(h + 1) * HW], B[6 + h][:], ACT.Copy).then_inc(sem("gate"), 1)

            def ln_root(l, t):
                act.wait_ge(*upto(f"ln{l}", "ln_var", t + 1))
                act.activation(att[:, 5, 4 + t:5 + t], att[:, 5, 2 * t + 1:2 * t + 2], ACT.Sqrt,
                               bias=eps5).then_inc(sem("ln_root"), 1)

            def evac_hi(a):
                g1, g0 = modcol(a)
                act.wait_ge(sem("mod_g"), 4)
                for q in range(4):
                    act.wait_ge(*upto(f"m{a}", "T", q + 1))
                    for r in range(2):
                        k = 2 * q + r
                        act.activation(XT_r[:, k, :], B[4 + q][:, r * S:(r + 1) * S], ACT.Identity, scale=g1(k),
                                       bias=g0(k)).then_inc(sem("xt_a"), 1)

            def mlp_group(l, it, last):
                n = f"mlp{l}"
                for p in range(2):
                    for b in range(2):
                        c = 2 * p + b + 1
                        if b == 0:
                            act.wait_ge(*upto(n, "mlp_h", it * 2 + (p + 1)))
                        else:
                            act.wait_ge(used, it * R2 + done(n, 2 * p)[1])
                        act.activation(relu_h[:, 2 * b:2 * b + 2, :], B[4 + b][:].rearrange("p (k s) -> p k s", k=2),
                                       ACT.Relu, bias=zero).then_inc(sem("mlp_relu"), 1)
                        act.wait_ge(*upto(n, "mlp_relu", it * 4 + c))
                        act.activation(hid[0][:, 2 * b:2 * b + 2, :], relu_h[:, 2 * b:2 * b + 2, :], ACT.Square,
                                       bias=zero).then_inc(sem("mlp_sq"), 1)
                    if not (last and p == 1):
                        split_hi(act, n, 2 * p + 2, it)
                        split_hi(act, n, 2 * p + 3, it)

            def attend(st, heads, sink, ot):
                for g in range(heads // 4):
                    act.wait_ge(*upto(st, "nm", g + 1))
                    for h in range(4):
                        for t, (a, b) in enumerate(((0, P), (P, 3 * P))):
                            act.activation(SC[:, h, a:b], SC[:, h, a:b], ACT.Exp, bias=att[:, 1, 4 * t + h:4 * t + h + 1],
                                           accum_out=att[:, 2, 4 * t + h:4 * t + h + 1]).then_inc(sem("e"), 1)
                    if sink:
                        act.activation(att[:, 4, 0:8], att[:, 3, 0:8], ACT.Exp, bias=zero).then_inc(sem("e"), 1)
                    for h in range(4):
                        act.wait_ge(*upto(st, "pt", 4 * g + h + 1))
                        act.activation(PT[:, h, :], B[4 + h % 2][:, 0:3 * P], ACT.Copy).then_inc(sem("pte"), 1)
                    act.wait_ge(*upto(st, "o", g + 1))
                    act.activation(ot[0][:, 2 * g:2 * g + 2, :], B[6 + g % 2][:].rearrange("p (m s) -> p m s", m=2),
                                   ACT.Copy).then_inc(sem("ot"), 1)

            split_hi(act, "ab_in", 1)
            evac_hi(0)
            split_hi(act, "ab_in", 2)
            act.wait_ge(*done("ab_in", 2))
            for c in range(3):
                act.activation(Z[:, 0, 408 * c:408 * c + 408], B[c][:, 0:408], ACT.Copy).then_inc(sem("z0"), 1)
            act.wait_ge(sem("z0"), 3)
            act.wait_ge(sem("z1"), 3)
            for t in range(TB):
                act.activation(XN[:, t, 0:256], Z[:, t, 768:1024], ACT.Square, bias=zero,
                               accum_out=stat[:, 20 + t:21 + t]).then_inc(sem("cq_sq"), 1)
            act.wait_ge(sem("cq_sq"), TB)
            act.activation(stat[:, 22:24], stat[:, 20:22], ACT.Sqrt, bias=eps6, scale=1.0 / 256).then_inc(sem("cq_root"), 1)
            split_hi(act, "ab_out", 0)
            split_hi(act, "ab_out", 1)
            act.wait_ge(*upto("fin", "ln_x", 2))
            act.wait_ge(sem("a_T"), 1)
            act.activation(aqT[:, 0:2, :], B[6][:].rearrange("p (m s) -> p m s", m=2), ACT.Copy).then_inc(sem("a_Te"), 1)
            act.activation(aqT[:, 2:4, :], B[7][:].rearrange("p (m s) -> p m s", m=2), ACT.Copy).then_inc(sem("a_Te"), 1)
            act.wait_ge(sem("k_T"), 1)
            act.activation(akT, B[4][:, 0:S], ACT.Copy).then_inc(sem("k_Te"), 1)
            act.activation(bkT, B[4][:, S:2 * S], ACT.Copy).then_inc(sem("k_Te"), 1)
            act.activation(ikT, B[5][:, 0:S], ACT.Copy).then_inc(sem("k_Te"), 1)
            act.wait_ge(sem("i_T"), 1)
            act.activation(iqT[:, 0:2, :], B[6][:].rearrange("p (m s) -> p m s", m=2), ACT.Copy).then_inc(sem("i_Te"), 1)
            act.activation(iqT[:, 2:4, :], B[7][:].rearrange("p (m s) -> p m s", m=2), ACT.Copy).then_inc(sem("i_Te"), 1)
            act.wait_ge(sem("b_T"), 1)
            act.activation(bqT[:, 0:2, :], B[4][:].rearrange("p (m s) -> p m s", m=2), ACT.Copy).then_inc(sem("b_Te"), 1)
            act.activation(bqT[:, 2:4, :], B[5][:].rearrange("p (m s) -> p m s", m=2), ACT.Copy).then_inc(sem("b_Te"), 1)
            for h in range(8):
                act.wait_ge(sem("ix_mm"), h + 1)
                if h >= 2:
                    act.wait_ge(sem("ix_acc"), 2 * (h - 1))
                act.activation(relu_i[:, h % 2, :], B[h % 4][:, 0:3 * P], ACT.Relu, bias=zero).then_inc(sem("ix_relu"), 1)
            attend("aa", 8, True, OTa)
            attend("bb", 8, False, OTb)
            gate_rows(0)
            load_ln(0, upto("bb", "o", 2))
            split_hi(act, "mlp0", 0)
            ln_root(0, 0)
            split_hi(act, "mlp0", 1)
            ln_root(0, 1)
            evac_hi(1)
            with act.Fori(0, 3) as it:
                mlp_group(0, it, False)
            gate_rows(1)
            load_ln(1, upto("ln0", "ln_x", 2))
            mlp_group(0, 3, True)
            split_hi(act, "c_in", 0)
            ln_root(1, 0)
            split_hi(act, "c_in", 1)
            ln_root(1, 1)
            evac_hi(2)
            for i in range(2, 6):
                split_hi(act, "c_in", i)
            act.wait_ge(*done("c_in", 5))
            for i in range(4):
                act.activation(arn(8192 + HW * i, HW), B[i][:], ACT.Copy).then_inc(sem("cv"), 1)
            act.wait_ge(*upto("ln1", "ln_x", 2))
            for m, dst in enumerate((arn(4096, 2048), arn(6144, 2048))):
                for i in range(4):
                    act.wait_ge(sem("c_T"), 4 * m + i + 1)
                    act.activation(dst[:, HW * i:HW * i + HW], B[4 + i][:], ACT.Copy).then_inc(sem("c_Te"), 1)
            split_hi(act, "c_out", 0)
            split_hi(act, "c_out", 1)
            attend("cc", 16, False, OTc)
            gate_rows(2)
            load_ln(2, upto("cc", "o", 4))
            split_hi(act, "mlp1", 0)
            ln_root(2, 0)
            split_hi(act, "mlp1", 1)
            ln_root(2, 1)
            evac_hi(3)
            with act.Fori(0, 3) as it:
                mlp_group(1, it, False)
            gate_rows(3)
            load_ln(3, upto("ln2", "ln_x", 2))
            mlp_group(1, 3, True)
            ln_root(3, 0)
            ln_root(3, 1)

        @block.tensor
        def _(pe):
            at = [0]

            def granule(w=SLOT):
                g = at[0]
                at[0] += 1
                pe.wait_ge(landed[slot_of(g)], FILL[g])
                return slot(slot_of(g), w)

            def transpose_x(st, base, src, ready):
                pe.wait_ge(*ready)
                for q in range(4):
                    for r in range(2):
                        for t in range(TB):
                            k = 2 * q + r
                            mm = pe.transpose(B[base + q][:, r * S + t * P:r * S + t * P + P],
                                              src[:, t, k * P:(k + 1) * P], ident)
                    mm.then_inc(sem("T"), 1)

            def xt_ready(st):
                pe.wait_ge(*upto(st, "xt_a", 4))
                pe.wait_ge(*upto(st, "xt_v", 4))

            def project_T(XTi, base):
                for j in range(2):
                    w = granule().rearrange("p (k n) -> p k n", k=4)
                    for kl in range(4):
                        k = 4 * j + kl
                        for f in range(8):
                            mm = pe.matmul(B[base + f // 2][:, (f % 2) * S:(f % 2) * S + S],
                                           w[:, kl, f * P:(f + 1) * P], XTi[:, k, :],
                                           start=(k == 0 and f % 2 == 0), stop=(k == KC - 1), skip_group_check=True)
                    mm.then_inc(used, 1)

            def project(XTi, base):
                for j in range(2):
                    w = granule().rearrange("p (k n) -> p k n", k=4)
                    for kl in range(4):
                        k = 4 * j + kl
                        for t in range(TB):
                            for h in range(2):
                                mm = pe.matmul(B[base + 2 * t + h][:], XTi(k)[:, t * P:(t + 1) * P],
                                               w[:, kl, h * HW:(h + 1) * HW], start=(k == 0), stop=(k == KC - 1))
                    mm.then_inc(used, 1)

            unit = [0]

            def ada(n):
                def combine(u):
                    pe.wait_ge(sem("ada_part"), u + 1)
                    if u:
                        pe.wait_ge(sem("ada_done"), u)
                    part = ada_part[:, u % 2, :]
                    for c in range(4):
                        mm = pe.matmul(B[7][:, c:c + 1], part[:, c * P:(c + 1) * P], quads[:, 0:1], start=True, stop=True)
                    mm.then_inc(sem("ada_comb"), 1)

                first = unit[0]
                for u in range(first, first + n):
                    w = granule().rearrange("p (k n) -> p k n", k=KC)
                    if u:
                        pe.wait_ge(sem("ada_part"), u)
                    for r in range(2):
                        for c in range(4):
                            mm = pe.matmul(B[6][32 * c:32 * c + 32, :], cs[:, 2 * c + r, :], w[:, 2 * c + r, :],
                                           start=(r == 0), stop=(r == 1))
                    mm.then_inc(used, 1)
                    if u > first:
                        combine(u - 1)
                combine(first + n - 1)
                unit[0] += n

            pe.wait_ge(sem("tab_landed"), 16)
            pe.wait_ge(sem("vec_landed"), 208)
            pe.transpose(B[4][:, 0:NVEC], vec[0:NVEC, 0, :], ident[0:NVEC, 0:NVEC])
            pe.transpose(B[4][:, P:P + NADA * 24], vec[0:NADA * 24, 1, :],
                         ident[0:NADA * 24, 0:NADA * 24]).then_inc(sem("vecT"), 1)
            transpose_x("mem", 0, MEMN, upto("mem", "xn", 2))
            xt_ready("mem")
            pe.wait_ge(sem("col_ready"), 2)
            project_T(MEMT, 4)
            project(lambda k: MEMT[:, k, :], 0)
            pe.wait_ge(sem("kT"), 4)
            transpose_x("mix", 4, XN, upto("mix", "xn", 2))
            xt_ready("mix")
            pe.wait_ge(sem("v"), 4)
            for j in range(4):
                w = granule().rearrange("p (k n) -> p k n", k=2)
                for kl in range(2):
                    k = 2 * j + kl
                    for f in range(12):
                        pe.matmul(B[f // 2][:, (f % 2) * S:(f % 2) * S + S], w[:, kl, f * P:(f + 1) * P],
                                  XT[:, k, :], start=(k == 0 and f % 2 == 0), stop=(k == KC - 1),
                                  skip_group_check=True)
                    for t in range(TB):
                        mm = pe.matmul(B[6 + t][:], XT[:, k, t * P:(t + 1) * P], w[:, kl, 1536:2048],
                                       start=(k == 0), stop=(k == KC - 1))
                mm.then_inc(used, 1)
            pe.wait_ge(sem("mix_u"), 2)
            pe.wait_ge(sem("cs"), 1)
            ada(5)
            pe.wait_ge(sem("dft_landed"), 16)
            pe.wait_ge(sem("mix_c"), 2)
            pe.wait_ge(sem("conv_g"), 2)
            for i, b in enumerate((2, 3, 4, 5)):
                for t in range(TB):
                    mm = pe.matmul(B[b][:], U[:, t, i * P:(i + 1) * P], dft[:, t, :], start=(t == 0), stop=(t == 1))
            mm.then_inc(sem("fft_seq"), 1)
            ada(3)
            pe.wait_ge(sem("fft_ev"), 4)
            for i in range(4):
                o = B[2 + i // 2][:, (i % 2) * S:(i % 2) * S + S]
                pe.matmul(o, tb_("cg"), FT[:, i, 0:S], start=True, stop=False)
                mm = pe.matmul(o, tb_("sg"), FT[:, i, S:2 * S], start=False, stop=True)
            mm.then_inc(sem("fft_grp"), 1)
            ada(2)
            for m in range(2):
                pe.wait_ge(sem("mix_sq"), m + 1)
                for i in range(4):
                    mm = pe.matmul(B[4][:, m * S:(m + 1) * S], ones, SQ[:, 4 * m + i, :], start=(i == 0), stop=(i == 3))
            mm.then_inc(sem("mix_ss"), 1)
            ada(2)
            pe.wait_ge(sem("mix_yn"), 8)
            project(lambda k: YT[:, k, :], 0)
            ada(2)
            transpose_x("xa", 0, XN, upto("xa", "xn", 2))
            xt_ready("xa")
            project_T(XT, 0)
            ada(1)
            pe.wait_ge(sem("qT"), 4)
            for h in range(4):
                for t in range(TB):
                    for c in range(2):
                        mm = pe.matmul(B[h][:, t * S:(t + 1) * S], QT[:, 2 * h + c, t * P:(t + 1) * P],
                                       KT[:, 2 * h + c, :], start=(c == 0), stop=(c == 1))
                mm.then_inc(sem("xa_s"), 1)
            ada(3)
            for h in range(4):
                pe.wait_ge(sem("xa_p"), 2 * h + 2)
                for m in range(2):
                    for t in range(TB):
                        mm = pe.transpose(B[h][:, m * S + t * P:m * S + t * P + P], PR[:, h, t, m * P:(m + 1) * P], ident)
                mm.then_inc(sem("xa_pt"), 1)
            for h in range(4):
                pe.wait_ge(sem("xa_pte"), h + 1)
                for c in range(2):
                    for m in range(2):
                        mm = pe.matmul(B[(4, 5, 0, 1)[h]][:, c * S:(c + 1) * S],
                                       V[:, m, h * 2 * P + c * P:h * 2 * P + c * P + P], PRT[:, h, m, :],
                                       start=(m == 0), stop=(m == 1))
                mm.then_inc(sem("xa_o"), 1)
            pe.wait_ge(sem("xa_ot"), 4)
            project(lambda k: OT[:, k, :], 0)
            ada(2)
            transpose_x("ffn", 0, XN, upto("ffn", "xn", 2))
            xt_ready("ffn")
            pe.wait_ge(sem("router_landed"), 32)
            for t in range(TB):
                for k in range(KC):
                    mm = pe.matmul(B[4][:, t * NE:(t + 1) * NE], XT[:, k, t * P:(t + 1) * P], wr[:, k, :],
                                   start=(k == 0), stop=(k == KC - 1))
            mm.then_inc(sem("logits"), 1)
            ada(4)
            assert at[0] == NPRE
            mask = [rt[:, 4 + t, 0:NE] for t in range(TB)]
            pe.wait_ge(sem("rt_mask"), 4)
            pe.matmul(B[5][:, 0:NE], tri, mask[0], start=True, stop=True)
            pe.matmul(B[5][:, NE:2 * NE], tri, mask[1], start=True, stop=False)
            pe.matmul(B[5][:, NE:2 * NE], ones, mask[0], start=False, stop=True)
            for t in range(TB):
                mm = pe.matmul(B[5][0:NCAND, 64:65], mrep[:, t, :], ones[:, 0:1], start=(t == 0), stop=(t == 1))
            mm.then_inc(sem("rt_pos"), 1)
            pe.wait_ge(sem("flag"), 1)
            pe.matmul(B[5][0:NCAND, 65:66], tri[0:NCAND, 0:NCAND], flag, start=True, stop=True).then_inc(sem("rank"), 1)
            pe.wait_ge(sem("chosen"), 1)
            pe.matmul(B[5][0:1, 96:112], tb_("cand_e")[0:NCAND, :], chosen, start=True, stop=True)
            pe.matmul(B[5][0:1, 112:128], tb_("cand_q")[0:NCAND, :], chosen, start=True, stop=True)
            pe.matmul(B[5][0:1, 128:129], ones[0:NCAND, 0:1], flag, start=True, stop=True).then_inc(sem("table_mm"), 1)

            def gather():
                for k in range(KC):
                    for t in range(TB):
                        mm = pe.matmul(B[3][:, k * CAP:(k + 1) * CAP], XN[:, t, k * P:(k + 1) * P], sel_tok[:, t, :],
                                       start=(t == 0), stop=(t == 1))
                mm.then_inc(sem("e_gather"), 1)

            def bias_gu():
                for m in range(2):
                    for h in range(2):
                        pe.matmul(B[m][CAP * h:CAP * h + CAP, :], selG, bias[:, m * D + h * HW:m * D + (h + 1) * HW],
                                  start=True, stop=False)

            def gate_up(j):
                w = slot(slot_of(NPRE + j)).rearrange("p (k n) -> p k n", k=2)
                for kl in range(2):
                    for m in range(2):
                        for h in range(2):
                            mm = pe.matmul(B[m][CAP * h:CAP * h + CAP, :], xe[:, 2 * j + kl, :],
                                           w[:, kl, m * D + h * HW:m * D + (h + 1) * HW],
                                           start=False, stop=(j == 3 and kl == 1))
                return mm

            def weights_T():
                for t in range(TB):
                    mm = pe.transpose(B[2][:, t * P:(t + 1) * P], wsel[:, t, :], ident)
                mm.then_inc(sem("e_wT"), 1)

            def hidden_T():
                for c in range(4):
                    mm = pe.transpose(B[3][:, c * P:(c + 1) * P], hh_[:, c * P:(c + 1) * P], ident)
                mm.then_inc(sem("e_hT"), 1)

            def bias_d():
                for h in range(2):
                    pe.matmul(B[2][CAP * h:CAP * h + CAP, :], selD, bias[:, 2 * D + h * HW:2 * D + (h + 1) * HW],
                              start=True, stop=False)

            def down(j):
                w = slot(slot_of(NPRE + 4 + j)).rearrange("p (k n) -> p k n", k=4)
                for c in range(4):
                    for h in range(2):
                        mm = pe.matmul(B[2][CAP * h:CAP * h + CAP, :], hT[:, c, CAP * j:CAP * j + CAP],
                                       w[:, c, h * HW:(h + 1) * HW], start=False, stop=(j == 1 and c == 3))
                return mm

            def scatter():
                for t in range(TB):
                    for h in range(2):
                        mm = pe.matmul(B[4 + 2 * t + h][:], wselT[:, h, t, :], ysb, start=False, stop=False,
                                       skip_group_check=True)
                return mm

            pe.wait_ge(sem("e_sel"), 2)
            gather()
            pe.wait_ge(sem("acc_zero"), 4)
            pe.wait_ge(sem("moe_zero"), 2)
            pe.wait_ge(sem("bias_landed"), 32)
            with pe.Fori(0, NE) as i:
                pe.wait_ge(sem("e_selG"), i + 1)
                pe.wait_ge(sem("e_xe"), i + 1)
                bias_gu()
                for j in range(4):
                    g = NPRE + j
                    pe.wait_ge(landed[slot_of(g)], i * 16 + FILL[g])
                    gate_up(j).then_inc(used, 1)
                    if j == 0:
                        pe.wait_ge(sem("e_y"), i + 1)
                        scatter()
                pe.wait_ge(sem("e_sel"), 2 * i + 4)
                gather()
                pe.wait_ge(sem("e_wsel"), 2 * i + 2)
                weights_T()
                pe.wait_ge(sem("e_xe"), i + 2)
                pe.wait_ge(sem("e_h"), i + 1)
                hidden_T()
                pe.wait_ge(sem("e_selD"), i + 1)
                pe.wait_ge(sem("e_wTe"), 2 * i + 2)
                bias_d()
                pe.wait_ge(sem("e_hTe"), i + 1)
                for j in range(2):
                    g = NPRE + 4 + j
                    pe.wait_ge(landed[slot_of(g)], i * 16 + FILL[g])
                    down(j).then_inc(used, 1)
            pe.wait_ge(sem("e_y"), NE + 1)
            scatter().then_inc(sem("acc_main"), 1)
            pe.wait_ge(sem("table_ready"), 1)
            n = nc.values_load(table_i[0:1, 32:33], engines=[ENG.PE], min_val=0, max_val=NX_MAX)
            with pe.If(n > 0):
                with pe.Fori(0, n) as i:
                    pe.wait_ge(sem("e_sel"), 2 * i + (2 * NE + 4))
                    gather()
                    pe.wait_ge(sem("e_selG"), i + (NE + 2))
                    pe.wait_ge(sem("e_xe"), i + (NE + 2))
                    bias_gu()
                    pe.wait_ge(sem("extra_landed"), 16 * PER_E * i + 16 * PER_E)
                    for j in range(4):
                        mm = gate_up(j)
                    mm.then_inc(sem("x_gu"), 1)
                    pe.wait_ge(sem("e_wsel"), 2 * i + (2 * NE + 2))
                    weights_T()
                    pe.wait_ge(sem("e_h"), i + (NE + 1))
                    hidden_T()
                    pe.wait_ge(sem("e_selD"), i + (NE + 1))
                    pe.wait_ge(sem("e_wTe"), 2 * i + (2 * NE + 2))
                    bias_d()
                    pe.wait_ge(sem("e_hTe"), i + (NE + 1))
                    for j in range(2):
                        mm = down(j)
                    mm.then_inc(sem("x_down"), 1)
                    pe.wait_ge(sem("e_y"), i + (NE + 2))
                    scatter().then_inc(sem("extra_used"), 1)
            at[0] = MOE_END

            def gate_rows(l):
                pe.wait_ge(*upto(f"ln{l}", "gate_diag", 1))
                for h in range(2):
                    mm = pe.matmul(B[6 + h][:], ones, XN[:, 0, h * HW:(h + 1) * HW], start=True, stop=True)
                mm.then_inc(sem("gate_mm"), 1)

            def attend(st, heads, q, k, v):
                def scores(g):
                    for h in range(4):
                        if g:
                            pe.wait_ge(*upto(st, "s", 4 * (g - 1) + h + 1))
                        a = 4 * g + h
                        pe.matmul(B[h][:, 0:P], q(a)[:, 0:P], k(a)[:, 0:P], start=True, stop=True)
                        pe.matmul(B[h][:, P:3 * P], q(a)[:, P:2 * P], k(a), start=True, stop=True).then_inc(
                            sem("sc"), 1)

                scores(0)
                for g in range(heads // 4):
                    if g + 1 < heads // 4:
                        scores(g + 1)
                    pe.wait_ge(*upto(st, "p", 2 * g + 2))
                    for h in range(4):
                        n = 4 * g + h
                        if n >= 2:
                            pe.wait_ge(*upto(st, "pte", n - 1))
                        for c in range(3):
                            mm = pe.transpose(B[4 + h % 2][:, c * P:(c + 1) * P], SC[:, h, c * P:(c + 1) * P], ident)
                        mm.then_inc(sem("pt"), 1)
                    if g >= 2:
                        pe.wait_ge(*upto(st, "ot", g - 1))
                        pe.wait_ge(*upto(st, "otl", g - 1))
                    for h in range(4):
                        pe.wait_ge(*upto(st, "pte", 4 * g + h + 1))
                        a, r = 4 * g + h, 64 * (h % 2)
                        o = B[6 + g % 2][r:r + 64, (h // 2) * S:(h // 2) * S + S]
                        pe.matmul(o, v(a, 0), PT[:, h, 0:S], start=True, stop=False, skip_group_check=True)
                        mm = pe.matmul(o[:, P:S], v(a, 1), PT[:, h, S:3 * P], start=False, stop=True,
                                       skip_group_check=True)
                    mm.then_inc(sem("o"), 1)

            def three(out, st, mv, start, stop):
                for a, b in ((0, 0), (0, 1), (1, 0)):
                    mm = pe.matmul(out, st[a], mv[b], start=start and a + b == 0, stop=stop and a == 1,
                                   skip_group_check=True)
                return mm

            def split_granule():
                n = split_no(at[0])
                at[0] += 1
                pe.wait_ge(sem("w_lo"), n)
                return pair(n)

            def chunks(parts, k):
                return [a.rearrange("p (k n) -> p k n", k=k) for a in parts]

            def cut3(parts, k, a, b):
                if len(parts) == 4:
                    parts, k = parts[2 * (k // 4):2 * (k // 4) + 2], k % 4
                return [x[:, k, a:b] for x in parts]

            def transpose_hat(a):
                st = "fin" if a == 0 else f"ln{a - 1}"
                for t in range(TB):
                    pe.wait_ge(*upto(st, "xhat", t + 1))
                    for k in range(KC):
                        mm = pe.transpose(B[4 + k // 2][:, (k % 2) * S + t * P:(k % 2) * S + t * P + P],
                                          X[:, t, k * P:(k + 1) * P], ident)
                        if t == 1 and k % 2 == 1:
                            mm.then_inc(sem("T"), 1)

            def x_chunk(a, k):
                pe.wait_ge(*upto(f"m{a}", "xt_a", k + 1))
                pe.wait_ge(*upto(f"m{a}", "xt_v", k + 1))

            def project3(x, base, ready=None, ln=None):
                for j in range(2):
                    w = chunks(split_granule(), 4)
                    if ln is None or j == 0:
                        for kl in range(4):
                            k = 4 * j + kl
                            if ready is not None:
                                x_chunk(ready, k)
                            for t in range(TB):
                                for h in range(2):
                                    mm = three(B[base + 2 * t + h][:], cut3(x, k, t * P, (t + 1) * P),
                                               cut3(w, kl, h * HW, (h + 1) * HW), k == 0, k == KC - 1)
                        mm.then_inc(used, 1)
                        if ln is not None:
                            gate_rows(ln)
                        continue
                    for t in range(TB):
                        for kl in range(4):
                            k = 4 * j + kl
                            for h in range(2):
                                mm = three(B[base + 2 * t + h][:], cut3(x, k, t * P, (t + 1) * P),
                                           cut3(w, kl, h * HW, (h + 1) * HW), k == 0, k == KC - 1)
                        mm.then_inc(sem("ln_y0") if t == 0 else used, 1)

            def mlp_group(l, it, last):
                n = f"mlp{l}"
                for p in range(2):
                    g = at[0] + 2 * p
                    pe.wait_ge(sem("w_lo"), it * R2 + split_no(g))
                    w = chunks(pair(split_no(g)), KC)
                    for b in range(2):
                        for k in range(KC):
                            if b == 0:
                                x_chunk(2 * l + 1, max(k, 1))
                            for r in range(2):
                                f = 2 * b + r
                                mm = three(B[4 + b][:, r * S:(r + 1) * S], cut3(w, k, f * P, (f + 1) * P),
                                           cut3((XT_r, XTL[2 * l + 1]), k, 0, S), k == 0 and r == 0, k == KC - 1)
                        mm.then_inc(sem("mlp_h") if b == 0 else used, 1)
                    g = g + 1
                    pe.wait_ge(sem("w_lo"), it * R2 + split_no(g))
                    w = chunks(pair(split_no(g)), 4)
                    if p == 0:
                        pe.wait_ge(*upto(n, "mlp_zero", 4))
                    for outer in range(2):
                        for inner in range(2):
                            tail = last and p == 1
                            b, ts = (inner, (outer,)) if tail else (outer, (0, 1) if inner == 0 else ())
                            if ts:
                                pe.wait_ge(*upto(n, "mlp_lo", it * 4 + (2 * p + b + 1)))
                            for r in range(2):
                                for t in ts:
                                    for h in range(2):
                                        mm = three(B[2 * t + h][:], cut3(hid, 2 * b + r, t * P, (t + 1) * P),
                                                   cut3(w, 2 * b + r, h * HW, (h + 1) * HW), False, False)
                        if tail:
                            mm.then_inc(sem("ln_y0") if outer == 0 else used, 1)
                    if not tail:
                        mm.then_inc(used, 1)

            def mlp(l):
                with pe.Fori(0, 3) as it:
                    mlp_group(l, it, False)
                gate_rows(2 * l + 1)
                mlp_group(l, 3, True)
                at[0] += 16

            transpose_hat(0)
            for j in range(3):
                kn = min(3, KC - 3 * j)
                w = [a[:, 0:kn * 1224].rearrange("p (k n) -> p k n", k=kn) for a in split_granule()]
                for kl in range(kn):
                    k = 3 * j + kl
                    x_chunk(0, k)
                    for t in range(TB):
                        if k == 0 and t == 1:
                            x_chunk(0, 3)
                        for c in range(3):
                            mm = three(B[3 * t + c][:, 0:408], cut3((XT_r, XTL[0]), k, t * P, (t + 1) * P),
                                       cut3(w, kl, 408 * c, 408 * c + 408), k == 0, k == KC - 1)
                mm.then_inc(used, 1)
            pe.wait_ge(sem("cq_n"), 2)
            for k in range(2):
                for t in range(TB):
                    mm = pe.transpose(B[6][:, k * S + t * P:k * S + t * P + P],
                                      XN[:, t, S + k * P:S + (k + 1) * P], ident)
            mm.then_inc(sem("cq_T"), 1)
            pe.wait_ge(sem("cqT"), 2)
            pe.wait_ge(sem("z0"), 3)
            pe.wait_ge(sem("z1"), 3)
            w = granule()
            for m in (1, 0):
                wm = w[:, m * 1024:(m + 1) * 1024].rearrange("p (k n) -> p k n", k=2)
                for t in range(TB):
                    for k in range(2):
                        mm = pe.matmul(B[2 * m + t][:], XTf[:, k * S + t * P:k * S + t * P + P], wm[:, k, :],
                                       start=(k == 0), stop=(k == 1))
                if m:
                    mm.then_inc(sem("iq_mm"), 1)
            mm.then_inc(used, 1)
            pe.wait_ge(sem("a_rope"), 2)
            R1a = R1b.rearrange("p (t n) -> p t n", t=TB)
            for j in range(4):
                for t in range(TB):
                    mm = pe.transpose(B[6 + j // 2][:, (j % 2) * S + t * P:(j % 2) * S + t * P + P],
                                      R1a[:, t, j * P:(j + 1) * P], ident)
            mm.then_inc(sem("a_T"), 1)
            pe.wait_ge(sem("k_rope"), 2)
            for t in range(TB):
                pe.transpose(B[4][:, t * P:(t + 1) * P], R1a[:, t, 512:640], ident)
                pe.transpose(B[4][:, S + t * P:S + (t + 1) * P], R2b[:, t, 0:P], ident)
                mm = pe.transpose(B[5][:, t * P:(t + 1) * P], R2b[:, t, P:2 * P], ident)
            mm.then_inc(sem("k_T"), 1)
            for m, (st, src, e) in enumerate((("i_", R4b, "a_Te"), ("b_", R1b, "k_Te"))):
                pe.wait_ge(sem(st + "rope"), 2)
                pe.wait_ge(sem(e), 2 + m)
                s2 = src[:, 0:1024].rearrange("p (t n) -> p t n", t=TB)
                for j in range(4):
                    for t in range(TB):
                        mm = pe.transpose(B[(6, 4)[m] + j // 2][:, (j % 2) * S + t * P:(j % 2) * S + t * P + P],
                                          s2[:, t, j * P:(j + 1) * P], ident)
                mm.then_inc(sem(st + "T"), 1)
            pe.wait_ge(sem("i_Te"), 2)
            pe.wait_ge(sem("k_Te"), 3)
            for h in range(8):
                if h >= 4:
                    pe.wait_ge(sem("ix_relu"), h - 3)
                r = 64 * (h % 2)
                pe.matmul(B[h % 4][:, 0:P], iqT[r:r + 64, h // 2, 0:P], ikT[r:r + 64, 0:P], start=True, stop=True)
                pe.matmul(B[h % 4][:, P:3 * P], iqT[r:r + 64, h // 2, P:S], ikT[r:r + 64, :], start=True,
                          stop=True).then_inc(sem("ix_mm"), 1)
            pe.wait_ge(sem("ix_relu"), 8)
            pe.wait_ge(sem("b_Te"), 2)
            attend("aa", 8, lambda a: aqT[64 * (a // 4):64 * (a // 4) + 64, a % 4, :],
                   lambda a: akT[64 * (a // 4):64 * (a // 4) + 64, :],
                   lambda a, t: Z[:, t, 640 + 64 * (a // 4):704 + 64 * (a // 4)])
            pe.wait_ge(*upto("aa", "s", 8))
            pe.wait_ge(*upto("aa", "otl", 2))
            attend("bb", 8, lambda a: bqT[64 * (a % 2):64 * (a % 2) + 64, a // 2, :],
                   lambda a: bkT[64 * (a % 2):64 * (a % 2) + 64, :], lambda a, t: Z[:, t, 1088:1152])
            pe.wait_ge(*upto("bb", "otl", 2))
            project3(OTa + OTb, 0, ln=0)
            transpose_hat(1)
            mlp(0)
            transpose_hat(2)
            x2 = (XT_r, XTL[2])
            project3(x2, 0, ready=2)
            project3(x2, 4)
            pe.wait_ge(sem("c_rope"), 4)
            project3(x2, 0)
            for m in range(2):
                pe.wait_ge(sem("c_rope"), 8)
                src = arn(2048 * m, 2048).rearrange("p (t n) -> p t n", t=TB)
                for q in range(4):
                    if m:
                        pe.wait_ge(sem("c_Te"), q + 1)
                    for r in range(2):
                        for t in range(TB):
                            k = 2 * q + r
                            mm = pe.transpose(B[4 + q][:, r * S + t * P:r * S + t * P + P],
                                              src[:, t, k * P:(k + 1) * P], ident)
                    mm.then_inc(sem("c_T"), 1)
            pe.wait_ge(sem("c_Te"), 8)
            pe.wait_ge(sem("cv"), 4)
            cqT = arn(4096, 2048).rearrange("p (k s) -> p k s", k=KC)
            ckT = arn(6144, 2048).rearrange("p (k s) -> p k s", k=KC)
            cv = arn(8192, 2048).rearrange("p (t n) -> p t n", t=TB)
            attend("cc", 16, lambda a: cqT[64 * (a % 2):64 * (a % 2) + 64, a // 2, :],
                   lambda a: ckT[64 * (a % 2):64 * (a % 2) + 64, a // 2, :], lambda a, t: cv[:, t, 64 * a:64 * a + 64])
            pe.wait_ge(*upto("cc", "otl", 4))
            project3(OTc, 0, ln=2)
            transpose_hat(3)
            mlp(1)

        @block.vector
        def _(dve):
            steps = [0]

            def link(ins):
                steps[0] += 1
                ins.then_inc(sem("dve_step"), 1)
                dve.wait_ge(sem("dve_step"), steps[0])

            def gain(name):
                return lambda k: col[:, VEC[name] + k:VEC[name] + k + 1]

            def bc(ap, n):
                return ap[:, :, None].to_broadcast((P, ap.shape[1], n))

            def norm(st, src, dst, at):
                dve.wait_ge(*upto(st, "root", 1))
                link(dve.reciprocal(stat[:, 64 + at:66 + at], stat[:, at + 2:at + 4]))
                for t in range(TB):
                    dve.tensor_scalar(dst[:, t, :], src[:, t, :], stat[:, 64 + at + t:65 + at + t], None,
                                      ALU.mult).then_inc(sem("xn"), 1)

            def evac_T(st, base, XTo, g1, g0=None):
                for q in (1, 3):
                    dve.wait_ge(*upto(st, "T", q + 1))
                    for r in range(2):
                        k = 2 * q + r
                        src = B[base + q][:, r * S:(r + 1) * S]
                        if g0 is None:
                            ins = dve.tensor_scalar(XTo[:, k, :], src, g1(k), None, ALU.mult)
                        else:
                            ins = dve.tensor_scalar(XTo[:, k, :], src, g1(k), g0(k), ALU.mult, ALU.add)
                        ins.then_inc(sem("xt_v"), 1)

            unit = [0]

            def ada(n):
                for _ in range(n):
                    u = unit[0]
                    unit[0] += 1
                    a, nb = u // 6, u % 6
                    dve.wait_ge(sem("ada_comb"), u + 1)
                    dve.scalar_tensor_tensor(mod[:, a, 4 * nb:4 * nb + 4], B[7][:, 0:4], float(nb >= 2),
                                             ada_bT[:, 24 * a + 4 * nb:24 * a + 4 * nb + 4], ALU.add,
                                             ALU.add).then_inc(sem("ada_done"), 1)

            def add_residual(st, base, w):
                dve.wait_ge(*done(w, 1))
                for t in range(TB):
                    for h in range(2):
                        xs = X[:, t, h * HW:(h + 1) * HW]
                        dve.tensor_tensor(xs, B[base + 2 * t + h][:], xs, ALU.add).then_inc(sem(st), 1)

            norm("mem", MEM, MEMN, 0)
            norm("mix", X, XN, 4)
            dve.wait_ge(sem("c_sig"), 1)
            link(dve.tensor_tensor(sil[:, 1, :], sil[:, 0, :], col[:, VEC["c_2"]:VEC["c_2"] + 8], ALU.mult))
            dve.tensor_copy(cs[:], bc(sil[:, 1, :], 32)).then_inc(sem("cs"), 1)
            evac_T("mem", 0, MEMT, gain("norm_mem"))
            dve.wait_ge(*done("w_v", 1))
            for t in range(TB):
                for h in range(2):
                    dve.tensor_copy(V[:, t, h * HW:(h + 1) * HW], B[2 * t + h][:]).then_inc(sem("v"), 1)
            evac_T("mix", 4, XT, gain("norm_mix"))
            dve.wait_ge(sem("mix_c"), 2)
            for i in range(2):
                dve.tensor_tensor(GP[:, 2 * i:2 * i + 2, 1:S + 1], CT[:, i * HW:(i + 1) * HW].rearrange(
                    "p (k s) -> p k s", k=2), B[4 + i][:].rearrange("p (k s) -> p k s", k=2),
                    ALU.mult).then_inc(sem("conv_g"), 1)
            dve.wait_ge(sem("conv_g"), 2)
            dve.wait_ge(sem("conv_pad"), 2)
            cw = VEC["conv_w"]
            for tap in (1, 0, 2):
                for k in range(4):
                    wcol = col[:, cw + 4 * tap + k:cw + 4 * tap + k + 1]
                    g = GP[:, k, tap:tap + S]
                    if tap == 1:
                        ins = dve.tensor_scalar(YT[:, k, :], g, wcol, None, ALU.mult)
                    else:
                        ins = dve.scalar_tensor_tensor(YT[:, k, :], g, wcol, YT[:, k, :], ALU.mult, ALU.add)
                    if k == 3:
                        link(ins)
            for i in range(2):
                y = YT[:, 2 * i:2 * i + 2, :]
                dve.tensor_tensor(y, B[i][:].rearrange("p (k s) -> p k s", k=2), y, ALU.mult).then_inc(sem("conv_y"), 1)
            ada(5)
            ada(3)
            dve.wait_ge(sem("conv_y"), 2)
            dve.wait_ge(sem("fft_grp"), 1)
            for i in range(2):
                dve.tensor_copy(YT[:, 4 + 2 * i:6 + 2 * i, :], B[2 + i][:].rearrange("p (k s) -> p k s", k=2)).then_inc(
                    sem("fft_y"), 1)
            ada(2)
            dve.wait_ge(sem("mix_rms"), 1)
            dve.wait_ge(sem("fft_y"), 2)
            link(dve.reciprocal(RMS, RMS))
            for k in range(8):
                gk = gain("g_conv_out")(k)
                dve.scalar_tensor_tensor(YT[:, k, :], YT[:, k, :], gk, RMS[:, k // 4, :], ALU.mult,
                                         ALU.mult).then_inc(sem("mix_yn"), 1)
            ada(2)
            add_residual("wout_x", 0, "w_out")
            norm("xa", X, XN, 8)
            ada(2)
            evac_T("xa", 0, XT, gain("norm_xattn"))
            ada(1)
            for h in range(4):
                dve.wait_ge(sem("xa_s"), h + 1)
                link(dve.reduce_max(att[:, 3, 2 * h:2 * h + 2], B[h][:].rearrange("p (t m) -> p t m", t=TB), AX.X))
                dve.tensor_scalar(att[:, 0, 2 * h:2 * h + 2], att[:, 3, 2 * h:2 * h + 2], -1.0 / 16, None,
                                  ALU.mult).then_inc(sem("xa_nm"), 1)
            for h in range(4):
                dve.wait_ge(sem("xa_e"), 2 * h + 2)
                link(dve.reciprocal(att[:, 4, 2 * h:2 * h + 2], att[:, 1, 2 * h:2 * h + 2]))
                for t in range(TB):
                    dve.tensor_scalar(PR[:, h, t, :], PR[:, h, t, :], att[:, 4, 2 * h + t:2 * h + t + 1], None,
                                      ALU.mult).then_inc(sem("xa_p"), 1)
            ada(3)
            add_residual("wo_x", 0, "w_o")
            norm("ffn", X, XN, 12)
            ada(2)
            evac_T("ffn", 0, XT, gain("norm_ffn"))
            dve.memset(logit[:, :, NE:NE + 4], 3e38).then_inc(sem("rt_pad"), 1)
            dve.memset(gat[:, NE, :], 0.0).then_inc(sem("rt_pad"), 1)
            dve.wait_ge(sem("rt_pad"), 2)
            dve.wait_ge(sem("logits"), 1)
            for t in range(TB):
                link(dve.tensor_tensor(logit[:, t, 0:NE], B[4][:, t * NE:(t + 1) * NE], brow[:], ALU.add))
                link(dve.max(rt[:, t, 40:48], logit[:, t, 0:NE + 4]))
                dve.tensor_scalar(att[:, 2, t:t + 1], rt[:, t, 44:45], -1.0, None, ALU.mult).then_inc(sem("rt_nm"), 1)
                link(dve.match_replace(rt[:, 2 + t, 0:NE + 4], rt[:, t, 40:48], logit[:, t, 0:NE + 4], TAKEN))
                dve.tensor_scalar(rt[:, 4 + t, 0:NE], rt[:, 2 + t, 0:NE], -2e38, None, ALU.is_lt).then_inc(
                    sem("rt_mask"), 1)
            dve.wait_ge(sem("rt_mask"), 2)
            for t in range(TB):
                dve.tensor_copy(mrep[:, t, :].rearrange("p (r e) -> p r e", r=NB_MAX - 1),
                                rt[:, 4 + t, None, 0:NE].to_broadcast((P, NB_MAX - 1, NE))).then_inc(sem("rt_mask"), 1)
            dve.wait_ge(sem("rt_e"), 2)
            for t in range(TB):
                link(dve.tensor_tensor(rt[:, 2 + t, 0:NE], rt[:, t, 0:NE], rt[:, 4 + t, 0:NE], ALU.mult))
                link(dve.reduce_sum(rt[:, t, 50:51], rt[:, 2 + t, 0:NE], AX.X))
                link(dve.reciprocal(rt[:, t, 51:52], rt[:, t, 50:51]))
                link(dve.tensor_scalar(gat[:, 0:NE, t], rt[:, 2 + t, 0:NE], rt[:, t, 51:52], None, ALU.mult))
                link(dve.tensor_scalar(rt[:, 2 + t, 0:NE], rt[:, 4 + t, 0:NE], -FAR, FAR, ALU.mult, ALU.add))
            ada(4)
            dve.wait_ge(sem("rt_pos"), 1)
            link(dve.memset(pos[:], FAR))
            for t in range(TB):
                link(dve.tensor_tensor(pos[:, 0, 0:NE, t], B[5][:, t * NE:(t + 1) * NE], rt[:, 2 + t, 0:NE], ALU.add))
            for b in range(1, NB_MAX):
                link(dve.tensor_scalar(pos[:, b], pos[:, 0], -float(CAP * b), None, ALU.add))
            dve.tensor_tensor(flag, B[5][0:NCAND, 64:65], tb_("thr")[0:NCAND], ALU.is_gt).then_inc(sem("flag"), 1)

            posf = pos[:].rearrange("p b e t -> p (b e) t")

            def select(q):
                for t in range(TB):
                    ins = dve.tensor_scalar(sel_tok[:, t, :], iota[:, 0:CAP], posf[:, bass.ds(q, 1), t], None,
                                            ALU.is_equal)
                    ins.then_inc(sem("e_sel"), 1)

            def expert_row(dst, e):
                return dve.tensor_scalar(dst, ones[:, 0:CAP], ident[:, bass.ds(e, 1)], None, ALU.mult)

            def weigh(q, e):
                for t in range(TB):
                    ins = dve.tensor_scalar(wsel[:, t, :], iota, posf[:, bass.ds(q, 1), t], gat[:, bass.ds(e, 1), t],
                                            ALU.is_equal, ALU.mult)
                    ins.then_inc(sem("e_wsel"), 1)

            def gains_xe():
                g = VEC["norm_ffn"]
                dve.tensor_tensor(xe, B[3][:].rearrange("p (k n) -> p k n", k=KC), bc(col[:, g:g + KC], CAP),
                                  ALU.mult).then_inc(sem("e_xe"), 1)

            def clamp():
                dve.tensor_scalar(gcl, B[0][:], 7.0, None, ALU.min).then_inc(sem("e_clamp"), 1)
                dve.tensor_scalar(ucl, B[1][:], 7.0, -7.0, ALU.min, ALU.max).then_inc(sem("e_clamp"), 1)

            def swiglu(i):
                dve.wait_ge(sem("e_sig"), i + 1)
                dve.wait_ge(sem("e_clamp"), 2 * i + 2)
                dve.tensor_tensor(gl, gcl, sig, ALU.mult).then_inc(sem("e_glu"), 1)
                dve.wait_ge(sem("e_glu"), i + 1)
                dve.scalar_tensor_tensor(hh_, ucl, 1.0, gl, ALU.add, ALU.mult).then_inc(sem("e_h"), 1)

            select(0)
            expert_row(selG, 0).then_inc(sem("e_selG"), 1)
            for b in range(4):
                if b != 1:
                    dve.memset(B[4 + b][:], 0.0).then_inc(sem("acc_zero"), 1)
            dve.wait_ge(sem("rank"), 1)
            dve.tensor_scalar(chosen, iota[0:NCAND, 0:NX_MAX], B[5][0:NCAND, 65:66], flag, ALU.is_equal,
                              ALU.mult).then_inc(sem("chosen"), 1)
            dve.wait_ge(sem("table_mm"), 1)
            dve.tensor_copy(table_i[0:1, 0:33], B[5][0:1, 96:129]).then_inc(sem("table_ready"), 1)
            dve.wait_ge(sem("table_ready"), 1)
            dve.memset(B[5][:], 0.0).then_inc(sem("acc_zero"), 1)
            dve.wait_ge(sem("e_gather"), 1)
            gains_xe()

            with dve.Fori(0, NE) as i:
                dve.wait_ge(used, i * PER_E + (NPRE + 1))
                select(i + 1)
                weigh(i, i)
                expert_row(selG, i + 1).then_inc(sem("e_selG"), 1)
                expert_row(selD, i).then_inc(sem("e_selD"), 1)
                dve.wait_ge(used, i * PER_E + (NPRE + 4))
                clamp()
                dve.wait_ge(sem("e_gather"), i + 2)
                gains_xe()
                swiglu(i)
            n = nc.values_load(table_i[0:1, 32:33], engines=[ENG.DVE], min_val=0, max_val=NX_MAX)
            dve.wait_ge(sem("acc_main"), 1)
            with dve.If(n > 0):
                with dve.Fori(0, n) as i:
                    e = nc.values_load(table_i[0:1, bass.ds(i, 1)], engines=[ENG.DVE], min_val=0, max_val=NE - 1)
                    q = nc.values_load(table_i[0:1, bass.ds(i + 16, 1)], engines=[ENG.DVE], min_val=0,
                                       max_val=NB_MAX * (NE + 1) - 1)
                    select(q)
                    weigh(q, e)
                    expert_row(selG, e).then_inc(sem("e_selG"), 1)
                    expert_row(selD, e).then_inc(sem("e_selD"), 1)
                    dve.wait_ge(sem("e_gather"), i + (NE + 2))
                    gains_xe()
                    dve.wait_ge(sem("x_gu"), i + 1)
                    clamp()
                    swiglu(i + NE)
                    dve.wait_ge(sem("extra_used"), i + 2)
            for t in range(TB):
                for h in range(2):
                    xs = X[:, t, h * HW:(h + 1) * HW]
                    dve.tensor_tensor(xs, B[4 + 2 * t + h][:], xs, ALU.add).then_inc(sem("moe_x"), 1)
            dve.wait_ge(*upto("fin", "root", 1))
            link(dve.reciprocal(stat[:, 80:82], stat[:, 18:20]))
            for t in range(TB):
                dve.tensor_scalar(X[:, t, :], X[:, t, :], stat[:, 80 + t:81 + t], None, ALU.mult).then_inc(
                    sem("xhat"), 1)

            def rope_angles():
                dve.wait_ge(sem("pos_landed"), 32)
                link(dve.tensor_copy(stat[:, 100:102], posi[:]))
                ang, kf, r = ropeS[:, :, 32:64], ropeS[:, :, 0:32], ropeC[:, :, 0:32]
                for t in range(TB):
                    link(dve.tensor_scalar(ang[:, t], tb_("inv"), stat[:, 100 + t:101 + t], None, ALU.mult))
                magic = 12582912.0
                c1 = 6.28125
                c2 = float(np.float32(np.floor((2 * np.pi - c1) * 2 ** 20) / 2 ** 20))
                c3 = 2 * np.pi - c1 - c2
                link(dve.tensor_scalar(kf, ang, 1.0 / (2 * np.pi), magic, ALU.mult, ALU.add))
                link(dve.tensor_scalar(kf, kf, -magic, None, ALU.add))
                for c in (c1, c2, c3):
                    link(dve.scalar_tensor_tensor(ang, kf, -c, ang, ALU.mult, ALU.add))
                link(dve.tensor_scalar(ang, ang, 3.1415925, -3.1415925, ALU.min, ALU.max))
                dve.scalar_tensor_tensor(r, ang, -1.0, ang, ALU.mult, ALU.max).then_inc(sem("rope_ang"), 1)

            def rope_tables():
                dve.wait_ge(sem("rope_sc"), 2)
                link(dve.tensor_copy(ropeC[:, :, 32:64], ropeC[:, :, 0:32]))
                link(dve.tensor_scalar(ropeS[:, :, 0:32], ropeS[:, :, 32:64], -1.0, None, ALU.mult))

            def rope(out, x, tmp, t, st):
                nd = len(out.shape) - 2

                def cs_(tile, a, b):
                    v = tile[:, t, a:b]
                    for _ in range(nd):
                        v = v[:, None]
                    return v.to_broadcast(tuple(out.shape[:-1]) + (b - a,))

                def half(v, a, b):
                    return v[:, :, :, a:b] if nd == 2 else v[:, :, a:b]

                dve.tensor_tensor(out, x, cs_(ropeC, 0, HD), ALU.mult)
                dve.tensor_tensor(half(tmp, 0, 32), half(x, 32, 64), cs_(ropeS, 0, 32), ALU.mult)
                link(dve.tensor_tensor(half(tmp, 32, 64), half(x, 0, 32), cs_(ropeS, 32, 64), ALU.mult))
                dve.tensor_tensor(out, out, tmp, ALU.add).then_inc(sem(st), 1)

            def modcol(a):
                return (lambda k: mod[:, a, 8 + k:9 + k]), (lambda k: mod[:, a, k:k + 1])

            def ot_lo(st, g, ot):
                dve.wait_ge(*upto(st, "ot", g + 1))
                dve.tensor_tensor(ot[1][:, 2 * g:2 * g + 2, :], B[6 + g % 2][:].rearrange("p (m s) -> p m s", m=2),
                                  ot[0][:, 2 * g:2 * g + 2, :].bitcast(F32), ALU.subtract).then_inc(sem("otl"), 1)

            def attend(st, heads, mask, sink, ot):
                for g in range(heads // 4):
                    if g:
                        dve.wait_ge(*upto(st, "pt", 4 * g))
                    for h in range(4):
                        dve.wait_ge(*upto(st, "sc", 4 * g + h + 1))
                        dve.scalar_tensor_tensor(SC[:, h, :], B[h][:, 0:3 * P], HD ** -0.5, mask, ALU.mult,
                                                 ALU.add).then_inc(sem("s"), 1)
                    dve.wait_ge(*upto(st, "s", 4 * g + 4))
                    dve.reduce_max(att[:, 0, 0:4], SC[:, :, 0:P], AX.X)
                    link(dve.reduce_max(att[:, 0, 4:8], SC[:, :, P:3 * P], AX.X))
                    if sink:
                        sk = sinkb[:, None, 4 * g:4 * g + 4].to_broadcast((P, TB, 4))
                        mx = att[:, 0, 0:8].rearrange("p (t h) -> p t h", t=TB)
                        link(dve.tensor_tensor(mx, mx, sk, ALU.max))
                    ins = dve.tensor_scalar(att[:, 1, 0:8], att[:, 0, 0:8], -1.0, None, ALU.mult)
                    if sink:
                        link(ins)
                        ins = dve.tensor_tensor(att[:, 3, 0:8].rearrange("p (t h) -> p t h", t=TB), sk,
                                                att[:, 1, 0:8].rearrange("p (t h) -> p t h", t=TB), ALU.add)
                    ins.then_inc(sem("nm"), 1)
                    dve.wait_ge(*upto(st, "e", (9 if sink else 8) * (g + 1)))
                    if sink:
                        link(dve.tensor_tensor(att[:, 2, 0:8], att[:, 2, 0:8], att[:, 4, 0:8], ALU.add))
                    link(dve.reciprocal(att[:, 0, 8:16], att[:, 2, 0:8]))
                    for t, (a, b) in enumerate(((0, P), (P, 3 * P))):
                        dve.tensor_tensor(SC[:, :, a:b], SC[:, :, a:b], bc(att[:, 0, 8 + 4 * t:12 + 4 * t], b - a),
                                          ALU.mult).then_inc(sem("p"), 1)
                    if g:
                        ot_lo(st, g - 1, ot)
                ot_lo(st, heads // 4 - 1, ot)

            def gate_diag(l):
                dve.tensor_tensor(XN[:, 0, :].rearrange("p (k n) -> p k n", k=KC),
                                  ident[:, None, :].to_broadcast((P, KC, P)), bc(mod[:, l, 16:24], P),
                                  ALU.mult).then_inc(sem("gate_diag"), 1)

            def layer_norm(l, w, last):
                dve.wait_ge(*upto(f"ln{l}", "gate", 2))
                dve.wait_ge(*upto(HATS[l], "ln_x", 2))
                for t in range(TB):
                    if t == 0:
                        dve.wait_ge(*upto(f"ln{l}", "ln_y0", 1))
                    else:
                        dve.wait_ge(*done(w, last))
                    for h in range(2):
                        ins = dve.tensor_tensor(XN[:, 0, h * HW:(h + 1) * HW], B[2 * t + h][:],
                                                XN[:, 1, h * HW:(h + 1) * HW], ALU.mult)
                    link(ins)
                    link(dve.scalar_tensor_tensor(X[:, t, :], X[:, t, :], 4.0 ** 0.25, XN[:, 0, :], ALU.mult, ALU.add))
                    for h in range(2):
                        ins = dve.bn_stats(rt[:, t, 6 * h:6 * h + 6], X[:, t, h * HW:(h + 1) * HW])
                    link(ins)
                    dve.bn_aggr(att[:, 5, 2 * t:2 * t + 2], rt[:, t, 0:12]).then_inc(sem("ln_var"), 1)
                    dve.wait_ge(*upto(f"ln{l}", "ln_root", t + 1))
                    link(dve.reciprocal(att[:, 5, 6 + t:7 + t], att[:, 5, 4 + t:5 + t]))
                    dve.tensor_scalar(X[:, t, :], X[:, t, :], att[:, 5, 2 * t:2 * t + 1], att[:, 5, 6 + t:7 + t],
                                      ALU.subtract, ALU.mult).then_inc(sem("xhat"), 1)
                    if l == 3:
                        dve.wait_ge(*upto("ln3", "ln_landed", 32))
                        dve.wait_ge(*upto("ln3", "xhat", t + 1))
                        link(dve.tensor_tensor(X[:, t, :], X[:, t, :], lng, ALU.mult))
                        dve.tensor_tensor(X[:, t, :], X[:, t, :], lnb, ALU.add).then_inc(sem("ln_x"), 1)

            def evac_lo(a):
                g1, g0 = modcol(a)
                for q in range(4):
                    dve.wait_ge(*upto(f"m{a}", "xt_a", 2 * q + 2))
                    for r in range(2):
                        k = 2 * q + r
                        if k >= 4:
                            dve.wait_ge(*upto(f"m{a}", "xt_v", k - 3))
                        ins = dve.scalar_tensor_tensor(XN[:, 0, k % 4 * S:k % 4 * S + S], B[4 + q][:, r * S:(r + 1) * S],
                                                       g1(k), XT_r[:, k, :].bitcast(F32), ALU.mult, ALU.subtract)
                    link(ins)
                    for r in range(2):
                        k = 2 * q + r
                        dve.tensor_scalar(XTL[a][:, k, :], XN[:, 0, k % 4 * S:k % 4 * S + S], g0(k), None,
                                          ALU.add).then_inc(sem("xt_v"), 1)
                dve.wait_ge(*upto(f"m{a}", "xt_v", KC))

            def mlp_group(l, it, last):
                n = f"mlp{l}"
                for p in range(2):
                    for b in range(2):
                        c = 2 * p + b + 1
                        dve.wait_ge(*upto(n, "mlp_relu", it * 4 + c))
                        hb = slice(2 * b, 2 * b + 2)
                        dve.tensor_tensor(sq_h[:, hb, :], relu_h[:, hb, :], relu_h[:, hb, :],
                                          ALU.mult).then_inc(sem("mlp_tt"), 1)
                        dve.wait_ge(*upto(n, "mlp_tt", it * 4 + c))
                        dve.wait_ge(*upto(n, "mlp_sq", it * 4 + c))
                        dve.tensor_tensor(hid[1][:, hb, :], sq_h[:, hb, :], hid[0][:, hb, :].bitcast(F32),
                                          ALU.subtract).then_inc(sem("mlp_lo"), 1)
                    if not (last and p == 1):
                        split_lo(dve, n, 2 * p + 2, it)
                        split_lo(dve, n, 2 * p + 3, it)

            def mlp(l):
                split_lo(dve, f"mlp{l}", 1)
                for b in range(4):
                    dve.memset(B[b][:], 0.0).then_inc(sem("mlp_zero"), 1)
                with dve.Fori(0, 3) as it:
                    mlp_group(l, it, False)
                gate_diag(2 * l + 1)
                mlp_group(l, 3, True)

            rope_angles()
            evac_lo(0)
            rope_tables()
            split_lo(dve, "ab_in", 1)
            split_lo(dve, "ab_in", 2)
            dve.wait_ge(*done("ab_in", 2))
            for c in range(3):
                dve.tensor_copy(Z[:, 1, 408 * c:408 * c + 408], B[3 + c][:, 0:408]).then_inc(sem("z1"), 1)
            dve.wait_ge(sem("cq_root"), 1)
            link(dve.reciprocal(stat[:, 84:86], stat[:, 22:24]))
            for t in range(TB):
                dve.tensor_scalar(XN[:, t, S:2 * S], Z[:, t, 768:1024], stat[:, 84 + t:85 + t], None,
                                  ALU.mult).then_inc(sem("cq_n"), 1)
            dve.wait_ge(sem("cq_T"), 1)
            for k in range(2):
                dve.tensor_scalar(XTf[:, k * S:(k + 1) * S], B[6][:, k * S:(k + 1) * S], gain("ab_q_norm_2")(k), None,
                                  ALU.mult).then_inc(sem("cqT"), 1)
            tmp = XNf[:, 512:1152]
            R1a = R1b.rearrange("p (t n) -> p t n", t=TB)
            for t in range(TB):
                out = R1a[:, t, 0:512].rearrange("p (j g d) -> p j g d", j=4, g=2)
                rope(out, Z[:, t, 0:512].rearrange("p (g j d) -> p j g d", j=4, g=2),
                     tmp[:, 0:512].rearrange("p (j g d) -> p j g d", j=4, g=2), t, "a_rope")
                dve.wait_ge(sem("a_rope"), t + 1)
            for t in range(TB):
                rope(R1a[:, t, 512:640].rearrange("p (g d) -> p g d", g=2),
                     Z[:, t, 512:640].rearrange("p (g d) -> p g d", g=2),
                     tmp[:, 0:128].rearrange("p (g d) -> p g d", g=2), t, "ak_rope")
                dve.wait_ge(sem("ak_rope"), t + 1)
                two = Z[:, t, 1024:1280 - 64].rearrange("p (m d) -> p m d", d=HD)[:, 0:3:2, :]
                rope(R2b[:, t, :].rearrange("p (m c d) -> p m c d", m=2, c=2)[:, :, 0, :], two,
                     tmp[:, 0:128].rearrange("p (g d) -> p g d", g=2), t, "bk_rope")
                dve.wait_ge(sem("bk_rope"), t + 1)
                r2 = R2b[:, t, :].rearrange("p (m c d) -> p m c d", m=2, c=2)
                dve.tensor_copy(r2[:, :, 1, :], r2[:, :, 0, :]).then_inc(sem("k_rope"), 1)
            dve.wait_ge(sem("iq_mm"), 1)
            for t in range(TB):
                rope(R4b[:, t * HW:(t + 1) * HW].rearrange("p (h d) -> p h d", d=HD),
                     B[2 + t][:].rearrange("p (h d) -> p h d", d=HD), tmp[:, 0:512].rearrange("p (h d) -> p h d", d=HD),
                     t, "i_rope")
                dve.wait_ge(sem("i_rope"), t + 1)
            dve.wait_ge(*done("uq", 0))
            dve.wait_ge(sem("k_T"), 1)
            for t in range(TB):
                rope(R1b[:, t * HW:(t + 1) * HW].rearrange("p (h d) -> p h d", d=HD),
                     B[t][:].rearrange("p (h d) -> p h d", d=HD), tmp[:, 0:512].rearrange("p (h d) -> p h d", d=HD),
                     t, "b_rope")
                dve.wait_ge(sem("b_rope"), t + 1)
            iw = rt[:, 0, 0:16].rearrange("p (t h) -> p t h", t=TB)
            link(dve.tensor_scalar(iw, Z[:, :, 1216:1224], 8 ** -0.5 * HD ** -0.5, None, ALU.mult))
            for h in range(8):
                dve.wait_ge(sem("ix_relu"), h + 1)
                if h:
                    dve.wait_ge(sem("ix_acc"), 2 * h)
                for t, (a, b) in enumerate(((0, P), (P, 3 * P))):
                    rl, w = relu_i[:, h % 2, a:b], iw[:, t, h:h + 1]
                    if h == 0:
                        ins = dve.tensor_scalar(idx[:, a:b], rl, w, None, ALU.mult)
                    else:
                        ins = dve.scalar_tensor_tensor(idx[:, a:b], rl, w, idx[:, a:b], ALU.mult, ALU.add)
                    ins.then_inc(sem("ix_acc"), 1)
            dve.wait_ge(sem("ix_acc"), 16)
            link(dve.tensor_tensor(idx, idx, tb_("full"), ALU.add))
            topk = 64
            for rnd in range(topk // 8):
                src = idx if rnd == 0 else left
                dve.max(rt[:, 1, 0:8], src[:, 0:P])
                link(dve.max(rt[:, 1, 8:16], src[:, P:3 * P]))
                dve.match_replace(left[:, 0:P], rt[:, 1, 0:8], src[:, 0:P], TAKEN)
                link(dve.match_replace(left[:, P:3 * P], rt[:, 1, 8:16], src[:, P:3 * P], TAKEN))
            link(dve.tensor_scalar(left, left, -2e38, NEG, ALU.is_gt, ALU.mult))
            link(dve.tensor_tensor(bmask, left, tb_("full"), ALU.add))
            dve.wait_ge(sem("sink_landed"), 16)
            attend("aa", 8, tb_("window"), True, OTa)
            dve.wait_ge(*upto("aa", "pt", 8))
            attend("bb", 8, bmask, False, OTb)
            dve.wait_ge(*upto("bb", "pt", 8))
            gate_diag(0)
            layer_norm(0, "ab_out", 1)
            evac_lo(1)
            mlp(0)
            layer_norm(1, "mlp0", 15)
            evac_lo(2)
            for i in range(1, 4):
                split_lo(dve, "c_in", i)
            tmps = XNf.rearrange("p (i n) -> p i n", i=4)
            for m in range(2):
                dve.wait_ge(*done("c_in", 2 * m + 1))
                dst = arn(2048 * m, 2048)
                for t in range(TB):
                    for h in range(2):
                        a = t * D + h * HW
                        rope(dst[:, a:a + HW].rearrange("p (h d) -> p h d", d=HD),
                             B[4 * m + 2 * t + h][:].rearrange("p (h d) -> p h d", d=HD),
                             tmps[:, 2 * t + h, :].rearrange("p (h d) -> p h d", d=HD), t, "c_rope")
                if m == 0:
                    split_lo(dve, "c_in", 4)
                    split_lo(dve, "c_in", 5)
            dve.wait_ge(sem("c_rope"), 8)
            attend("cc", 16, tb_("full"), False, OTc)
            dve.wait_ge(*upto("cc", "pt", 16))
            gate_diag(2)
            layer_norm(2, "c_out", 1)
            evac_lo(3)
            mlp(1)
            layer_norm(3, "mlp1", 15)


_INS = ["x", "mem", "norm_mix", "w_in", "conv_w", "g_conv_out", "g_fft_out", "w_out", "norm_xattn", "norm_mem", "w_q",
        "w_k", "w_v", "w_o", "norm_ffn", "w_router", "b_router", "w_gate_up", "b_gate_up", "w_down", "b_down",
        "norm_final", "c_2", "positions_2", "ab_w_in_2", "ab_q_norm_2", "ab_w_uq_2", "ab_w_uiq_2", "ab_sinks_2",
        "ab_w_out_2", "c_w_in_2", "c_w_out_2", "ada_w_2", "ada_b_2", "ln_g_2", "ln_b_2", "mlp_w1_2", "mlp_w2_2"]


def kernel(**inputs):
    import concourse.bacc as bacc
    from concourse.bass_utils import run_bass_kernel_spmd

    nc = bacc.Bacc("TRN2", target_bir_lowering=False, num_devices=1)
    arrays = {f"in_{name}": np.ascontiguousarray(inputs[name]) for name in _INS}
    arrays["in_tables"], arrays["in_dft"] = tables()
    aps = {n: nc.dram_tensor(n, a.shape, mybir.dt.from_np(a.dtype), kind="ExternalInput").ap()
           for n, a in arrays.items()}
    out = nc.dram_tensor("out", (1, S, D), F32, kind="ExternalOutput").ap()
    build_program(nc, {n: aps[f"in_{n}"] for n in _INS}, aps["in_tables"], aps["in_dft"], out)
    r = run_bass_kernel_spmd(nc, [arrays], core_ids=[0])
    return r.results[0]["out"]
```

```python
from contextlib import ExitStack

import numpy as np
import concourse.bass as bass
from concourse import mybir

F32 = mybir.dt.float32
I32 = mybir.dt.int32
F32R = mybir.dt.float32r
ALU = mybir.AluOpType
ACT = mybir.ActivationFunctionType
AX = mybir.AxisListType
ENG = mybir.EngineType

P = 128
S = 256
TB = S // P
D = 1024
KC = D // P
NE = 32
TOPK = 4
CAP = 64
NB_MAX = S // CAP
NCAND = (NB_MAX - 1) * NE
NX_MAX = S * TOPK // CAP
SLOT = 4096
HW = 512
HD = 64
NEG = -1e30
TAKEN = -3e38
FAR = 10000.0

T_COLS = {}


def tables():
    p = np.arange(P)[:, None]
    c = np.arange(P)[None, :]
    parts = {}
    parts["ident"] = (p == c) * 1.0
    parts["tri"] = (p < c) * 1.0
    parts["ones"] = np.ones((P, P))
    parts["quads"] = (p % 32 == 0) * 1.0
    parts["iota"] = np.repeat(c % CAP, P, 0)
    causal = np.where(c <= p, 0.0, NEG)
    parts["full"] = np.concatenate([causal, np.zeros((P, P)), causal], 1)
    parts["window"] = np.concatenate([causal, np.where(c > p, 0.0, NEG), causal], 1)
    ang = 2 * np.pi * np.outer(np.arange(64), np.arange(64)) / 64
    same = np.kron(np.eye(2), np.ones((64, 64)))
    parts["cg"] = np.tile(np.cos(ang), (2, 2)) * same / 8
    parts["sg"] = -np.tile(np.sin(ang), (2, 2)) * same / 8
    inv = np.float32(10000.0) ** (-np.arange(0, HD, 2, dtype=np.float32) / np.float32(HD))
    parts["inv"] = np.repeat(inv[None], P, 0)
    parts["eps5"] = np.full((P, 1), 1e-5)
    parts["eps6"] = np.full((P, 1), 1e-6)
    parts["zero"] = np.zeros((P, 1))
    parts["halfpi"] = np.full((P, 1), np.pi / 2)
    q = np.minimum(np.arange(P), NCAND - 1)[:, None]
    parts["thr"] = CAP * (1 + q // NE)
    parts["cand_e"] = q % NE
    parts["cand_q"] = (1 + q // NE) * (NE + 1) + q % NE
    parts["shift"] = np.repeat(CAP * np.arange(NB_MAX)[None], P, 0)
    at = 0
    for n, a in parts.items():
        T_COLS[n] = (at, at + a.shape[1])
        at += a.shape[1]
    t = np.concatenate([np.asarray(a, np.float32) for a in parts.values()], 1)
    ang = 2 * np.pi * (np.outer(np.arange(S), np.arange(S)) % S) / S
    dft = np.concatenate([np.cos(ang), np.sin(ang)], 1) / 16
    return np.ascontiguousarray(t), np.ascontiguousarray(dft.astype(np.float32))


tables()
TAB_W = max(b for _, b in T_COLS.values())

VEC = {"norm_mix": 0, "norm_xattn": 8, "norm_mem": 16, "norm_ffn": 24, "g_conv_out": 32, "g_fft_out": 36,
       "conv_w": 40, "ab_q_norm_2": 52, "c_2": 54, "norm_final": 62, "ln_g_2": 70, "ln_b_2": 94}
NVEC = 118
NADA = 4
ADA_UNITS = NADA * 6

ADA_AT = [("mix_in", 5), ("fft", 3), ("yfft", 2), ("mixss", 2), ("mix_out", 2), ("q", 1), ("scores", 3),
          ("w_o", 2), ("router", 4)]


def pre_stream():
    out = [("w_k", i) for i in range(2)] + [("w_v", i) for i in range(2)] + [("w_in", i) for i in range(4)]
    u = 0
    tail = {"mixss": [("w_out", 0), ("w_out", 1)], "mix_out": [("w_q", 0), ("w_q", 1)],
            "scores": [("w_o", 0), ("w_o", 1)]}
    for name, n in ADA_AT:
        out += [("ada", u + i) for i in range(n)]
        u += n
        out += tail.get(name, [])
    assert u == ADA_UNITS
    return out


PRE = pre_stream()
NPRE = len(PRE)
R0 = 4
R1 = 6
E_SLOTS = [4, 5] + [(NPRE - R0 + j) % R0 for j in range(R0)]
SPLIT = [p for p in PRE if p[0] != "ada"]
PER_E = 6
MOE_END = NPRE + NE * PER_E
POST = ([("ab_in", i) for i in range(3)] + [("uq", 0)] + [("ab_out", i) for i in range(2)] + [("mlp0", i) for i in range(16)]
        + [("c_in", i) for i in range(6)] + [("c_out", i) for i in range(2)] + [("mlp1", i) for i in range(16)])
SLOTS = 8
R2 = 4
POST_SLOTS = [6, 7] + E_SLOTS[0:2]
PAIRS = (E_SLOTS[2:4], E_SLOTS[4:6])
UQ = POST.index(("uq", 0))


def slot_of(g):
    if g < NPRE:
        return g % R0
    return E_SLOTS[(g - NPRE) % R1] if g < MOE_END else POST_SLOTS[(g - MOE_END) % R2]


FILL, OWNER = {}, {}


def lay_stream():
    count, last = [0] * SLOTS, {}
    for g in range(MOE_END + len(POST)):
        s = slot_of(g)
        count[s] += 2 if g == MOE_END + UQ else 1
        FILL[g] = 16 * count[s]
        OWNER[g] = last.get(s)
        last[s] = g


lay_stream()


def split_no(g):
    q = g - MOE_END
    assert q >= 0 and q != UQ
    return 2 * len(SPLIT) + q + 1 - (q > UQ)


NORMS = ("mem", "mix", "xa", "ffn", "fin")
TURNS = ("mem", "mix", "xa", "ffn", "m0", "m1", "m2", "m3")
HATS = ("fin", "ln0", "ln1", "ln2", "ln3")
LNS = ("ln0", "ln1", "ln2", "ln3")
ATTNS = {"ab": (8, 4), "cc": (8, 0)}


def exps_of(st, u):
    return 4 * u + min(u, ATTNS[st][1])


SHARES = {}
for _kind, _per in (("sq", 2), ("root", 1), ("xn", 2)):
    SHARES[_kind] = [(st, _per) for st in NORMS]
for _kind in ("T", "xt_a", "xt_v"):
    SHARES[_kind] = [(st, 4) for st in TURNS]
SHARES["xt_a"] = [(st, 4 if st == "ffn" else 8) for st in TURNS]
SHARES["xt_v"] = SHARES["xt_a"]
for _kind, _per in (("xhat", 2), ("ln_x", 2)):
    SHARES[_kind] = [(st, _per) for st in HATS]
for _kind, _per in (("ln_y0", 1), ("ln_var", 2), ("ln_root", 2), ("ln_landed", 32), ("gate_diag", 1), ("gate_mm", 1),
                    ("gate", 2)):
    SHARES[_kind] = [(st, _per) for st in LNS]
for _kind, _per in (("sc", 2), ("s", 2), ("nm", 1), ("p", 2), ("pt", 2), ("pte", 2)):
    SHARES[_kind] = [(st, _per * u) for st, (u, _) in ATTNS.items()]
for _kind in ("o", "ot", "otl"):
    SHARES[_kind] = [(st, u // 2) for st, (u, _) in ATTNS.items()]
for _kind in ("op_hi", "op_lo"):
    SHARES[_kind] = [("y", 2), ("xo", 4)]
SHARES["e"] = [(st, exps_of(st, u)) for st, (u, _) in ATTNS.items()]
for _kind, _per in (("mlp_zero", 4), ("mlp_h", 8), ("mlp_relu", 16), ("mlp_sq", 16), ("mlp_tt", 16), ("mlp_lo", 16)):
    SHARES[_kind] = [(st, _per) for st in ("mlp0", "mlp1")]


def base_of(st, kind):
    at = 0
    for name, n in SHARES[kind]:
        if name == st:
            return at
        at += n
    raise KeyError(st)


def build_program(nc, A, tab_d, dft_d, out_d):
    ctx = ExitStack()
    with ctx:
        sems = {}

        def sem(name):
            if name not in sems:
                sems[name] = ctx.enter_context(nc.semaphore(name))
            return sems[name]

        def done(name, i):
            g = PRE.index((name, i)) if (name, i) in PRE else MOE_END + POST.index((name, i))
            return sem("granules_used"), g + 1

        def upto(st, kind, v):
            return sem(kind), v + base_of(st, kind)

        def sb(name, shape, dt=F32):
            return ctx.enter_context(nc.sbuf_tensor("sb_" + name, shape, dt))

        wide = {"ring": [P, SLOTS * SLOT], "XT": [P, KC, S], "arena": [P, 5 * 2048]}
        at = (nc.sbuf_base + 31) // 32 * 32
        sb("fence", [P, 8 + sum(int(np.prod(w[1:])) for w in wide.values())])
        pairs = [[nc.alloc_sbuf_tensor_at(f"w_{part}{i}", [P, SLOT], F32R, offset=at + 4 * SLOT * s)
                  for part, s in zip(("hi", "lo"), slots)] for i, slots in enumerate(PAIRS)]
        halves = [[nc.alloc_sbuf_tensor_at(f"half_{part}{i}", [P, SLOT // 2], F32R, offset=at + 4 * SLOT * (R0 + i) + b)
                   for part, b in (("hi", 0), ("lo", 2 * SLOT))] for i in range(2)]
        for name, shape in wide.items():
            wide[name] = [nc.alloc_sbuf_tensor_at(n, shape, dt, offset=at)
                          for n, dt in ((name, F32), (name + "_r", F32R))[:1 if name == "ring" else 2]]
            at += 4 * int(np.prod(shape[1:]))
        ring, = wide["ring"]
        XT, XT_r = wide["XT"]
        arena, arena_r = wide["arena"]

        B = [ctx.enter_context(nc.psum_tensor(f"bank{i}", [P, HW], F32)) for i in range(8)]
        tab = sb("tab", [P, TAB_W])
        X = sb("X", [P, TB, D])
        XN = sb("XN", [P, TB, D])
        vec = sb("vec", [P, 2, P])
        col = sb("col", [P, NVEC])
        ada_bT = sb("ada_bT", [P, NADA * 24])
        mod = sb("mod", [P, NADA, 24])
        cs = sb("cs", [P, KC, 32])
        sil = sb("sil", [P, 2, 8])
        stat = sb("stat", [P, 128])
        pos = sb("pos", [P, NB_MAX, NE + 1, TB])
        gat = sb("gat", [P, NE + 1, TB])
        logit = sb("logit", [P, TB, 40])
        rt = sb("rt", [P, 6, 64])
        brow = sb("brow", [P, NE])
        wr = sb("wr", [P, KC, NE])
        table_i = sb("table_i", [1, 40], I32)
        ropeC = sb("ropeC", [P, TB, HD])
        ropeS = sb("ropeS", [P, TB, HD])
        posi = sb("posi", [P, TB], I32)
        att = sb("att", [P, 6, 16])
        mrep = vec[:, :, 0:NCAND]
        sinkb = stat[:, 48:56]
        flag = stat[0:NCAND, 56:57]
        chosen = stat[0:NCAND, 104:104 + NX_MAX]

        def tb_(n):
            a, b = T_COLS[n]
            return tab[:, a:b]

        ident, tri, ones, quads, iota = (tb_(n) for n in ("ident", "tri", "ones", "quads", "iota"))
        eps5, eps6, zero = tb_("eps5"), tb_("eps6"), tb_("zero")

        def slot(s, w=SLOT):
            return ring[:, s * SLOT:s * SLOT + w]

        def arn(a, w):
            return arena[:, a:a + w]

        def arn_r(a, w):
            return arena_r[:, a:a + w]

        def pair(n):
            return [part[:] for part in pairs[(n - 1) % 2]]

        XT_rf = XT_r[:].rearrange("p k s -> p (k s)")

        ext = ring[:, 6 * SLOT:8 * SLOT]
        MEM = arn(0, 2048).rearrange("p (t d) -> p t d", t=TB)
        MEMN = arn(2048, 2048).rearrange("p (t d) -> p t d", t=TB)
        MEMT, XTmix, XTxa, YTs, OTx = ([x.rearrange("p (k s) -> p k s", k=KC) for x in xs] for xs in (
            (arn_r(4096, 2048), arn_r(6144, 2048)), (XT_rf, arn_r(2048, 2048)), (XT_rf, arn_r(6144, 2048)),
            (arn_r(4096, 2048), arn_r(2048, 2048)), (arn_r(4096, 2048), arn_r(6144, 2048))))
        KT = ext[:, 0:2048].rearrange("p (k s) -> p k s", k=KC)
        V = ext[:, 2048:4096].rearrange("p (t d) -> p t d", t=TB)
        dft = ext[:, 4096:5120].rearrange("p (t n) -> p t n", t=TB)
        ada_part = ext[:, 5120:6144].rearrange("p (i n) -> p i n", i=2)
        QT = ext[:, 6144:8192].rearrange("p (k s) -> p k s", k=KC)
        CT = arn(0, 1024)
        U = arn(1024, 1024).rearrange("p (t n) -> p t n", t=TB)
        SQ = arn(2048, 2048).rearrange("p (k s) -> p k s", k=8)
        FT = arn(4096, 2048).rearrange("p (k n) -> p k n", k=4)
        GP = arn(6144, 4 * (S + 2)).rearrange("p (k s) -> p k s", k=4)
        RMS = arn(7300, 512).rearrange("p (k s) -> p k s", k=2)
        YT = arn(8192, 2048).rearrange("p (k s) -> p k s", k=8)
        PR = arn(0, 2048).rearrange("p (h t m) -> p h t m", h=4, t=TB)
        PRT = arn(2048, 2048).rearrange("p (h m s) -> p h m s", h=4, m=2)
        bias = arn(0, 3 * D)
        gcl, ucl, sig, gl, hh_ = (arn(3072 + 512 * i, 512) for i in range(5))
        hT = arn(5632, 512).rearrange("p (c n) -> p c n", c=4)
        ysb = arn(6144, 512)
        sel_tok = arn(6656, TB * CAP).rearrange("p (t n) -> p t n", t=TB)
        wsel = arn(6784, TB * P).rearrange("p (t n) -> p t n", t=TB)
        wselT = arn(7040, 2 * TB * P).rearrange("p (h t n) -> p h t n", h=2, t=TB)
        selG = arn(7552, CAP)
        selD = arn(7616, CAP)
        xe = arn(7680, KC * CAP).rearrange("p (k n) -> p k n", k=KC)
        nfin = arn(8192, D)
        Z = arn(0, 2 * 1224).rearrange("p (t n) -> p t n", t=TB)
        R1b = arn(2448, 1280)
        R2b = arn(3728, 512).rearrange("p (t n) -> p t n", t=TB)
        R4b = arn(4240, 1024)
        aqT = arn(5264, 1024).rearrange("p (k s) -> p k s", k=4)
        bqT = arn(6288, 1024).rearrange("p (k s) -> p k s", k=4)
        iqT = arn(7312, 1024).rearrange("p (k s) -> p k s", k=4)
        akT = arn(8336, 256)
        bkT = arn(8592, 256)
        ikT = arn(8848, 256)
        OTa, OTb = ([arn_r(a, 1024).rearrange("p (k s) -> p k s", k=4) for a in at]
                    for at in ((9104, 2448), (4240, 7312)))
        OTc = [arn_r(a, 2048).rearrange("p (k s) -> p k s", k=KC) for a in (0, 2048)]
        lng = arn(5264, D)
        lnb = arn(6288, D)
        hid = [arn_r(a, 1024).rearrange("p (k s) -> p k s", k=4) for a in (0, 1024)]
        relu_h, sq_h = (arn(a, 1024).rearrange("p (k s) -> p k s", k=4) for a in (2048, 3072))

        def OTab(g):
            return [x[:, 2 * (g % 2):2 * (g % 2) + 2, :] for x in (OTa, OTb)[g // 2]]

        def OTcc(g):
            return [x[:, 2 * g:2 * g + 2, :] for x in OTc]

        IX_BANKS = (6, 7, 4, 5)
        XTL = {a: arn_r(4096 if a == 0 else 8192, 2048).rearrange("p (k s) -> p k s", k=KC) for a in range(4)}

        XNf = XN[:].rearrange("p t d -> p (t d)")
        XTf = XT[:].rearrange("p k s -> p (k s)")
        SC = XNf[:, 0:1536].rearrange("p (h n) -> p h n", h=4)
        idx = XNf[:, 1536:1920]
        PT = XTf[:, 0:1536].rearrange("p (h n) -> p h n", h=4)
        bmask = XTf[:, 1536:1920]
        relu_i = R1b[:, 0:768].rearrange("p (i n) -> p i n", i=2)
        left = R1b[:, 768:1152]

        used = sem("granules_used")
        landed = [sem(f"slot{s}_landed") for s in range(SLOTS)]

        def kview(a, k):
            return a.rearrange("(k p) n -> p k n", p=P)

        W2 = {n: kview(A[n][0], KC) for n in ("w_k", "w_v", "w_in", "w_out", "w_q", "w_o", "ab_w_in_2",
                                              "ab_w_out_2", "c_w_in_2", "c_w_out_2")}

        def granule_source(name, i, s):
            if name in ("w_k", "w_v", "w_out", "w_q", "w_o"):
                return [(slot(s).rearrange("p (k n) -> p k n", k=4), W2[name][:, 4 * i:4 * i + 4, :])]
            if name == "w_in":
                return [(slot(s).rearrange("p (k n) -> p k n", k=2), W2[name][:, 2 * i:2 * i + 2, :])]
            if name == "ada":
                a, nb = i // 6, i % 6
                src = A["ada_w_2"][a // 2, a % 2].rearrange("(k p) n -> p k n", p=P)
                return [(slot(s).rearrange("p (k n) -> p k n", k=8), src[:, :, HW * nb:HW * nb + HW])]
            if name == "ab_in":
                k = min(3, KC - 3 * i)
                return [(slot(s, k * 1224).rearrange("p (k n) -> p k n", k=k), W2["ab_w_in_2"][:, 3 * i:3 * i + k, :])]
            if name == "uq":
                return [(slot(s)[:, j * 1024:(j + 1) * 1024].rearrange("p (k n) -> p k n", k=2),
                         kview(A[w][0], 2)) for j, w in enumerate(("ab_w_uq_2", "ab_w_uiq_2"))]
            if name in ("ab_out", "c_out"):
                w = W2["ab_w_out_2" if name == "ab_out" else "c_w_out_2"]
                return [(slot(s).rearrange("p (k n) -> p k n", k=4), w[:, 4 * i:4 * i + 4, :])]
            assert name == "c_in"
            return [(slot(s).rearrange("p (k n) -> p k n", k=4),
                     W2["c_w_in_2"][:, 4 * (i % 2):4 * (i % 2) + 4, D * (i // 2):D * (i // 2) + D])]

        block = ctx.enter_context(nc.Block())

        def granule_no(name, i):
            return MOE_END + POST.index((name, i))

        def width(name, i):
            return SLOT if name != "ab_in" else min(3, KC - 3 * i) * 1224

        def rope_on(eng, link, out, x, tmp, t, st):
            nd = len(out.shape) - 2

            def cs_(tile, a, b):
                v = tile[:, t, a:b]
                for _ in range(nd):
                    v = v[:, None]
                return v.to_broadcast(tuple(out.shape[:-1]) + (b - a,))

            def half(v, a, b):
                return v[:, :, :, a:b] if nd == 2 else v[:, :, a:b]

            eng.tensor_tensor(out, x, cs_(ropeC, 0, HD), ALU.mult)
            eng.tensor_tensor(half(tmp, 0, 32), half(x, 32, 64), cs_(ropeS, 0, 32), ALU.mult)
            link(eng.tensor_tensor(half(tmp, 32, 64), half(x, 0, 32), cs_(ropeS, 32, 64), ALU.mult))
            ins = eng.tensor_tensor(out, out, tmp, ALU.add)
            if st is None:
                link(ins)
            else:
                ins.then_inc(sem(st), 1)

        def half_no(name, h):
            return 2 * SPLIT.index((name, 0)) + h + 1

        def half_raw(name, h):
            g = PRE.index((name, h // 2))
            return g, slot(slot_of(g))[:, (h % 2) * SLOT // 2:(h % 2 + 1) * SLOT // 2]

        def half_hi(act, name, *hs):
            for h in hs:
                n = half_no(name, h)
                g, raw = half_raw(name, h)
                act.wait_ge(landed[slot_of(g)], FILL[g])
                if n > 2:
                    if n % 2:
                        act.wait_ge(sem("half_used"), (n - 1) // 2)
                    else:
                        act.wait_ge(*done(*SPLIT[(n - 3) // 2]))
                act.activation(halves[(n - 1) % 2][0][:], raw, ACT.Copy).then_inc(sem("w_hi"), 1)

        def half_lo(eng, name, *hs):
            for h in hs:
                n = half_no(name, h)
                hi, lo = halves[(n - 1) % 2]
                eng.wait_ge(sem("w_hi"), n)
                if n > 1:
                    eng.wait_ge(sem("w_lo"), n - 1)
                eng.tensor_tensor(lo[:], half_raw(name, h)[1], hi[:].bitcast(F32), ALU.subtract).then_inc(
                    sem("w_lo"), 1)

        def split_hi(act, name, i, it=None):
            g = granule_no(name, i)
            n = split_no(g)
            step = 0 if it is None else it * R2
            act.wait_ge(landed[slot_of(g)], (0 if it is None else it * 16) + FILL[g])
            if n > 2 * len(SPLIT) + 2:
                before = g - 2 - (g - 2 <= MOE_END + UQ <= g)
                act.wait_ge(used, step + (before + 1))
            else:
                act.wait_ge(used, MOE_END)
            w = width(name, i)
            act.activation(pair(n)[0][:, 0:w], slot(slot_of(g), w), ACT.Copy).then_inc(sem("w_hi"), 1)

        def split_lo(eng, name, i, it=None):
            n = split_no(granule_no(name, i))
            step = 0 if it is None else it * R2
            hi, lo = pair(n)
            w = width(name, i)
            eng.wait_ge(sem("w_hi"), step + n)
            eng.wait_ge(sem("w_lo"), step + (n - 1))
            eng.tensor_tensor(lo[:, 0:w], slot(slot_of(granule_no(name, i)), w), hi[:, 0:w].bitcast(F32),
                              ALU.subtract).then_inc(sem("w_lo"), 1)

        @block.sync
        def _(sp):
            sp.dma_start(MEM, A["mem"][0].rearrange("(t p) d -> p t d", p=P)).then_inc(sem("mem_landed"), 16)
            sp.dma_start(tab[:], tab_d).then_inc(sem("tab_landed"), 16)

            def vec_rows(name, ap):
                n = ap.shape[0]
                sp.dma_start(vec[VEC[name]:VEC[name] + n, 0, :], ap).then_inc(sem("vec_landed"), 16)

            def rows(ap):
                return ap.rearrange("(k p) -> k p", p=P)

            for n in ("norm_mem", "norm_mix", "norm_xattn", "norm_ffn", "g_conv_out", "g_fft_out", "ab_q_norm_2"):
                vec_rows(n, rows(A[n][0]))
            vec_rows("conv_w", A["conv_w"][0].rearrange("t (k p) -> (t k) p", p=P))
            vec_rows("c_2", rows(A["c_2"][0]))
            vec_rows("norm_final", rows(A["norm_final"]))
            for n in ("ln_g_2", "ln_b_2"):
                vec_rows(n, A[n].rearrange("a b (k p) -> (a b k) p", p=P)[0:24])
            sp.dma_start(vec[0:NADA * 24, 1, :], A["ada_b_2"].rearrange("a b (k p) -> (a b k) p", p=P)).then_inc(
                sem("vec_landed"), 16)
            sp.dma_start(X[:], A["x"][0].rearrange("(t p) d -> p t d", p=P)).then_inc(sem("x_landed"), 16)

            def fill(g, name, i):
                o = OWNER[g]
                if o is not None and PRE[o] in SPLIT:
                    sp.wait_ge(sem("w_hi"), half_no(PRE[o][0], 2 * PRE[o][1] + 1))
                    sp.wait_ge(sem("w_lo"), half_no(PRE[o][0], 2 * PRE[o][1] + 1))
                elif o is not None:
                    sp.wait_ge(used, o + 1)
                for dst, src in granule_source(name, i, slot_of(g)):
                    sp.dma_start(dst, src).then_inc(landed[slot_of(g)], 16)

            for g, (name, i) in enumerate(PRE):
                fill(g, name, i)
                if g == 3:
                    sp.dma_start(wr[:], kview(A["w_router"][0], KC)).then_inc(sem("router_landed"), 16)
                    sp.dma_start(brow[:], A["b_router"][0:1, :].to_broadcast((P, NE))).then_inc(sem("router_landed"), 16)
                    for t in range(TB):
                        sp.dma_start(posi[:, t:t + 1], A["positions_2"][0, t * P:(t + 1) * P, None]).then_inc(
                            sem("pos_landed"), 16)
                    sp.dma_start(sinkb, A["ab_sinks_2"][0:1, :].to_broadcast((P, 8))).then_inc(sem("sink_landed"), 16)
                    sp.dma_start(dft, dft_d.rearrange("(t p) n -> p t n", p=P)).then_inc(sem("dft_landed"), 16)

            def expert_slot(j):
                return slot_of(NPRE + j)

            def expert_source(j, e):
                if j < 4:
                    return A["w_gate_up"][0, bass.ds(e, 1), 2 * P * j:2 * P * (j + 1), :].rearrange(
                        "e (k p) n -> p (e k) n", p=P)
                return A["w_down"][0, bass.ds(e, 1), 4 * P * (j - 4):4 * P * (j - 3), :].rearrange(
                    "e (k p) n -> p (e k) n", p=P)

            for j in range(PER_E):
                if OWNER[NPRE + j] is None:
                    sp.wait_ge(used, PRE.index(("w_o", 1)) + 1)
                else:
                    sp.wait_ge(used, OWNER[NPRE + j] + 1)
                s = expert_slot(j)
                sp.dma_start(slot(s).rearrange("p (k n) -> p k n", k=2 if j < 4 else 4),
                             expert_source(j, 0)).then_inc(landed[s], 16)
            with sp.Fori(1, NE) as e:
                for j in range(PER_E):
                    s = expert_slot(j)
                    sp.wait_ge(used, e * PER_E + (NPRE + j + 1 - PER_E))
                    sp.dma_start(slot(s).rearrange("p (k n) -> p k n", k=2 if j < 4 else 4),
                                 expert_source(j, e)).then_inc(landed[s], 16)

            sp.wait_ge(sem("table_ready"), 1)
            n = nc.values_load(table_i[0:1, 32:33], engines=[ENG.SP], min_val=0, max_val=NX_MAX)
            with sp.If(n > 0):
                sp.wait_ge(used, MOE_END)
                with sp.Fori(0, n) as i:
                    e = nc.values_load(table_i[0:1, bass.ds(i, 1)], engines=[ENG.SP], min_val=0, max_val=NE - 1)
                    sp.wait_ge(sem("extra_used"), i + 1)
                    for j in range(PER_E):
                        sp.dma_start(slot(expert_slot(j)).rearrange("p (k n) -> p k n", k=2 if j < 4 else 4),
                                     expert_source(j, e)).then_inc(sem("extra_landed"), 16)
                sp.wait_ge(sem("moe_x"), 1)

            g = MOE_END
            for name, count in (("ab_in", 3), ("uq", 1), ("ab_out", 2), ("mlp0", 16), ("c_in", 6), ("c_out", 2),
                                ("mlp1", 16)):
                if name[:3] != "mlp":
                    for i in range(count):
                        o = OWNER[g]
                        if o is None:
                            sp.wait_ge(used, NPRE)
                        elif o < MOE_END:
                            sp.wait_ge(used, o + 1)
                        else:
                            sp.wait_ge(sem("w_hi"), split_no(o))
                            sp.wait_ge(sem("w_lo"), split_no(o))
                        for dst, src in granule_source(name, i, slot_of(g)):
                            sp.dma_start(dst, src).then_inc(landed[slot_of(g)], 16)
                        g += 1
                    continue
                if name == "mlp0":
                    sp.wait_ge(*done("uq", 0))
                l = int(name[3])
                w1 = A["mlp_w1_2"][l].rearrange("(k p) n -> p k n", p=P)
                w2 = A["mlp_w2_2"][l].rearrange("(k p) n -> p k n", p=P)
                with sp.Fori(0, 4) as i:
                    for j in range(R2):
                        s = slot_of(g + j)
                        n = split_no(g + j) - R2
                        sp.wait_ge(sem("w_hi"), i * R2 + n)
                        sp.wait_ge(sem("w_lo"), i * R2 + n)
                        if j % 2 == 0:
                            src = w1[:, :, bass.ds(i * (2 * HW) + (j // 2) * HW, HW)]
                            dst = slot(s).rearrange("p (k n) -> p k n", k=8)
                        else:
                            src = w2[:, bass.ds(i * 8 + (j // 2) * 4, 4), :]
                            dst = slot(s).rearrange("p (k n) -> p k n", k=4)
                        sp.dma_start(dst, src).then_inc(landed[s], 16)
                g += 16
            for t in range(TB):
                sp.wait_ge(*upto("ln3", "ln_x", t + 1))
                sp.dma_start(out_d[0, t * P:(t + 1) * P, :], X[:, t, :]).then_inc(sem("stored"), 16)
            sp.wait_ge(sem("stored"), 16 * TB)

        @block.gpsimd
        def _(pool):
            half_lo(pool, "w_in", 0, 1)
            pool.wait_ge(*done("w_v", 1))
            pool.memset(GP[:, :, 0:1], 0.0).then_inc(sem("conv_pad"), 1)
            pool.memset(GP[:, :, S + 1:S + 2], 0.0).then_inc(sem("conv_pad"), 1)
            for w in ("w_q", "w_o"):
                half_lo(pool, w, 0, 1)
            pool.wait_ge(sem("wo_x"), 4)
            pool.memset(bias, 0.0).then_inc(sem("moe_zero"), 1)
            pool.memset(ysb, 0.0).then_inc(sem("e_y"), 1)
            pool.memset(arn(7040, 512), 0.0).then_inc(sem("moe_zero"), 1)
            pool.memset(stat[:, 127:128], 0.0).then_inc(sem("extra_used"), 1)

            def cols(name, n):
                return col[:, VEC[name]:VEC[name] + 8 * n].rearrange("p (a k) -> p a k", k=8)

            part = stat[:, 24:48].rearrange("p (a k) -> p a k", k=8)
            pool.wait_ge(sem("ada_done"), ADA_UNITS)
            pool.wait_ge(sem("col_ready"), 2)
            pool.tensor_tensor(part, mod[:, 1:4, 8:16], cols("ln_b_2", 3), ALU.mult).then_inc(sem("mod_g"), 1)
            pool.wait_ge(sem("mod_g"), 1)
            pool.tensor_tensor(mod[:, 1:4, 0:8], mod[:, 1:4, 0:8], part, ALU.add).then_inc(sem("mod_g"), 1)
            pool.tensor_tensor(mod[:, 1:4, 8:16], mod[:, 1:4, 8:16], cols("ln_g_2", 3), ALU.mult).then_inc(sem("mod_g"), 1)
            pool.tensor_tensor(mod[:, 0:1, 8:16], mod[:, 0:1, 8:16], cols("norm_final", 1), ALU.mult).then_inc(
                sem("mod_g"), 1)

            def w_lo(name, i):
                split_lo(pool, name, i)

            def affine(st, t):
                steps = [(nfin, ALU.mult)] if st == "fin" else [(lng, ALU.mult), (lnb, ALU.add)]
                for n, (row, op) in enumerate(steps):
                    ins = pool.tensor_tensor(X[:, t, :], X[:, t, :], row, op)
                    if n + 1 < len(steps):
                        ins.then_inc(sem("pool_step"), 1)
                        pool_steps[0] += 1
                        pool.wait_ge(sem("pool_step"), pool_steps[0])
                ins.then_inc(sem("ln_x"), 1)

            pool_steps = [0]
            w_lo("ab_in", 0)
            pool.wait_ge(sem("nfin_landed"), 16)
            pool.wait_ge(*upto("m0", "T", 4))
            for t in range(TB):
                affine("fin", t)

            def link(ins):
                pool_steps[0] += 1
                ins.then_inc(sem("pool_step"), 1)
                pool.wait_ge(sem("pool_step"), pool_steps[0])

            tmp_g = XTf[:, 1024:1536]
            R1a = R1b.rearrange("p (t n) -> p t n", t=TB)
            pool.wait_ge(sem("z0"), 3)
            pool.wait_ge(sem("z1"), 3)
            pool.wait_ge(sem("rope_tables"), 1)
            for t in range(TB):
                out = R1a[:, t, 0:512].rearrange("p (j g d) -> p j g d", j=4, g=2)
                rope_on(pool, link, out, Z[:, t, 0:512].rearrange("p (g j d) -> p j g d", j=4, g=2),
                     tmp_g[:, 0:512].rearrange("p (j g d) -> p j g d", j=4, g=2), t, "a_rope")
                pool.wait_ge(sem("a_rope"), t + 1)
            w_lo("ab_out", 0)
            w_lo("ab_out", 1)
            for l, after in enumerate(("mlp0", "c_in", "mlp1")):
                w_lo(after, 0)
                pool.wait_ge(*upto(f"m{l + 1}", "T", 4))
                pool.wait_ge(*upto(f"ln{l}", "ln_landed", 32))
                for t in range(TB):
                    affine(f"ln{l}", t)
                if after == "c_in":
                    w_lo("c_out", 0)
                    w_lo("c_out", 1)

        @block.scalar
        def _(act):
            def norm_stats(st, src, junk, at, ready, late=None):
                if late is not None:
                    act.activation(stat[:, late:late + 1], eps5, ACT.Sqrt, bias=zero)
                for t in range(TB):
                    act.wait_ge(ready[0], ready[1] if late is None else ready[1] // TB * (t + 1))
                    act.activation(junk[:, t, :], src[:, t, :], ACT.Square, bias=zero,
                                   accum_out=stat[:, at + t:at + t + 1]).then_inc(sem("sq"), 1)
                act.wait_ge(*upto(st, "sq", TB))
                act.activation(stat[:, at + 2:at + 4], stat[:, at:at + 2], ACT.Sqrt, bias=eps5,
                               scale=1.0 / D).then_inc(sem("root"), 1)

            def evac_split(st, base, x, g1):
                for q in range(4):
                    act.wait_ge(*upto(st, "T", q + 1))
                    for r in range(2):
                        k = 2 * q + r
                        act.activation(x[0][:, k, :], B[base + q][:, r * S:(r + 1) * S], ACT.Copy,
                                       scale=g1(k)).then_inc(sem("xt_a"), 1)

            def evac_T(st, base, XTo, g1):
                for n, q in enumerate((0, 2)):
                    act.wait_ge(*upto(st, "T", q + 1))
                    for r in range(2):
                        k = 2 * q + r
                        src = B[base + q][:, r * S:(r + 1) * S]
                        act.activation(XTo[:, k, :], src, ACT.Copy, scale=g1(k)).then_inc(sem("xt_a"), 1)

            unit = [0]

            def ada(n):
                for _ in range(n):
                    u = unit[0]
                    unit[0] += 1
                    act.wait_ge(*done("ada", u))
                    if u >= 2:
                        act.wait_ge(sem("ada_comb"), u - 1)
                    act.activation(ada_part[:, u % 2, :], B[6][:], ACT.Copy).then_inc(sem("ada_part"), 1)

            def gain(name):
                return lambda k: col[:, VEC[name] + k:VEC[name] + k + 1]

            act.wait_ge(sem("tab_landed"), 16)
            norm_stats("mem", MEM, MEMN, 0, (sem("mem_landed"), 16))
            norm_stats("mix", X, XN, 4, (sem("x_landed"), 16))
            act.wait_ge(sem("vecT"), 1)
            act.activation(col[:], B[4][:, 0:NVEC], ACT.Copy).then_inc(sem("col_ready"), 1)
            act.activation(ada_bT[:], B[4][:, 128:128 + NADA * 24], ACT.Copy).then_inc(sem("col_ready"), 1)
            act.wait_ge(sem("col_ready"), 2)
            act.activation(sil[:, 0, :], col[:, VEC["c_2"]:VEC["c_2"] + 8], ACT.Sigmoid,
                           bias=zero).then_inc(sem("c_sig"), 1)
            evac_split("mem", 0, MEMT, gain("norm_mem"))
            half_hi(act, "w_k", 0, 1, 2, 3)
            half_hi(act, "w_v", 0, 1)
            act.wait_ge(*done("w_k", 1))
            for i in range(4):
                act.activation(KT[:, 2 * i:2 * i + 2, :], B[4 + i][:].rearrange("p (k s) -> p k s", k=2),
                               ACT.Copy).then_inc(sem("kT"), 1)
            half_hi(act, "w_v", 2, 3)
            half_hi(act, "w_in", 0)
            evac_split("mix", 4, XTmix, gain("norm_mix"))
            half_hi(act, "w_in", *range(1, 8))
            act.wait_ge(*done("w_in", 3))
            for i in range(2):
                act.activation(CT[:, i * HW:(i + 1) * HW], B[2 + i][:], ACT.Copy).then_inc(sem("mix_c"), 1)
            for t in range(TB):
                act.activation(U[:, t, :], B[6 + t][:], ACT.Copy).then_inc(sem("mix_u"), 1)
            ada(5)
            act.wait_ge(sem("fft_seq"), 1)
            for i, b in enumerate((2, 3, 4, 5)):
                act.activation(FT[:, i, :], B[b][:], ACT.Copy).then_inc(sem("fft_ev"), 1)
            ada(3)
            act.wait_ge(sem("conv_y"), 2)
            act.activation(SQ[:, 0:4, :], YT[:, 0:4, :], ACT.Square, bias=zero).then_inc(sem("mix_sq"), 1)
            ada(2)
            act.wait_ge(sem("fft_y"), 2)
            act.activation(SQ[:, 4:8, :], YT[:, 4:8, :], ACT.Square, bias=zero).then_inc(sem("mix_sq"), 1)
            act.wait_ge(sem("mix_ss"), 1)
            act.activation(RMS[:, 0:2, :], B[4][:].rearrange("p (k s) -> p k s", k=2), ACT.Sqrt, bias=eps5,
                           scale=1.0 / 512).then_inc(sem("mix_rms"), 1)
            ada(2)
            for m in range(2):
                act.wait_ge(sem("mix_yn"), 4 * m + 4)
                act.activation(YTs[0][:, 4 * m:4 * m + 4, :], YT[:, 4 * m:4 * m + 4, :], ACT.Copy).then_inc(sem("op_hi"), 1)
            half_hi(act, "w_out", 0, 1, 2, 3)
            norm_stats("xa", X, XN, 8, (sem("wout_x"), 4), 57)
            half_hi(act, "w_q", 0, 1)
            ada(2)
            evac_split("xa", 0, XTxa, gain("norm_xattn"))
            half_hi(act, "w_q", 2, 3)
            act.wait_ge(*done("w_q", 1))
            for i in range(4):
                act.activation(QT[:, 2 * i:2 * i + 2, :], B[i][:].rearrange("p (k s) -> p k s", k=2), ACT.Copy).then_inc(sem("qT"), 1)
            ada(1)
            for h in range(4):
                act.wait_ge(sem("xa_nm"), h + 1)
                for t in range(TB):
                    act.activation(PR[:, h, t, :], B[h][:, t * S:(t + 1) * S], ACT.Exp, scale=1.0 / 16,
                                   bias=att[:, 0, 2 * h + t:2 * h + t + 1],
                                   accum_out=att[:, 1, 2 * h + t:2 * h + t + 1]).then_inc(sem("xa_e"), 1)
            ada(3)
            half_hi(act, "w_o", 0, 1)
            for h in range(4):
                act.wait_ge(sem("xa_pt"), h + 1)
                act.activation(PRT[:, h, :, :], B[h][:].rearrange("p (m s) -> p m s", m=2), ACT.Copy).then_inc(
                    sem("xa_pte"), 1)
            for h in range(4):
                act.wait_ge(sem("xa_o"), h + 1)
                act.activation(OTx[0][:, 2 * h:2 * h + 2, :], B[(4, 5, 0, 1)[h]][:].rearrange(
                    "p (m s) -> p m s", m=2), ACT.Copy).then_inc(sem("op_hi"), 1)
            half_hi(act, "w_o", 2, 3)
            norm_stats("ffn", X, XN, 12, (sem("wo_x"), 4), 58)
            ada(2)
            evac_T("ffn", 0, XT, gain("norm_ffn"))
            act.wait_ge(sem("moe_zero"), 1)
            act.dma_start(bias[0:NE, 0:2 * D], A["b_gate_up"][0]).then_inc(sem("bias_landed"), 16)
            act.dma_start(bias[0:NE, 2 * D:3 * D], A["b_down"][0]).then_inc(sem("bias_landed"), 16)
            act.dma_start(nfin, A["norm_final"][None, :].to_broadcast((P, D))).then_inc(sem("nfin_landed"), 16)
            act.wait_ge(sem("rt_nm"), TB)
            for t in range(TB):
                act.activation(rt[:, t, 0:NE], logit[:, t, 0:NE], ACT.Exp,
                               bias=att[:, 2, t:t + 1]).then_inc(sem("rt_e"), 1)
            ada(4)

            def expert(i, down_done):
                act.wait_ge(sem("e_clamp"), 2 * i + 1)
                act.activation(sig, gcl, ACT.Sigmoid, bias=zero, scale=1.702).then_inc(sem("e_sig"), 1)
                act.wait_ge(sem("e_wT"), i + 1)
                act.activation(wselT[0:CAP, 0], B[2][0:CAP, 0:TB * P].rearrange("p (t n) -> p t n", t=TB),
                               ACT.Copy).then_inc(sem("e_wTe"), 1)
                act.activation(wselT[CAP:P, 1], B[2][CAP:P, 0:TB * P].rearrange("p (t n) -> p t n", t=TB),
                               ACT.Copy).then_inc(sem("e_wTe"), 1)
                act.wait_ge(sem("e_hT"), i + 1)
                act.activation(hT, B[3][:].rearrange("p (c n) -> p c n", c=4), ACT.Copy).then_inc(sem("e_hTe"), 1)
                act.wait_ge(*down_done)
                act.activation(ysb, B[2][:], ACT.Copy).then_inc(sem("e_y"), 1)

            with act.Fori(0, NE) as i:
                expert(i, (used, i * PER_E + (NPRE + PER_E)))
            act.wait_ge(sem("table_ready"), 1)
            n = nc.values_load(table_i[0:1, 32:33], engines=[ENG.Activation], min_val=0, max_val=NX_MAX)
            with act.If(n > 0):
                with act.Fori(0, n) as i:
                    expert(i + NE, (sem("x_down"), i + 1))

            split_hi(act, "ab_in", 0)
            norm_stats("fin", X, XN, 16, (sem("moe_x"), 4), 59)

            def modcol(a):
                return (lambda k: mod[:, a, 8 + k:9 + k]), (lambda k: mod[:, a, k:k + 1])

            def load_ln(l, ready):
                act.wait_ge(*ready)
                act.dma_start(lng, A["ln_g_2"][l // 2, l % 2, None, :].to_broadcast((P, D))).then_inc(sem("ln_landed"), 16)
                act.dma_start(lnb, A["ln_b_2"][l // 2, l % 2, None, :].to_broadcast((P, D))).then_inc(sem("ln_landed"), 16)

            def gate_rows(l):
                act.wait_ge(*upto(f"ln{l}", "gate_mm", 1))
                for h in range(2):
                    act.activation(XN[:, 1, h * HW:(h + 1) * HW], B[6 + h][:], ACT.Copy).then_inc(sem("gate"), 1)

            def ln_root(l, t):
                act.wait_ge(*upto(f"ln{l}", "ln_var", t + 1))
                act.activation(att[:, 5, 4 + t:5 + t], att[:, 5, 2 * t + 1:2 * t + 2], ACT.Sqrt,
                               bias=eps5).then_inc(sem("ln_root"), 1)

            def evac_hi(a):
                g1, g0 = modcol(a)
                act.wait_ge(sem("mod_g"), 4)
                for q in range(4):
                    act.wait_ge(*upto(f"m{a}", "T", q + 1))
                    for r in range(2):
                        k = 2 * q + r
                        act.activation(XT_r[:, k, :], B[4 + q][:, r * S:(r + 1) * S], ACT.Identity, scale=g1(k),
                                       bias=g0(k)).then_inc(sem("xt_a"), 1)

            def mlp_group(l, it, last):
                n = f"mlp{l}"
                for p in range(2):
                    for b in range(2):
                        c = 2 * p + b + 1
                        if b == 0:
                            act.wait_ge(*upto(n, "mlp_h", it * 2 + (p + 1)))
                        else:
                            act.wait_ge(used, it * R2 + done(n, 2 * p)[1])
                        act.activation(relu_h[:, 2 * b:2 * b + 2, :], B[4 + b][:].rearrange("p (k s) -> p k s", k=2),
                                       ACT.Relu, bias=zero).then_inc(sem("mlp_relu"), 1)
                        act.wait_ge(*upto(n, "mlp_relu", it * 4 + c))
                        act.activation(hid[0][:, 2 * b:2 * b + 2, :], relu_h[:, 2 * b:2 * b + 2, :], ACT.Square,
                                       bias=zero).then_inc(sem("mlp_sq"), 1)
                    if not (last and p == 1):
                        split_hi(act, n, 2 * p + 2, it)
                        split_hi(act, n, 2 * p + 3, it)

            def exps(st, u):
                act.wait_ge(*upto(st, "nm", u + 1))
                c = 4 * (u % 2)
                for h in range(2):
                    for t, (a, b) in enumerate(((0, P), (P, 3 * P))):
                        i = c + 2 * t + h
                        sc = SC[:, 2 * (u % 2) + h, a:b]
                        act.activation(sc, sc, ACT.Exp, bias=att[:, 1, i:i + 1],
                                       accum_out=att[:, 2, i:i + 1]).then_inc(sem("e"), 1)
                if u < ATTNS[st][1]:
                    act.activation(att[:, 4, c:c + 4], att[:, 3, c:c + 4], ACT.Exp, bias=zero).then_inc(sem("e"), 1)

            def attend(st, ot):
                units = ATTNS[st][0]

                def outputs(g):
                    act.wait_ge(*upto(st, "o", g + 1))
                    act.activation(ot(g)[0], B[6 + g % 2][:].rearrange("p (m s) -> p m s", m=2),
                                   ACT.Copy).then_inc(sem("ot"), 1)

                for u in range(units):
                    for h in range(2):
                        n = 2 * u + h
                        act.wait_ge(*upto(st, "pt", n + 1))
                        act.activation(PT[:, n % 4, :], B[4 + h][:, 0:3 * P], ACT.Copy).then_inc(sem("pte"), 1)
                    if u >= 2 and u % 2 == 0:
                        outputs(u // 2 - 1)
                    if u + 2 < units:
                        exps(st, u + 2)
                outputs(units // 2 - 1)

            evac_hi(0)
            split_hi(act, "ab_in", 1)
            act.wait_ge(sem("rope_ang"), 1)
            act.activation(ropeS[:, :, 32:64], ropeS[:, :, 32:64], ACT.Sin, bias=zero).then_inc(sem("rope_sc"), 1)
            act.activation(ropeC[:, :, 0:32], ropeC[:, :, 0:32], ACT.Sin, bias=tb_("halfpi"),
                           scale=-1.0).then_inc(sem("rope_sc"), 1)
            split_hi(act, "ab_in", 2)
            act.wait_ge(*done("ab_in", 2))
            for c in range(3):
                act.activation(Z[:, 0, 408 * c:408 * c + 408], B[c][:, 0:408], ACT.Copy).then_inc(sem("z0"), 1)
            act.wait_ge(sem("z0"), 3)
            act.wait_ge(sem("z1"), 3)
            for t in range(TB):
                act.activation(XN[:, t, 0:256], Z[:, t, 768:1024], ACT.Square, bias=zero,
                               accum_out=stat[:, 20 + t:21 + t]).then_inc(sem("cq_sq"), 1)
            act.wait_ge(sem("cq_sq"), TB)
            act.activation(stat[:, 22:24], stat[:, 20:22], ACT.Sqrt, bias=eps6, scale=1.0 / 256).then_inc(sem("cq_root"), 1)
            split_hi(act, "ab_out", 0)
            split_hi(act, "ab_out", 1)
            act.wait_ge(*upto("fin", "ln_x", 2))
            act.wait_ge(sem("a_T"), 1)
            act.activation(aqT[:, 0:2, :], B[6][:].rearrange("p (m s) -> p m s", m=2), ACT.Copy).then_inc(sem("a_Te"), 1)
            act.activation(aqT[:, 2:4, :], B[7][:].rearrange("p (m s) -> p m s", m=2), ACT.Copy).then_inc(sem("a_Te"), 1)
            act.wait_ge(sem("k_T"), 1)
            act.activation(akT, B[4][:, 0:S], ACT.Copy).then_inc(sem("k_Te"), 1)
            act.activation(bkT, B[4][:, S:2 * S], ACT.Copy).then_inc(sem("k_Te"), 1)
            act.activation(ikT, B[5][:, 0:S], ACT.Copy).then_inc(sem("k_Te"), 1)
            act.wait_ge(sem("i_T"), 1)
            act.activation(iqT[:, 0:2, :], B[6][:].rearrange("p (m s) -> p m s", m=2), ACT.Copy).then_inc(sem("i_Te"), 1)
            act.activation(iqT[:, 2:4, :], B[7][:].rearrange("p (m s) -> p m s", m=2), ACT.Copy).then_inc(sem("i_Te"), 1)
            act.wait_ge(sem("b_T"), 1)
            act.activation(bqT[:, 0:2, :], B[4][:].rearrange("p (m s) -> p m s", m=2), ACT.Copy).then_inc(sem("b_Te"), 1)
            act.activation(bqT[:, 2:4, :], B[5][:].rearrange("p (m s) -> p m s", m=2), ACT.Copy).then_inc(sem("b_Te"), 1)
            for h in range(8):
                act.wait_ge(sem("ix_mm"), h + 1)
                if h >= 2:
                    act.wait_ge(sem("ix_acc"), 2 * (h - 1))
                act.activation(relu_i[:, h % 2, :], B[IX_BANKS[h % 4]][:, 0:3 * P], ACT.Relu,
                               bias=zero).then_inc(sem("ix_relu"), 1)
            exps("ab", 0)
            exps("ab", 1)
            attend("ab", OTab)
            gate_rows(0)
            load_ln(0, upto("ab", "o", 4))
            split_hi(act, "mlp0", 0)
            ln_root(0, 0)
            split_hi(act, "mlp0", 1)
            ln_root(0, 1)
            evac_hi(1)
            with act.Fori(0, 3) as it:
                mlp_group(0, it, False)
            gate_rows(1)
            load_ln(1, upto("ln0", "ln_x", 2))
            mlp_group(0, 3, True)
            split_hi(act, "c_in", 0)
            ln_root(1, 0)
            split_hi(act, "c_in", 1)
            ln_root(1, 1)
            evac_hi(2)
            for i in range(2, 6):
                split_hi(act, "c_in", i)
            act.wait_ge(*done("c_in", 5))
            for i in range(4):
                act.activation(arn(8192 + HW * i, HW), B[i][:], ACT.Copy).then_inc(sem("cv"), 1)
            act.wait_ge(*upto("ln1", "ln_x", 2))
            for m, dst in enumerate((arn(4096, 2048), arn(6144, 2048))):
                for i in range(4):
                    act.wait_ge(sem("c_T"), 4 * m + i + 1)
                    act.activation(dst[:, HW * i:HW * i + HW], B[4 + i][:], ACT.Copy).then_inc(sem("c_Te"), 1)
            split_hi(act, "c_out", 0)
            split_hi(act, "c_out", 1)
            exps("cc", 0)
            exps("cc", 1)
            attend("cc", OTcc)
            gate_rows(2)
            load_ln(2, upto("cc", "o", 4))
            split_hi(act, "mlp1", 0)
            ln_root(2, 0)
            split_hi(act, "mlp1", 1)
            ln_root(2, 1)
            evac_hi(3)
            with act.Fori(0, 3) as it:
                mlp_group(1, it, False)
            gate_rows(3)
            load_ln(3, upto("ln2", "ln_x", 2))
            mlp_group(1, 3, True)
            ln_root(3, 0)
            ln_root(3, 1)

        @block.tensor
        def _(pe):
            at = [0]

            def granule(w=SLOT):
                g = at[0]
                at[0] += 1
                pe.wait_ge(landed[slot_of(g)], FILL[g])
                return slot(slot_of(g), w)

            def transpose_x(st, base, src, ready):
                pe.wait_ge(*ready)
                for q in range(4):
                    for r in range(2):
                        for t in range(TB):
                            k = 2 * q + r
                            mm = pe.transpose(B[base + q][:, r * S + t * P:r * S + t * P + P],
                                              src[:, t, k * P:(k + 1) * P], ident)
                    mm.then_inc(sem("T"), 1)

            def xt_ready(st):
                pe.wait_ge(*upto(st, "xt_a", 4))
                pe.wait_ge(*upto(st, "xt_v", 4))

            def three(out, st, mv, start, stop):
                for a, b in ((0, 0), (0, 1), (1, 0)):
                    mm = pe.matmul(out, st[a], mv[b], start=start and a + b == 0, stop=stop and a == 1,
                                   skip_group_check=True)
                return mm

            def cut3(parts, k, a, b):
                if len(parts) == 4:
                    parts, k = parts[2 * (k // 4):2 * (k // 4) + 2], k % 4
                return [x[:, k, a:b] for x in parts]

            n_half = [0]

            def split_half(k):
                n_half[0] += 1
                pe.wait_ge(sem("w_lo"), n_half[0])
                return [x[:].rearrange("p (k n) -> p k n", k=k) for x in halves[(n_half[0] - 1) % 2]]

            def half_done(mm):
                mm.then_inc(*((sem("half_used"), 1) if n_half[0] % 2 else (used, 1)))
                at[0] += n_half[0] % 2 == 0

            def chunk_ready(st, k):
                pe.wait_ge(*upto(st, "xt_a", k + 1))
                pe.wait_ge(*upto(st, "xt_v", k + 1))

            def project_T(x, base, st=None):
                for k in range(KC):
                    w = split_half(2) if k % 2 == 0 else w
                    if st is not None:
                        chunk_ready(st, KC - 1 if st == "xa" else k)
                    for f in range(8):
                        mm = three(B[base + f // 2][:, (f % 2) * S:(f % 2) * S + S], cut3(w, k % 2, f * P, (f + 1) * P),
                                   cut3(x, k, 0, S), k == 0 and f % 2 == 0, k == KC - 1)
                    if k % 2 == 1:
                        half_done(mm)

            def project(x, base, ready=lambda k: None):
                for k in range(KC):
                    w = split_half(2) if k % 2 == 0 else w
                    ready(k)
                    for t in range(TB):
                        for h in range(2):
                            mm = three(B[base + 2 * t + h][:], cut3(x, k, t * P, (t + 1) * P),
                                       cut3(w, k % 2, h * HW, (h + 1) * HW), k == 0, k == KC - 1)
                    if k % 2 == 1:
                        half_done(mm)

            unit = [0]

            def ada(n):
                def combine(u):
                    pe.wait_ge(sem("ada_part"), u + 1)
                    if u:
                        pe.wait_ge(sem("ada_done"), u)
                    part = ada_part[:, u % 2, :]
                    for c in range(4):
                        mm = pe.matmul(B[7][:, c:c + 1], part[:, c * P:(c + 1) * P], quads[:, 0:1], start=True, stop=True)
                    mm.then_inc(sem("ada_comb"), 1)

                first = unit[0]
                for u in range(first, first + n):
                    w = granule().rearrange("p (k n) -> p k n", k=KC)
                    if u:
                        pe.wait_ge(sem("ada_part"), u)
                    for r in range(2):
                        for c in range(4):
                            mm = pe.matmul(B[6][32 * c:32 * c + 32, :], cs[:, 2 * c + r, :], w[:, 2 * c + r, :],
                                           start=(r == 0), stop=(r == 1))
                    mm.then_inc(used, 1)
                    if u > first:
                        combine(u - 1)
                combine(first + n - 1)
                unit[0] += n

            pe.wait_ge(sem("tab_landed"), 16)
            pe.wait_ge(sem("vec_landed"), 208)
            pe.transpose(B[4][:, 0:NVEC], vec[0:NVEC, 0, :], ident[0:NVEC, 0:NVEC])
            pe.transpose(B[4][:, P:P + NADA * 24], vec[0:NADA * 24, 1, :],
                         ident[0:NADA * 24, 0:NADA * 24]).then_inc(sem("vecT"), 1)
            transpose_x("mem", 0, MEMN, upto("mem", "xn", 2))
            pe.wait_ge(sem("col_ready"), 2)
            project_T(MEMT, 4, "mem")
            project(MEMT, 0)
            pe.wait_ge(sem("kT"), 4)
            transpose_x("mix", 4, XN, upto("mix", "xn", 2))
            pe.wait_ge(sem("v"), 4)
            for k in range(KC):
                w = split_half(1)
                chunk_ready("mix", k)
                for f in range(12):
                    if k == 0 and f == 8:
                        chunk_ready("mix", KC - 1)
                    three(B[f // 2][:, (f % 2) * S:(f % 2) * S + S], cut3(w, 0, f * P, (f + 1) * P),
                          cut3(XTmix, k, 0, S), k == 0 and f % 2 == 0, k == KC - 1)
                for t in range(TB):
                    mm = three(B[6 + t][:], cut3(XTmix, k, t * P, (t + 1) * P), cut3(w, 0, 1536, 2048), k == 0, k == KC - 1)
                half_done(mm)
            pe.wait_ge(sem("mix_u"), 2)
            pe.wait_ge(sem("cs"), 1)
            ada(5)
            pe.wait_ge(sem("dft_landed"), 16)
            pe.wait_ge(sem("mix_c"), 2)
            pe.wait_ge(sem("conv_g"), 2)
            for i, b in enumerate((2, 3, 4, 5)):
                for t in range(TB):
                    mm = pe.matmul(B[b][:], U[:, t, i * P:(i + 1) * P], dft[:, t, :], start=(t == 0), stop=(t == 1))
            mm.then_inc(sem("fft_seq"), 1)
            ada(3)
            pe.wait_ge(sem("fft_ev"), 4)
            for i in range(4):
                o = B[2 + i // 2][:, (i % 2) * S:(i % 2) * S + S]
                pe.matmul(o, tb_("cg"), FT[:, i, 0:S], start=True, stop=False)
                mm = pe.matmul(o, tb_("sg"), FT[:, i, S:2 * S], start=False, stop=True)
            mm.then_inc(sem("fft_grp"), 1)
            ada(2)
            for m in range(2):
                pe.wait_ge(sem("mix_sq"), m + 1)
                for i in range(4):
                    mm = pe.matmul(B[4][:, m * S:(m + 1) * S], ones, SQ[:, 4 * m + i, :], start=(i == 0), stop=(i == 3))
            mm.then_inc(sem("mix_ss"), 1)
            ada(2)
            project(YTs, 0, lambda k: pe.wait_ge(*upto("y", "op_lo", k // 4 + 1)))
            ada(2)
            transpose_x("xa", 0, XN, upto("xa", "xn", 2))
            project_T(XTxa, 0, "xa")
            ada(1)
            pe.wait_ge(sem("qT"), 4)
            for h in range(4):
                for t in range(TB):
                    for c in range(2):
                        mm = pe.matmul(B[h][:, t * S:(t + 1) * S], QT[:, 2 * h + c, t * P:(t + 1) * P],
                                       KT[:, 2 * h + c, :], start=(c == 0), stop=(c == 1))
                mm.then_inc(sem("xa_s"), 1)
            ada(3)
            for h in range(4):
                pe.wait_ge(sem("xa_p"), 2 * h + 2)
                for m in range(2):
                    for t in range(TB):
                        mm = pe.transpose(B[h][:, m * S + t * P:m * S + t * P + P], PR[:, h, t, m * P:(m + 1) * P], ident)
                mm.then_inc(sem("xa_pt"), 1)
            for h in range(4):
                pe.wait_ge(sem("xa_pte"), h + 1)
                for c in range(2):
                    for m in range(2):
                        mm = pe.matmul(B[(4, 5, 0, 1)[h]][:, c * S:(c + 1) * S],
                                       V[:, m, h * 2 * P + c * P:h * 2 * P + c * P + P], PRT[:, h, m, :],
                                       start=(m == 0), stop=(m == 1))
                mm.then_inc(sem("xa_o"), 1)
            pe.wait_ge(*upto("xo", "op_lo", 4))
            project(OTx, 0)
            ada(2)
            transpose_x("ffn", 0, XN, upto("ffn", "xn", 2))
            xt_ready("ffn")
            pe.wait_ge(sem("router_landed"), 32)
            for t in range(TB):
                for k in range(KC):
                    mm = pe.matmul(B[4][:, t * NE:(t + 1) * NE], XT[:, k, t * P:(t + 1) * P], wr[:, k, :],
                                   start=(k == 0), stop=(k == KC - 1))
            mm.then_inc(sem("logits"), 1)
            def gather():
                for k in range(KC):
                    for t in range(TB):
                        mm = pe.matmul(B[3][:, k * CAP:(k + 1) * CAP], XN[:, t, k * P:(k + 1) * P], sel_tok[:, t, :],
                                       start=(t == 0), stop=(t == 1))
                mm.then_inc(sem("e_gather"), 1)

            ada(1)
            mask = [rt[:, 4 + t, 0:NE] for t in range(TB)]
            pe.wait_ge(sem("rt_mask"), 4)
            pe.matmul(B[5][:, 0:NE], tri, mask[0], start=True, stop=True)
            pe.matmul(B[5][:, NE:2 * NE], tri, mask[1], start=True, stop=False)
            pe.matmul(B[5][:, NE:2 * NE], ones, mask[0], start=False, stop=True)
            for t in range(TB):
                mm = pe.matmul(B[5][0:NCAND, 64:65], mrep[:, t, :], ones[:, 0:1], start=(t == 0), stop=(t == 1))
            mm.then_inc(sem("rt_pos"), 1)
            ada(1)
            pe.wait_ge(sem("flag"), 1)
            pe.matmul(B[5][0:NCAND, 65:66], tri[0:NCAND, 0:NCAND], flag, start=True, stop=True).then_inc(sem("rank"), 1)
            ada(1)
            pe.wait_ge(sem("chosen"), 1)
            pe.matmul(B[5][0:1, 96:112], tb_("cand_e")[0:NCAND, :], chosen, start=True, stop=True)
            pe.matmul(B[5][0:1, 112:128], tb_("cand_q")[0:NCAND, :], chosen, start=True, stop=True)
            pe.matmul(B[5][0:1, 128:129], ones[0:NCAND, 0:1], flag, start=True, stop=True).then_inc(sem("table_mm"), 1)
            ada(1)
            pe.wait_ge(sem("e_sel"), 2)
            gather()
            assert at[0] == NPRE

            def bias_gu():
                for m in range(2):
                    for h in range(2):
                        pe.matmul(B[m][CAP * h:CAP * h + CAP, :], selG, bias[:, m * D + h * HW:m * D + (h + 1) * HW],
                                  start=True, stop=False)

            def gate_up(j):
                w = slot(slot_of(NPRE + j)).rearrange("p (k n) -> p k n", k=2)
                for kl in range(2):
                    for m in range(2):
                        for h in range(2):
                            mm = pe.matmul(B[m][CAP * h:CAP * h + CAP, :], xe[:, 2 * j + kl, :],
                                           w[:, kl, m * D + h * HW:m * D + (h + 1) * HW],
                                           start=False, stop=(j == 3 and kl == 1))
                return mm

            def weights_T():
                for t in range(TB):
                    mm = pe.transpose(B[2][:, t * P:(t + 1) * P], wsel[:, t, :], ident)
                mm.then_inc(sem("e_wT"), 1)

            def hidden_T():
                for c in range(4):
                    mm = pe.transpose(B[3][:, c * P:(c + 1) * P], hh_[:, c * P:(c + 1) * P], ident)
                mm.then_inc(sem("e_hT"), 1)

            def bias_d():
                for h in range(2):
                    pe.matmul(B[2][CAP * h:CAP * h + CAP, :], selD, bias[:, 2 * D + h * HW:2 * D + (h + 1) * HW],
                              start=True, stop=False)

            def down(j):
                w = slot(slot_of(NPRE + 4 + j)).rearrange("p (k n) -> p k n", k=4)
                for c in range(4):
                    for h in range(2):
                        mm = pe.matmul(B[2][CAP * h:CAP * h + CAP, :], hT[:, c, CAP * j:CAP * j + CAP],
                                       w[:, c, h * HW:(h + 1) * HW], start=False, stop=(j == 1 and c == 3))
                return mm

            def scatter():
                for t in range(TB):
                    for h in range(2):
                        mm = pe.matmul(B[4 + 2 * t + h][:], wselT[:, h, t, :], ysb, start=False, stop=False,
                                       skip_group_check=True)
                return mm

            pe.wait_ge(sem("moe_zero"), 2)
            pe.wait_ge(sem("bias_landed"), 32)
            with pe.Fori(0, NE) as i:
                pe.wait_ge(sem("e_selG"), i + 1)
                pe.wait_ge(sem("e_xe"), i + 1)
                bias_gu()
                for j in range(4):
                    g = NPRE + j
                    pe.wait_ge(landed[slot_of(g)], i * 16 + FILL[g])
                    gate_up(j).then_inc(used, 1)
                    if j == 0:
                        pe.wait_ge(sem("acc_zero"), 4)
                        pe.wait_ge(sem("e_y"), i + 1)
                        scatter()
                pe.wait_ge(sem("e_sel"), 2 * i + 4)
                gather()
                pe.wait_ge(sem("e_wsel"), 2 * i + 2)
                weights_T()
                pe.wait_ge(sem("e_xe"), i + 2)
                pe.wait_ge(sem("e_h"), i + 1)
                hidden_T()
                pe.wait_ge(sem("e_selD"), i + 1)
                pe.wait_ge(sem("e_wTe"), 2 * i + 2)
                bias_d()
                pe.wait_ge(sem("e_hTe"), i + 1)
                for j in range(2):
                    g = NPRE + 4 + j
                    pe.wait_ge(landed[slot_of(g)], i * 16 + FILL[g])
                    down(j).then_inc(used, 1)
            pe.wait_ge(sem("e_y"), NE + 1)
            scatter().then_inc(sem("acc_main"), 1)
            pe.wait_ge(sem("table_ready"), 1)
            n = nc.values_load(table_i[0:1, 32:33], engines=[ENG.PE], min_val=0, max_val=NX_MAX)
            with pe.If(n > 0):
                with pe.Fori(0, n) as i:
                    pe.wait_ge(sem("e_sel"), 2 * i + (2 * NE + 4))
                    gather()
                    pe.wait_ge(sem("e_selG"), i + (NE + 2))
                    pe.wait_ge(sem("e_xe"), i + (NE + 2))
                    bias_gu()
                    pe.wait_ge(sem("extra_landed"), 16 * PER_E * i + 16 * PER_E)
                    for j in range(4):
                        mm = gate_up(j)
                    mm.then_inc(sem("x_gu"), 1)
                    pe.wait_ge(sem("e_wsel"), 2 * i + (2 * NE + 2))
                    weights_T()
                    pe.wait_ge(sem("e_h"), i + (NE + 1))
                    hidden_T()
                    pe.wait_ge(sem("e_selD"), i + (NE + 1))
                    pe.wait_ge(sem("e_wTe"), 2 * i + (2 * NE + 2))
                    bias_d()
                    pe.wait_ge(sem("e_hTe"), i + (NE + 1))
                    for j in range(2):
                        mm = down(j)
                    mm.then_inc(sem("x_down"), 1)
                    pe.wait_ge(sem("e_y"), i + (NE + 2))
                    scatter().then_inc(sem("extra_used"), 1)
            at[0] = MOE_END

            def gate_rows(l):
                pe.wait_ge(*upto(f"ln{l}", "gate_diag", 1))
                for h in range(2):
                    mm = pe.matmul(B[6 + h][:], ones, XN[:, 0, h * HW:(h + 1) * HW], start=True, stop=True)
                mm.then_inc(sem("gate_mm"), 1)

            def scores(st, u, q, k):
                for h in range(2):
                    a, b = 2 * u + h, B[2 * (u % 2) + h]
                    if u >= 2:
                        pe.wait_ge(*upto(st, "s", a - 3))
                    pe.matmul(b[:, 0:P], q(a)[:, 0:P], k(a)[:, 0:P], start=True, stop=True)
                    pe.matmul(b[:, P:3 * P], q(a)[:, P:2 * P], k(a), start=True, stop=True).then_inc(sem("sc"), 1)

            def attend(st, q, k, v):
                units = ATTNS[st][0]
                for u in range(units):
                    g = u // 2
                    if u + 2 < units:
                        scores(st, u + 2, q, k)
                    pe.wait_ge(*upto(st, "p", 2 * u + 2))
                    for h in range(2):
                        n = 2 * u + h
                        if n >= 2:
                            pe.wait_ge(*upto(st, "pte", n - 1))
                        for c in range(3):
                            mm = pe.transpose(B[4 + h][:, c * P:(c + 1) * P], SC[:, n % 4, c * P:(c + 1) * P], ident)
                        mm.then_inc(sem("pt"), 1)
                    if g >= 2 and u % 2 == 0:
                        pe.wait_ge(*upto(st, "otl", g - 1))
                    for h in range(2):
                        a = 2 * u + h
                        pe.wait_ge(*upto(st, "pte", a + 1))
                        r = 64 * (a % 2)
                        o = B[6 + g % 2][r:r + 64, (u % 2) * S:(u % 2) * S + S]
                        pe.matmul(o, v(a, 0), PT[:, a % 4, 0:S], start=True, stop=False, skip_group_check=True)
                        mm = pe.matmul(o[:, P:S], v(a, 1), PT[:, a % 4, S:3 * P], start=False, stop=True,
                                       skip_group_check=True)
                    if u % 2 == 1:
                        mm.then_inc(sem("o"), 1)

            def split_granule():
                n = split_no(at[0])
                at[0] += 1
                pe.wait_ge(sem("w_lo"), n)
                return pair(n)

            def chunks(parts, k):
                return [a.rearrange("p (k n) -> p k n", k=k) for a in parts]

            def transpose_hat(a):
                st = "fin" if a == 0 else f"ln{a - 1}"
                for t in range(TB):
                    pe.wait_ge(*upto(st, "xhat", t + 1))
                    for k in range(KC):
                        mm = pe.transpose(B[4 + k // 2][:, (k % 2) * S + t * P:(k % 2) * S + t * P + P],
                                          X[:, t, k * P:(k + 1) * P], ident)
                        if t == 1 and k % 2 == 1:
                            mm.then_inc(sem("T"), 1)

            def x_chunk(a, k):
                pe.wait_ge(*upto(f"m{a}", "xt_a", k + 1))
                pe.wait_ge(*upto(f"m{a}", "xt_v", k + 1))

            def project3(x, base, ready=None, ln=None):
                for j in range(2):
                    w = chunks(split_granule(), 4)
                    if ln is None or j == 0:
                        for kl in range(4):
                            k = 4 * j + kl
                            if ready is not None:
                                x_chunk(ready, k)
                            for t in range(TB):
                                for h in range(2):
                                    mm = three(B[base + 2 * t + h][:], cut3(x, k, t * P, (t + 1) * P),
                                               cut3(w, kl, h * HW, (h + 1) * HW), k == 0, k == KC - 1)
                        mm.then_inc(used, 1)
                        if ln is not None:
                            gate_rows(ln)
                        continue
                    for t in range(TB):
                        for kl in range(4):
                            k = 4 * j + kl
                            for h in range(2):
                                mm = three(B[base + 2 * t + h][:], cut3(x, k, t * P, (t + 1) * P),
                                           cut3(w, kl, h * HW, (h + 1) * HW), k == 0, k == KC - 1)
                        mm.then_inc(sem("ln_y0") if t == 0 else used, 1)

            def mlp_group(l, it, last):
                n = f"mlp{l}"
                for p in range(2):
                    g = at[0] + 2 * p
                    pe.wait_ge(sem("w_lo"), it * R2 + split_no(g))
                    w = chunks(pair(split_no(g)), KC)
                    for b in range(2):
                        for k in range(KC):
                            if b == 0:
                                x_chunk(2 * l + 1, max(k, 1))
                            for r in range(2):
                                f = 2 * b + r
                                mm = three(B[4 + b][:, r * S:(r + 1) * S], cut3(w, k, f * P, (f + 1) * P),
                                           cut3((XT_r, XTL[2 * l + 1]), k, 0, S), k == 0 and r == 0, k == KC - 1)
                        mm.then_inc(sem("mlp_h") if b == 0 else used, 1)
                    g = g + 1
                    pe.wait_ge(sem("w_lo"), it * R2 + split_no(g))
                    w = chunks(pair(split_no(g)), 4)
                    if p == 0:
                        pe.wait_ge(*upto(n, "mlp_zero", 4))
                    for outer in range(2):
                        for inner in range(2):
                            tail = last and p == 1
                            b, ts = (inner, (outer,)) if tail else (outer, (0, 1) if inner == 0 else ())
                            if ts:
                                pe.wait_ge(*upto(n, "mlp_lo", it * 4 + (2 * p + b + 1)))
                            for r in range(2):
                                for t in ts:
                                    for h in range(2):
                                        mm = three(B[2 * t + h][:], cut3(hid, 2 * b + r, t * P, (t + 1) * P),
                                                   cut3(w, 2 * b + r, h * HW, (h + 1) * HW), False, False)
                        if tail:
                            mm.then_inc(sem("ln_y0") if outer == 0 else used, 1)
                    if not tail:
                        mm.then_inc(used, 1)

            def mlp(l):
                with pe.Fori(0, 3) as it:
                    mlp_group(l, it, False)
                gate_rows(2 * l + 1)
                mlp_group(l, 3, True)
                at[0] += 16

            transpose_hat(0)
            for j in range(3):
                kn = min(3, KC - 3 * j)
                w = [a[:, 0:kn * 1224].rearrange("p (k n) -> p k n", k=kn) for a in split_granule()]
                for kl in range(kn):
                    k = 3 * j + kl
                    x_chunk(0, k)
                    for t in range(TB):
                        if k == 0 and t == 1:
                            x_chunk(0, 3)
                        for c in range(3):
                            mm = three(B[3 * t + c][:, 0:408], cut3((XT_r, XTL[0]), k, t * P, (t + 1) * P),
                                       cut3(w, kl, 408 * c, 408 * c + 408), k == 0, k == KC - 1)
                mm.then_inc(used, 1)
            pe.wait_ge(sem("cq_n"), 2)
            for k in range(2):
                for t in range(TB):
                    mm = pe.transpose(B[6][:, k * S + t * P:k * S + t * P + P],
                                      XN[:, t, S + k * P:S + (k + 1) * P], ident)
            mm.then_inc(sem("cq_T"), 1)
            pe.wait_ge(sem("cqT"), 2)
            pe.wait_ge(sem("z0"), 3)
            pe.wait_ge(sem("z1"), 3)
            w = granule()
            for m in (1, 0):
                wm = w[:, m * 1024:(m + 1) * 1024].rearrange("p (k n) -> p k n", k=2)
                for t in range(TB):
                    for k in range(2):
                        mm = pe.matmul(B[2 * m + t][:], XTf[:, k * S + t * P:k * S + t * P + P], wm[:, k, :],
                                       start=(k == 0), stop=(k == 1))
                if m:
                    mm.then_inc(sem("iq_mm"), 1)
            mm.then_inc(used, 1)
            pe.wait_ge(sem("a_rope"), 2)
            R1a = R1b.rearrange("p (t n) -> p t n", t=TB)
            for j in range(4):
                for t in range(TB):
                    mm = pe.transpose(B[6 + j // 2][:, (j % 2) * S + t * P:(j % 2) * S + t * P + P],
                                      R1a[:, t, j * P:(j + 1) * P], ident)
            mm.then_inc(sem("a_T"), 1)
            pe.wait_ge(sem("k_rope"), 2)
            for t in range(TB):
                pe.transpose(B[4][:, t * P:(t + 1) * P], R1a[:, t, 512:640], ident)
                pe.transpose(B[4][:, S + t * P:S + (t + 1) * P], R2b[:, t, 0:P], ident)
                mm = pe.transpose(B[5][:, t * P:(t + 1) * P], R2b[:, t, P:2 * P], ident)
            mm.then_inc(sem("k_T"), 1)
            for m, (st, src, e) in enumerate((("i_", R4b, "a_Te"), ("b_", R1b, "k_Te"))):
                pe.wait_ge(sem(st + "rope"), 2)
                pe.wait_ge(sem(e), 2 + m)
                s2 = src[:, 0:1024].rearrange("p (t n) -> p t n", t=TB)
                for j in range(4):
                    for t in range(TB):
                        mm = pe.transpose(B[(6, 4)[m] + j // 2][:, (j % 2) * S + t * P:(j % 2) * S + t * P + P],
                                          s2[:, t, j * P:(j + 1) * P], ident)
                mm.then_inc(sem(st + "T"), 1)
            pe.wait_ge(sem("i_Te"), 2)
            pe.wait_ge(sem("k_Te"), 3)
            pe.wait_ge(sem("b_Te"), 2)

            def q_ab(a):
                if a < 8:
                    return aqT[64 * (a // 4):64 * (a // 4) + 64, a % 4, :]
                return bqT[64 * (a % 2):64 * (a % 2) + 64, (a - 8) // 2, :]

            def k_ab(a):
                if a < 8:
                    return akT[64 * (a // 4):64 * (a // 4) + 64, :]
                return bkT[64 * (a % 2):64 * (a % 2) + 64, :]

            def v_ab(a, t):
                return Z[:, t, 640 + 64 * (a // 4):704 + 64 * (a // 4)] if a < 8 else Z[:, t, 1088:1152]

            scores("ab", 0, q_ab, k_ab)
            scores("ab", 1, q_ab, k_ab)
            for h in range(8):
                if h >= 4:
                    pe.wait_ge(sem("ix_relu"), h - 3)
                r, b = 64 * (h % 2), B[IX_BANKS[h % 4]]
                pe.matmul(b[:, 0:P], iqT[r:r + 64, h // 2, 0:P], ikT[r:r + 64, 0:P], start=True, stop=True)
                pe.matmul(b[:, P:3 * P], iqT[r:r + 64, h // 2, P:S], ikT[r:r + 64, :], start=True,
                          stop=True).then_inc(sem("ix_mm"), 1)
            pe.wait_ge(sem("ix_relu"), 8)
            attend("ab", q_ab, k_ab, v_ab)
            pe.wait_ge(*upto("ab", "otl", 4))
            project3(OTa + OTb, 0, ln=0)
            transpose_hat(1)
            mlp(0)
            transpose_hat(2)
            x2 = (XT_r, XTL[2])
            project3(x2, 0, ready=2)
            project3(x2, 4)
            pe.wait_ge(sem("c_rope"), 4)
            project3(x2, 0)
            for m in range(2):
                pe.wait_ge(sem("c_rope"), 8)
                src = arn(2048 * m, 2048).rearrange("p (t n) -> p t n", t=TB)
                for q in range(4):
                    if m:
                        pe.wait_ge(sem("c_Te"), q + 1)
                    for r in range(2):
                        for t in range(TB):
                            k = 2 * q + r
                            mm = pe.transpose(B[4 + q][:, r * S + t * P:r * S + t * P + P],
                                              src[:, t, k * P:(k + 1) * P], ident)
                    mm.then_inc(sem("c_T"), 1)
            pe.wait_ge(sem("c_Te"), 8)
            pe.wait_ge(sem("cv"), 4)
            cqT = arn(4096, 2048).rearrange("p (k s) -> p k s", k=KC)
            ckT = arn(6144, 2048).rearrange("p (k s) -> p k s", k=KC)
            cv = arn(8192, 2048).rearrange("p (t n) -> p t n", t=TB)
            q_c = lambda a: cqT[64 * (a % 2):64 * (a % 2) + 64, a // 2, :]
            k_c = lambda a: ckT[64 * (a % 2):64 * (a % 2) + 64, a // 2, :]
            scores("cc", 0, q_c, k_c)
            scores("cc", 1, q_c, k_c)
            attend("cc", q_c, k_c, lambda a, t: cv[:, t, 64 * a:64 * a + 64])
            pe.wait_ge(*upto("cc", "otl", 4))
            project3(OTc, 0, ln=2)
            transpose_hat(3)
            mlp(1)

        @block.vector
        def _(dve):
            steps = [0]

            def link(ins):
                steps[0] += 1
                ins.then_inc(sem("dve_step"), 1)
                dve.wait_ge(sem("dve_step"), steps[0])

            def gain(name):
                return lambda k: col[:, VEC[name] + k:VEC[name] + k + 1]

            def bc(ap, n):
                return ap[:, :, None].to_broadcast((P, ap.shape[1], n))

            def norm(st, src, dst, at):
                dve.wait_ge(*upto(st, "root", 1))
                link(dve.reciprocal(stat[:, 64 + at:66 + at], stat[:, at + 2:at + 4]))
                for t in range(TB):
                    dve.tensor_scalar(dst[:, t, :], src[:, t, :], stat[:, 64 + at + t:65 + at + t], None,
                                      ALU.mult).then_inc(sem("xn"), 1)

            def evac_split(st, base, x, g1):
                for q in range(4):
                    dve.wait_ge(*upto(st, "xt_a", 2 * q + 2))
                    for r in range(2):
                        k = 2 * q + r
                        dve.scalar_tensor_tensor(x[1][:, k, :], B[base + q][:, r * S:(r + 1) * S], g1(k),
                                                 x[0][:, k, :].bitcast(F32), ALU.mult, ALU.subtract).then_inc(
                                                     sem("xt_v"), 1)

            def evac_T(st, base, XTo, g1):
                for q in (1, 3):
                    dve.wait_ge(*upto(st, "T", q + 1))
                    for r in range(2):
                        k = 2 * q + r
                        src = B[base + q][:, r * S:(r + 1) * S]
                        dve.tensor_scalar(XTo[:, k, :], src, g1(k), None, ALU.mult).then_inc(sem("xt_v"), 1)

            unit = [0]

            def ada(n):
                for _ in range(n):
                    u = unit[0]
                    unit[0] += 1
                    a, nb = u // 6, u % 6
                    dve.wait_ge(sem("ada_comb"), u + 1)
                    dve.scalar_tensor_tensor(mod[:, a, 4 * nb:4 * nb + 4], B[7][:, 0:4], float(nb >= 2),
                                             ada_bT[:, 24 * a + 4 * nb:24 * a + 4 * nb + 4], ALU.add,
                                             ALU.add).then_inc(sem("ada_done"), 1)

            def add_residual(st, base, w):
                dve.wait_ge(*done(w, 1))
                for t in range(TB):
                    for h in range(2):
                        xs = X[:, t, h * HW:(h + 1) * HW]
                        dve.tensor_tensor(xs, B[base + 2 * t + h][:], xs, ALU.add).then_inc(sem(st), 1)

            norm("mem", MEM, MEMN, 0)
            norm("mix", X, XN, 4)
            dve.wait_ge(sem("c_sig"), 1)
            link(dve.tensor_tensor(sil[:, 1, :], sil[:, 0, :], col[:, VEC["c_2"]:VEC["c_2"] + 8], ALU.mult))
            dve.tensor_copy(cs[:], bc(sil[:, 1, :], 32)).then_inc(sem("cs"), 1)
            evac_split("mem", 0, MEMT, gain("norm_mem"))
            half_lo(dve, "w_k", 0, 1, 2, 3)
            half_lo(dve, "w_v", 0, 1, 2, 3)
            dve.wait_ge(*done("w_v", 1))
            for t in range(TB):
                for h in range(2):
                    dve.tensor_copy(V[:, t, h * HW:(h + 1) * HW], B[2 * t + h][:]).then_inc(sem("v"), 1)
            evac_split("mix", 4, XTmix, gain("norm_mix"))
            half_lo(dve, "w_in", *range(2, 8))
            dve.wait_ge(sem("mix_c"), 2)
            for i in range(2):
                dve.tensor_tensor(GP[:, 2 * i:2 * i + 2, 1:S + 1], CT[:, i * HW:(i + 1) * HW].rearrange(
                    "p (k s) -> p k s", k=2), B[4 + i][:].rearrange("p (k s) -> p k s", k=2),
                    ALU.mult).then_inc(sem("conv_g"), 1)
            dve.wait_ge(sem("conv_g"), 2)
            dve.wait_ge(sem("conv_pad"), 2)
            cw = VEC["conv_w"]
            for tap in (1, 0, 2):
                for k in range(4):
                    wcol = col[:, cw + 4 * tap + k:cw + 4 * tap + k + 1]
                    g = GP[:, k, tap:tap + S]
                    if tap == 1:
                        ins = dve.tensor_scalar(YT[:, k, :], g, wcol, None, ALU.mult)
                    else:
                        ins = dve.scalar_tensor_tensor(YT[:, k, :], g, wcol, YT[:, k, :], ALU.mult, ALU.add)
                    if k == 3:
                        link(ins)
            for i in range(2):
                y = YT[:, 2 * i:2 * i + 2, :]
                dve.tensor_tensor(y, B[i][:].rearrange("p (k s) -> p k s", k=2), y, ALU.mult).then_inc(sem("conv_y"), 1)
            ada(5)
            ada(3)
            dve.wait_ge(sem("conv_y"), 2)
            dve.wait_ge(sem("fft_grp"), 1)
            for i in range(2):
                dve.tensor_copy(YT[:, 4 + 2 * i:6 + 2 * i, :], B[2 + i][:].rearrange("p (k s) -> p k s", k=2)).then_inc(
                    sem("fft_y"), 1)
            ada(2)
            dve.wait_ge(sem("mix_rms"), 1)
            dve.wait_ge(sem("fft_y"), 2)
            link(dve.reciprocal(RMS, RMS))
            for k in range(8):
                gk = gain("g_conv_out")(k)
                dve.scalar_tensor_tensor(YT[:, k, :], YT[:, k, :], gk, RMS[:, k // 4, :], ALU.mult,
                                         ALU.mult).then_inc(sem("mix_yn"), 1)
            ada(2)
            for m in range(2):
                dve.wait_ge(*upto("y", "op_hi", m + 1))
                dve.tensor_tensor(YTs[1][:, 4 * m:4 * m + 4, :], YT[:, 4 * m:4 * m + 4, :],
                                  YTs[0][:, 4 * m:4 * m + 4, :].bitcast(F32), ALU.subtract).then_inc(sem("op_lo"), 1)
            half_lo(dve, "w_out", 0, 1, 2, 3)
            add_residual("wout_x", 0, "w_out")
            norm("xa", X, XN, 8)
            ada(2)
            evac_split("xa", 0, XTxa, gain("norm_xattn"))
            half_lo(dve, "w_q", 2, 3)
            ada(1)
            for h in range(4):
                dve.wait_ge(sem("xa_s"), h + 1)
                link(dve.reduce_max(att[:, 3, 2 * h:2 * h + 2], B[h][:].rearrange("p (t m) -> p t m", t=TB), AX.X))
                dve.tensor_scalar(att[:, 0, 2 * h:2 * h + 2], att[:, 3, 2 * h:2 * h + 2], -1.0 / 16, None,
                                  ALU.mult).then_inc(sem("xa_nm"), 1)
            for h in range(4):
                dve.wait_ge(sem("xa_e"), 2 * h + 2)
                link(dve.reciprocal(att[:, 4, 2 * h:2 * h + 2], att[:, 1, 2 * h:2 * h + 2]))
                for t in range(TB):
                    dve.tensor_scalar(PR[:, h, t, :], PR[:, h, t, :], att[:, 4, 2 * h + t:2 * h + t + 1], None,
                                      ALU.mult).then_inc(sem("xa_p"), 1)
            ada(3)
            for h in range(4):
                dve.wait_ge(*upto("xo", "op_hi", h + 1))
                dve.tensor_tensor(OTx[1][:, 2 * h:2 * h + 2, :], B[(4, 5, 0, 1)[h]][:].rearrange(
                    "p (m s) -> p m s", m=2), OTx[0][:, 2 * h:2 * h + 2, :].bitcast(F32),
                    ALU.subtract).then_inc(sem("op_lo"), 1)
            half_lo(dve, "w_o", 2, 3)
            add_residual("wo_x", 0, "w_o")
            norm("ffn", X, XN, 12)
            ada(2)
            evac_T("ffn", 0, XT, gain("norm_ffn"))
            dve.memset(logit[:, :, NE:NE + 4], 3e38).then_inc(sem("rt_pad"), 1)
            dve.memset(gat[:, NE, :], 0.0).then_inc(sem("rt_pad"), 1)
            dve.wait_ge(sem("rt_pad"), 2)
            dve.wait_ge(sem("logits"), 1)
            for t in range(TB):
                link(dve.tensor_tensor(logit[:, t, 0:NE], B[4][:, t * NE:(t + 1) * NE], brow[:], ALU.add))
                link(dve.max(rt[:, t, 40:48], logit[:, t, 0:NE + 4]))
                dve.tensor_scalar(att[:, 2, t:t + 1], rt[:, t, 44:45], -1.0, None, ALU.mult).then_inc(sem("rt_nm"), 1)
                link(dve.match_replace(rt[:, 2 + t, 0:NE + 4], rt[:, t, 40:48], logit[:, t, 0:NE + 4], TAKEN))
                dve.tensor_scalar(rt[:, 4 + t, 0:NE], rt[:, 2 + t, 0:NE], -2e38, None, ALU.is_lt).then_inc(
                    sem("rt_mask"), 1)
            dve.wait_ge(sem("rt_mask"), 2)
            for t in range(TB):
                dve.tensor_copy(mrep[:, t, :].rearrange("p (r e) -> p r e", r=NB_MAX - 1),
                                rt[:, 4 + t, None, 0:NE].to_broadcast((P, NB_MAX - 1, NE))).then_inc(sem("rt_mask"), 1)
            dve.wait_ge(sem("rt_e"), 2)
            for t in range(TB):
                link(dve.tensor_tensor(rt[:, 2 + t, 0:NE], rt[:, t, 0:NE], rt[:, 4 + t, 0:NE], ALU.mult))
                link(dve.reduce_sum(rt[:, t, 50:51], rt[:, 2 + t, 0:NE], AX.X))
                link(dve.reciprocal(rt[:, t, 51:52], rt[:, t, 50:51]))
                link(dve.tensor_scalar(gat[:, 0:NE, t], rt[:, 2 + t, 0:NE], rt[:, t, 51:52], None, ALU.mult))
                link(dve.tensor_scalar(rt[:, 2 + t, 0:NE], rt[:, 4 + t, 0:NE], -FAR, FAR, ALU.mult, ALU.add))
            ada(1)
            dve.wait_ge(sem("rt_pos"), 1)
            link(dve.memset(pos[:], FAR))
            for t in range(TB):
                link(dve.tensor_tensor(pos[:, 0, 0:NE, t], B[5][:, t * NE:(t + 1) * NE], rt[:, 2 + t, 0:NE], ALU.add))
            for b in range(1, NB_MAX):
                link(dve.tensor_scalar(pos[:, b], pos[:, 0], -float(CAP * b), None, ALU.add))
            dve.tensor_tensor(flag, B[5][0:NCAND, 64:65], tb_("thr")[0:NCAND], ALU.is_gt).then_inc(sem("flag"), 1)
            ada(1)

            posf = pos[:].rearrange("p b e t -> p (b e) t")

            def select(q):
                for t in range(TB):
                    ins = dve.tensor_scalar(sel_tok[:, t, :], iota[:, 0:CAP], posf[:, bass.ds(q, 1), t], None,
                                            ALU.is_equal)
                    ins.then_inc(sem("e_sel"), 1)

            def expert_row(dst, e):
                return dve.tensor_scalar(dst, ones[:, 0:CAP], ident[:, bass.ds(e, 1)], None, ALU.mult)

            def weigh(q, e):
                for t in range(TB):
                    ins = dve.tensor_scalar(wsel[:, t, :], iota, posf[:, bass.ds(q, 1), t], gat[:, bass.ds(e, 1), t],
                                            ALU.is_equal, ALU.mult)
                    ins.then_inc(sem("e_wsel"), 1)

            def gains_xe():
                g = VEC["norm_ffn"]
                dve.tensor_tensor(xe, B[3][:].rearrange("p (k n) -> p k n", k=KC), bc(col[:, g:g + KC], CAP),
                                  ALU.mult).then_inc(sem("e_xe"), 1)

            def clamp():
                dve.tensor_scalar(gcl, B[0][:], 7.0, None, ALU.min).then_inc(sem("e_clamp"), 1)
                dve.tensor_scalar(ucl, B[1][:], 7.0, -7.0, ALU.min, ALU.max).then_inc(sem("e_clamp"), 1)

            def swiglu(i):
                dve.wait_ge(sem("e_sig"), i + 1)
                dve.wait_ge(sem("e_clamp"), 2 * i + 2)
                dve.tensor_tensor(gl, gcl, sig, ALU.mult).then_inc(sem("e_glu"), 1)
                dve.wait_ge(sem("e_glu"), i + 1)
                dve.scalar_tensor_tensor(hh_, ucl, 1.0, gl, ALU.add, ALU.mult).then_inc(sem("e_h"), 1)

            select(0)
            expert_row(selG, 0).then_inc(sem("e_selG"), 1)
            dve.wait_ge(sem("rank"), 1)
            dve.tensor_scalar(chosen, iota[0:NCAND, 0:NX_MAX], B[5][0:NCAND, 65:66], flag, ALU.is_equal,
                              ALU.mult).then_inc(sem("chosen"), 1)
            ada(1)
            dve.wait_ge(sem("table_mm"), 1)
            dve.tensor_copy(table_i[0:1, 0:33], B[5][0:1, 96:129]).then_inc(sem("table_ready"), 1)
            dve.wait_ge(sem("table_ready"), 1)
            ada(1)
            dve.wait_ge(sem("e_gather"), 1)
            gains_xe()
            dve.wait_ge(sem("ada_done"), ADA_UNITS)
            for b in range(4):
                dve.memset(B[4 + b][:], 0.0).then_inc(sem("acc_zero"), 1)

            with dve.Fori(0, NE) as i:
                dve.wait_ge(used, i * PER_E + (NPRE + 1))
                select(i + 1)
                weigh(i, i)
                expert_row(selG, i + 1).then_inc(sem("e_selG"), 1)
                expert_row(selD, i).then_inc(sem("e_selD"), 1)
                dve.wait_ge(used, i * PER_E + (NPRE + 4))
                clamp()
                dve.wait_ge(sem("e_gather"), i + 2)
                gains_xe()
                swiglu(i)
            n = nc.values_load(table_i[0:1, 32:33], engines=[ENG.DVE], min_val=0, max_val=NX_MAX)
            dve.wait_ge(sem("acc_main"), 1)
            with dve.If(n > 0):
                with dve.Fori(0, n) as i:
                    e = nc.values_load(table_i[0:1, bass.ds(i, 1)], engines=[ENG.DVE], min_val=0, max_val=NE - 1)
                    q = nc.values_load(table_i[0:1, bass.ds(i + 16, 1)], engines=[ENG.DVE], min_val=0,
                                       max_val=NB_MAX * (NE + 1) - 1)
                    select(q)
                    weigh(q, e)
                    expert_row(selG, e).then_inc(sem("e_selG"), 1)
                    expert_row(selD, e).then_inc(sem("e_selD"), 1)
                    dve.wait_ge(sem("e_gather"), i + (NE + 2))
                    gains_xe()
                    dve.wait_ge(sem("x_gu"), i + 1)
                    clamp()
                    swiglu(i + NE)
                    dve.wait_ge(sem("extra_used"), i + 2)
            for t in range(TB):
                for h in range(2):
                    xs = X[:, t, h * HW:(h + 1) * HW]
                    dve.tensor_tensor(xs, B[4 + 2 * t + h][:], xs, ALU.add).then_inc(sem("moe_x"), 1)
            dve.wait_ge(*upto("fin", "root", 1))
            link(dve.reciprocal(stat[:, 80:82], stat[:, 18:20]))
            for t in range(TB):
                dve.tensor_scalar(X[:, t, :], X[:, t, :], stat[:, 80 + t:81 + t], None, ALU.mult).then_inc(
                    sem("xhat"), 1)

            def rope_angles():
                dve.wait_ge(sem("pos_landed"), 32)
                link(dve.tensor_copy(stat[:, 100:102], posi[:]))
                ang, kf, r = ropeS[:, :, 32:64], ropeS[:, :, 0:32], ropeC[:, :, 0:32]
                for t in range(TB):
                    link(dve.tensor_scalar(ang[:, t], tb_("inv"), stat[:, 100 + t:101 + t], None, ALU.mult))
                magic = 12582912.0
                c1 = 6.28125
                c2 = float(np.float32(np.floor((2 * np.pi - c1) * 2 ** 20) / 2 ** 20))
                c3 = 2 * np.pi - c1 - c2
                link(dve.tensor_scalar(kf, ang, 1.0 / (2 * np.pi), magic, ALU.mult, ALU.add))
                link(dve.tensor_scalar(kf, kf, -magic, None, ALU.add))
                for c in (c1, c2, c3):
                    link(dve.scalar_tensor_tensor(ang, kf, -c, ang, ALU.mult, ALU.add))
                link(dve.tensor_scalar(ang, ang, 3.1415925, -3.1415925, ALU.min, ALU.max))
                dve.scalar_tensor_tensor(r, ang, -1.0, ang, ALU.mult, ALU.max).then_inc(sem("rope_ang"), 1)

            def rope_tables():
                dve.wait_ge(sem("rope_sc"), 2)
                link(dve.tensor_copy(ropeC[:, :, 32:64], ropeC[:, :, 0:32]))
                dve.tensor_scalar(ropeS[:, :, 0:32], ropeS[:, :, 32:64], -1.0, None, ALU.mult).then_inc(sem("rope_tables"), 1)
                dve.wait_ge(sem("rope_tables"), 1)

            def modcol(a):
                return (lambda k: mod[:, a, 8 + k:9 + k]), (lambda k: mod[:, a, k:k + 1])

            def ot_lo(st, g, ot):
                dve.wait_ge(*upto(st, "ot", g + 1))
                dve.tensor_tensor(ot(g)[1], B[6 + g % 2][:].rearrange("p (m s) -> p m s", m=2),
                                  ot(g)[0].bitcast(F32), ALU.subtract).then_inc(sem("otl"), 1)

            def front(st, u, mask):
                sink = u < ATTNS[st][1]
                c = 4 * (u % 2)
                sc = SC[:, 2 * (u % 2):2 * (u % 2) + 2, :]
                if u >= 2:
                    dve.wait_ge(*upto(st, "pt", 2 * u - 2))
                for h in range(2):
                    dve.wait_ge(*upto(st, "sc", 2 * u + h + 1))
                    dve.scalar_tensor_tensor(sc[:, h, :], B[2 * (u % 2) + h][:, 0:3 * P], HD ** -0.5, mask, ALU.mult,
                                             ALU.add).then_inc(sem("s"), 1)
                dve.wait_ge(*upto(st, "s", 2 * u + 2))
                dve.reduce_max(att[:, 0, c:c + 2], sc[:, :, 0:P], AX.X)
                link(dve.reduce_max(att[:, 0, c + 2:c + 4], sc[:, :, P:3 * P], AX.X))
                if sink:
                    sk = sinkb[:, None, 2 * u:2 * u + 2].to_broadcast((P, TB, 2))
                    mx = att[:, 0, c:c + 4].rearrange("p (t h) -> p t h", t=TB)
                    link(dve.tensor_tensor(mx, mx, sk, ALU.max))
                ins = dve.tensor_scalar(att[:, 1, c:c + 4], att[:, 0, c:c + 4], -1.0, None, ALU.mult)
                if sink:
                    link(ins)
                    ins = dve.tensor_tensor(att[:, 3, c:c + 4].rearrange("p (t h) -> p t h", t=TB), sk,
                                            att[:, 1, c:c + 4].rearrange("p (t h) -> p t h", t=TB), ALU.add)
                ins.then_inc(sem("nm"), 1)

            def attend(st, mask, ot, after_front):
                units = ATTNS[st][0]

                def weights(u):
                    c = 4 * (u % 2)
                    sc = SC[:, 2 * (u % 2):2 * (u % 2) + 2, :]
                    dve.wait_ge(*upto(st, "e", exps_of(st, u + 1)))
                    if u < ATTNS[st][1]:
                        link(dve.tensor_tensor(att[:, 2, c:c + 4], att[:, 2, c:c + 4], att[:, 4, c:c + 4], ALU.add))
                    link(dve.reciprocal(att[:, 0, 8 + c:12 + c], att[:, 2, c:c + 4]))
                    for t, (a, b) in enumerate(((0, P), (P, 3 * P))):
                        r = att[:, 0, 8 + c + 2 * t:10 + c + 2 * t]
                        dve.tensor_tensor(sc[:, :, a:b], sc[:, :, a:b], bc(r, b - a), ALU.mult).then_inc(sem("p"), 1)

                for u in range(units):
                    weights(u)
                    if u + 2 < units:
                        front(st, u + 2, mask(u + 2))
                    if u in after_front:
                        after_front[u]()
                    if u >= 3 and u % 2 == 1:
                        ot_lo(st, (u - 3) // 2, ot)
                ot_lo(st, units // 2 - 1, ot)

            def gate_diag(l):
                dve.tensor_tensor(XN[:, 0, :].rearrange("p (k n) -> p k n", k=KC),
                                  ident[:, None, :].to_broadcast((P, KC, P)), bc(mod[:, l, 16:24], P),
                                  ALU.mult).then_inc(sem("gate_diag"), 1)

            def layer_norm(l, w, last):
                dve.wait_ge(*upto(f"ln{l}", "gate", 2))
                dve.wait_ge(*upto(HATS[l], "ln_x", 2))
                for t in range(TB):
                    if t == 0:
                        dve.wait_ge(*upto(f"ln{l}", "ln_y0", 1))
                    else:
                        dve.wait_ge(*done(w, last))
                    for h in range(2):
                        ins = dve.tensor_tensor(XN[:, 0, h * HW:(h + 1) * HW], B[2 * t + h][:],
                                                XN[:, 1, h * HW:(h + 1) * HW], ALU.mult)
                    link(ins)
                    link(dve.scalar_tensor_tensor(X[:, t, :], X[:, t, :], 4.0 ** 0.25, XN[:, 0, :], ALU.mult, ALU.add))
                    for h in range(2):
                        ins = dve.bn_stats(rt[:, t, 6 * h:6 * h + 6], X[:, t, h * HW:(h + 1) * HW])
                    link(ins)
                    dve.bn_aggr(att[:, 5, 2 * t:2 * t + 2], rt[:, t, 0:12]).then_inc(sem("ln_var"), 1)
                    dve.wait_ge(*upto(f"ln{l}", "ln_root", t + 1))
                    link(dve.reciprocal(att[:, 5, 6 + t:7 + t], att[:, 5, 4 + t:5 + t]))
                    dve.tensor_scalar(X[:, t, :], X[:, t, :], att[:, 5, 2 * t:2 * t + 1], att[:, 5, 6 + t:7 + t],
                                      ALU.subtract, ALU.mult).then_inc(sem("xhat"), 1)
                    if l == 3:
                        dve.wait_ge(*upto("ln3", "ln_landed", 32))
                        dve.wait_ge(*upto("ln3", "xhat", t + 1))
                        link(dve.tensor_tensor(X[:, t, :], X[:, t, :], lng, ALU.mult))
                        dve.tensor_tensor(X[:, t, :], X[:, t, :], lnb, ALU.add).then_inc(sem("ln_x"), 1)

            def evac_lo(a):
                g1, g0 = modcol(a)
                for q in range(4):
                    dve.wait_ge(*upto(f"m{a}", "xt_a", 2 * q + 2))
                    for r in range(2):
                        k = 2 * q + r
                        if k >= 4:
                            dve.wait_ge(*upto(f"m{a}", "xt_v", k - 3))
                        ins = dve.scalar_tensor_tensor(XN[:, 0, k % 4 * S:k % 4 * S + S], B[4 + q][:, r * S:(r + 1) * S],
                                                       g1(k), XT_r[:, k, :].bitcast(F32), ALU.mult, ALU.subtract)
                    link(ins)
                    for r in range(2):
                        k = 2 * q + r
                        dve.tensor_scalar(XTL[a][:, k, :], XN[:, 0, k % 4 * S:k % 4 * S + S], g0(k), None,
                                          ALU.add).then_inc(sem("xt_v"), 1)
                dve.wait_ge(*upto(f"m{a}", "xt_v", KC))

            def mlp_group(l, it, last):
                n = f"mlp{l}"
                for p in range(2):
                    for b in range(2):
                        c = 2 * p + b + 1
                        dve.wait_ge(*upto(n, "mlp_relu", it * 4 + c))
                        hb = slice(2 * b, 2 * b + 2)
                        dve.tensor_tensor(sq_h[:, hb, :], relu_h[:, hb, :], relu_h[:, hb, :],
                                          ALU.mult).then_inc(sem("mlp_tt"), 1)
                        dve.wait_ge(*upto(n, "mlp_tt", it * 4 + c))
                        dve.wait_ge(*upto(n, "mlp_sq", it * 4 + c))
                        dve.tensor_tensor(hid[1][:, hb, :], sq_h[:, hb, :], hid[0][:, hb, :].bitcast(F32),
                                          ALU.subtract).then_inc(sem("mlp_lo"), 1)
                    if not (last and p == 1):
                        split_lo(dve, n, 2 * p + 2, it)
                        split_lo(dve, n, 2 * p + 3, it)

            def mlp(l):
                split_lo(dve, f"mlp{l}", 1)
                for b in range(4):
                    dve.memset(B[b][:], 0.0).then_inc(sem("mlp_zero"), 1)
                gate_diag(2 * l + 1)
                with dve.Fori(0, 3) as it:
                    mlp_group(l, it, False)
                mlp_group(l, 3, True)

            evac_lo(0)
            rope_angles()
            split_lo(dve, "ab_in", 1)
            rope_tables()
            split_lo(dve, "ab_in", 2)
            dve.wait_ge(*done("ab_in", 2))
            for c in range(3):
                dve.tensor_copy(Z[:, 1, 408 * c:408 * c + 408], B[3 + c][:, 0:408]).then_inc(sem("z1"), 1)
            dve.wait_ge(sem("cq_root"), 1)
            link(dve.reciprocal(stat[:, 84:86], stat[:, 22:24]))
            for t in range(TB):
                dve.tensor_scalar(XN[:, t, S:2 * S], Z[:, t, 768:1024], stat[:, 84 + t:85 + t], None,
                                  ALU.mult).then_inc(sem("cq_n"), 1)
            dve.wait_ge(sem("cq_T"), 1)
            for k in range(2):
                dve.tensor_scalar(XTf[:, k * S:(k + 1) * S], B[6][:, k * S:(k + 1) * S], gain("ab_q_norm_2")(k), None,
                                  ALU.mult).then_inc(sem("cqT"), 1)
            def rope(*a):
                rope_on(dve, link, *a)

            tmp = XNf[:, 512:1024]
            R1a = R1b.rearrange("p (t n) -> p t n", t=TB)
            for t in range(TB):
                rope(R1a[:, t, 512:640].rearrange("p (g d) -> p g d", g=2),
                     Z[:, t, 512:640].rearrange("p (g d) -> p g d", g=2),
                     tmp[:, 0:128].rearrange("p (g d) -> p g d", g=2), t, None)
                two = Z[:, t, 1024:1280 - 64].rearrange("p (m d) -> p m d", d=HD)[:, 0:3:2, :]
                rope(R2b[:, t, :].rearrange("p (m c d) -> p m c d", m=2, c=2)[:, :, 0, :], two,
                     tmp[:, 0:128].rearrange("p (g d) -> p g d", g=2), t, None)
                r2 = R2b[:, t, :].rearrange("p (m c d) -> p m c d", m=2, c=2)
                dve.tensor_copy(r2[:, :, 1, :], r2[:, :, 0, :]).then_inc(sem("k_rope"), 1)
            dve.wait_ge(sem("iq_mm"), 1)
            for t in range(TB):
                rope(R4b[:, t * HW:(t + 1) * HW].rearrange("p (h d) -> p h d", d=HD),
                     B[2 + t][:].rearrange("p (h d) -> p h d", d=HD), tmp[:, 0:512].rearrange("p (h d) -> p h d", d=HD),
                     t, "i_rope")
                dve.wait_ge(sem("i_rope"), t + 1)
            dve.wait_ge(*done("uq", 0))
            dve.wait_ge(sem("k_T"), 1)
            for t in range(TB):
                rope(R1b[:, t * HW:(t + 1) * HW].rearrange("p (h d) -> p h d", d=HD),
                     B[t][:].rearrange("p (h d) -> p h d", d=HD), tmp[:, 0:512].rearrange("p (h d) -> p h d", d=HD),
                     t, "b_rope")
                dve.wait_ge(sem("b_rope"), t + 1)
            iw = rt[:, 0, 0:16].rearrange("p (t h) -> p t h", t=TB)
            link(dve.tensor_scalar(iw, Z[:, :, 1216:1224], 8 ** -0.5 * HD ** -0.5, None, ALU.mult))
            dve.wait_ge(sem("sink_landed"), 16)
            for u in range(2):
                front("ab", u, tb_("window"))
            for h in range(8):
                dve.wait_ge(sem("ix_relu"), h + 1)
                if h:
                    dve.wait_ge(sem("ix_acc"), 2 * h)
                for t, (a, b) in enumerate(((0, P), (P, 3 * P))):
                    rl, w = relu_i[:, h % 2, a:b], iw[:, t, h:h + 1]
                    if h == 0:
                        ins = dve.tensor_scalar(idx[:, a:b], rl, w, None, ALU.mult)
                    else:
                        ins = dve.scalar_tensor_tensor(idx[:, a:b], rl, w, idx[:, a:b], ALU.mult, ALU.add)
                    ins.then_inc(sem("ix_acc"), 1)
            dve.wait_ge(sem("ix_acc"), 16)
            link(dve.tensor_tensor(idx, idx, tb_("full"), ALU.add))
            topk = 64
            rounds = topk // 8

            def choose(a, b):
                for rnd in range(a, b):
                    src = idx if rnd == 0 else left
                    dve.max(rt[:, 1, 0:8], src[:, 0:P])
                    link(dve.max(rt[:, 1, 8:16], src[:, P:3 * P]))
                    dve.match_replace(left[:, 0:P], rt[:, 1, 0:8], src[:, 0:P], TAKEN)
                    link(dve.match_replace(left[:, P:3 * P], rt[:, 1, 8:16], src[:, P:3 * P], TAKEN))
                if b == rounds:
                    link(dve.tensor_scalar(left, left, -2e38, NEG, ALU.is_gt, ALU.mult))
                    link(dve.tensor_tensor(bmask, left, tb_("full"), ALU.add))

            choose(0, 3)
            attend("ab", lambda u: tb_("window") if u < 4 else bmask, OTab,
                   {0: lambda: choose(3, 6), 1: lambda: choose(6, rounds)})
            dve.wait_ge(*upto("ab", "pt", 16))
            gate_diag(0)
            layer_norm(0, "ab_out", 1)
            evac_lo(1)
            mlp(0)
            layer_norm(1, "mlp0", 15)
            evac_lo(2)
            for i in range(1, 4):
                split_lo(dve, "c_in", i)
            tmps = XNf.rearrange("p (i n) -> p i n", i=4)
            for m in range(2):
                dve.wait_ge(*done("c_in", 2 * m + 1))
                dst = arn(2048 * m, 2048)
                for t in range(TB):
                    for h in range(2):
                        a = t * D + h * HW
                        rope(dst[:, a:a + HW].rearrange("p (h d) -> p h d", d=HD),
                             B[4 * m + 2 * t + h][:].rearrange("p (h d) -> p h d", d=HD),
                             tmps[:, 2 * t + h, :].rearrange("p (h d) -> p h d", d=HD), t, "c_rope")
                if m == 0:
                    split_lo(dve, "c_in", 4)
                    split_lo(dve, "c_in", 5)
            dve.wait_ge(sem("c_rope"), 8)
            front("cc", 0, tb_("full"))
            front("cc", 1, tb_("full"))
            attend("cc", lambda u: tb_("full"), OTcc, {})
            dve.wait_ge(*upto("cc", "pt", 16))
            gate_diag(2)
            layer_norm(2, "c_out", 1)
            evac_lo(3)
            mlp(1)
            layer_norm(3, "mlp1", 15)


_INS = ["x", "mem", "norm_mix", "w_in", "conv_w", "g_conv_out", "g_fft_out", "w_out", "norm_xattn", "norm_mem", "w_q",
        "w_k", "w_v", "w_o", "norm_ffn", "w_router", "b_router", "w_gate_up", "b_gate_up", "w_down", "b_down",
        "norm_final", "c_2", "positions_2", "ab_w_in_2", "ab_q_norm_2", "ab_w_uq_2", "ab_w_uiq_2", "ab_sinks_2",
        "ab_w_out_2", "c_w_in_2", "c_w_out_2", "ada_w_2", "ada_b_2", "ln_g_2", "ln_b_2", "mlp_w1_2", "mlp_w2_2"]


def kernel(**inputs):
    import concourse.bacc as bacc
    from concourse.bass_utils import run_bass_kernel_spmd

    nc = bacc.Bacc("TRN2", target_bir_lowering=False, num_devices=1)
    arrays = {f"in_{name}": np.ascontiguousarray(inputs[name]) for name in _INS}
    arrays["in_tables"], arrays["in_dft"] = tables()
    aps = {n: nc.dram_tensor(n, a.shape, mybir.dt.from_np(a.dtype), kind="ExternalInput").ap()
           for n, a in arrays.items()}
    out = nc.dram_tensor("out", (1, S, D), F32, kind="ExternalOutput").ap()
    build_program(nc, {n: aps[f"in_{n}"] for n in _INS}, aps["in_tables"], aps["in_dft"], out)
    r = run_bass_kernel_spmd(nc, [arrays], core_ids=[0])
    return r.results[0]["out"]
```
